# Optimizing a Trainium2 kernel written in Bass

```python
import math
import jax, jax.numpy as jnp
from jax import lax
import numpy as np

D_MODEL = 2048
BATCH = 1
SEQ = 256
DEPTH = 1

D_MIX = D_MODEL
A_WIDTH = D_MIX // 2
A_HEADS = 8
A_HEAD_DIM = A_WIDTH // A_HEADS
IDX_HEADS = 16
IDX_DIM = 64
TOPK_MAX = 256
Q_BLOCK = 64
B_WIDTH = D_MIX - A_WIDTH
B_HEADS = 4
B_KEY_WIDTH = B_WIDTH // 2
B_DK = B_KEY_WIDTH // B_HEADS
B_DV = B_WIDTH // B_HEADS
GATE_RANK = 16
GATE_TEMP = 16.0
CHUNK = 64
NUM_BUCKETS = 32
MAX_DISTANCE = 128
EPS = 1e-6

IN_WIDTHS = (A_WIDTH, A_WIDTH, A_WIDTH, A_WIDTH,
             IDX_HEADS * IDX_DIM, IDX_DIM, IDX_HEADS,
             B_KEY_WIDTH, B_KEY_WIDTH, B_WIDTH, B_WIDTH,
             GATE_RANK)
IN_COLS = sum(IN_WIDTHS)

kernel_name = "hymba_dsa_gla_adaln_trunk"

def rmsnorm(x, g):
    x32 = x.astype(jnp.float32)
    r = x32 * lax.rsqrt(jnp.mean(x32 * x32, axis=-1, keepdims=True) + EPS)
    return (r * g.astype(jnp.float32)).astype(x.dtype)

def t5_bucket(dist):
    max_exact = NUM_BUCKETS // 2
    d = jnp.maximum(dist, 0)
    df = jnp.maximum(d, 1).astype(jnp.float32)
    large = max_exact + (jnp.log(df / max_exact) / math.log(MAX_DISTANCE / max_exact)
                         * (NUM_BUCKETS - max_exact)).astype(jnp.int32)
    large = jnp.minimum(large, NUM_BUCKETS - 1)
    return jnp.where(d < max_exact, d, large)

def dsa_attention(q, k, v, iq, ik, iw, rel_bias):
    bsz, T, H, dh = q.shape
    topk = min(TOPK_MAX, T // 4)
    nb = T // Q_BLOCK

    def blockify(a):
        return jnp.moveaxis(a.reshape((bsz, nb, Q_BLOCK) + a.shape[2:]), 1, 0)

    key_pos = jnp.arange(T, dtype=jnp.int32)
    ik32 = ik.astype(jnp.float32)
    iw32 = iw.astype(jnp.float32) * (IDX_HEADS ** -0.5 * IDX_DIM ** -0.5)
    gather = jax.vmap(lambda kb, ib: kb[ib])

    def one_block(args):
        qb, iqb, iwb, start = args
        qpos = start + jnp.arange(Q_BLOCK, dtype=jnp.int32)
        s = jnp.einsum('bqjd,bsd->bqsj', iqb.astype(jnp.float32), ik32)
        score = jnp.einsum('bqsj,bqj->bqs', jax.nn.relu(s), iwb)
        causal = key_pos[None, :] <= qpos[:, None]
        score = jnp.where(causal[None], score, -jnp.inf)
        _, idx = lax.top_k(score, topk)
        valid = idx <= qpos[None, :, None]
        ks = gather(k, idx)
        vs = gather(v, idx)
        logits = jnp.einsum('bqhd,bqkhd->bhqk', qb, ks,
                            preferred_element_type=jnp.float32) * (dh ** -0.5)
        bucket = t5_bucket(qpos[None, :, None] - idx)
        logits = logits + jnp.moveaxis(rel_bias.astype(jnp.float32)[bucket], -1, 1)
        logits = jnp.where(valid[:, None], logits, -jnp.inf)
        p = jax.nn.softmax(logits, axis=-1)
        return jnp.einsum('bhqk,bqkhd->bqhd', p.astype(v.dtype), vs)

    starts = jnp.arange(nb, dtype=jnp.int32) * Q_BLOCK
    out = lax.map(one_block, (blockify(q), blockify(iq), blockify(iw32), starts))
    return jnp.moveaxis(out, 0, 1).reshape(bsz, T, H, dh)

def gla_chunked(q, k, v, log_a):
    bsz, T, H, dk = q.shape
    dv = v.shape[-1]
    nc = T // CHUNK
    f32 = jnp.float32

    def chunks(a):
        return jnp.moveaxis(a.astype(f32).reshape((bsz, nc, CHUNK) + a.shape[2:]), 1, 0)

    tri = jnp.tril(jnp.ones((CHUNK, CHUNK), dtype=bool))[None, :, :, None, None]

    def step(S, inp):
        qc, kc, vc, gc = inp
        b = jnp.cumsum(gc, axis=1)
        b_last = b[:, -1]
        o_inter = jnp.einsum('bthk,bhkv->bthv', qc * jnp.exp(b), S)
        diff = b[:, :, None] - b[:, None, :]
        decay = jnp.exp(jnp.where(tri, diff, -jnp.inf))
        attn = jnp.einsum('bthk,bshk,btshk->bhts', qc, kc, decay)
        o_intra = jnp.einsum('bhts,bshv->bthv', attn, vc)
        k_dec = kc * jnp.exp(b_last[:, None] - b)
        S_new = jnp.exp(b_last)[..., None] * S + jnp.einsum('bshk,bshv->bhkv', k_dec, vc)
        return S_new, o_inter + o_intra

    S0 = jnp.zeros((bsz, H, dk, dv), f32)
    _, o = lax.scan(step, S0, (chunks(q), chunks(k), chunks(v), chunks(log_a)))
    return jnp.moveaxis(o, 0, 1).reshape(bsz, T, H, dv).astype(v.dtype)

def hybrid_layer(x, shift, scale, gate, norm_g, w_in, w_alpha_up, b_alpha, gla_g,
                 w_out, rel_bias):
    bsz, T, _ = x.shape
    h = rmsnorm(x, norm_g) * (1.0 + scale[:, None]) + shift[:, None]
    proj = jnp.einsum('btd,dc->btc', h, w_in)
    points = np.cumsum(IN_WIDTHS)[:-1].tolist()
    aq, ak, av, ag, iq, ik, iw, bq, bk, bv, bg, ba = jnp.split(proj, points, axis=-1)

    heads_a = lambda a: a.reshape(bsz, T, A_HEADS, A_HEAD_DIM)
    a_out = dsa_attention(heads_a(aq), heads_a(ak), heads_a(av),
                          iq.reshape(bsz, T, IDX_HEADS, IDX_DIM), ik, iw, rel_bias)
    a_out = a_out.reshape(bsz, T, A_WIDTH) * jax.nn.silu(ag)

    pre = jnp.einsum('btr,rk->btk', ba, w_alpha_up) + b_alpha
    log_a = jax.nn.log_sigmoid(pre.astype(jnp.float32)) / GATE_TEMP
    heads_k = lambda a: a.reshape(bsz, T, B_HEADS, B_DK)
    b_out = gla_chunked(heads_k(bq) * (B_DK ** -0.5), heads_k(bk),
                        bv.reshape(bsz, T, B_HEADS, B_DV), heads_k(log_a))
    b_out = rmsnorm(b_out, gla_g).reshape(bsz, T, B_WIDTH) * jax.nn.silu(bg)

    y = jnp.einsum('btc,cd->btd', jnp.concatenate([a_out, b_out], axis=-1), w_out)
    return x + gate[:, None] * y

def setup_inputs(seed: int = 0) -> dict:
    key = jax.random.key(seed)
    ks = jax.random.split(key, 12)
    f32 = jnp.float32
    nrm = lambda k, shape, s: jax.random.normal(k, shape, f32) * s
    return {
        "x": nrm(ks[0], (BATCH, SEQ, D_MODEL), 1.0),
        "c": nrm(ks[1], (BATCH, D_MODEL), 1.0),
        "w_ada": nrm(ks[2], (DEPTH, D_MODEL, 3 * D_MODEL), 0.5 * D_MODEL ** -0.5),
        "b_ada": nrm(ks[3], (DEPTH, 3 * D_MODEL), 0.02),
        "norm_g": 1.0 + nrm(ks[4], (DEPTH, D_MODEL), 0.02),
        "w_in": nrm(ks[5], (DEPTH, D_MODEL, IN_COLS), D_MODEL ** -0.5),
        "w_alpha_up": nrm(ks[6], (DEPTH, GATE_RANK, B_KEY_WIDTH), GATE_RANK ** -0.5),
        "b_alpha": nrm(ks[7], (DEPTH, B_KEY_WIDTH), 0.02),
        "gla_g": 1.0 + nrm(ks[8], (DEPTH, B_DV), 0.02),
        "w_out": nrm(ks[9], (DEPTH, D_MIX, D_MODEL), D_MIX ** -0.5),
        "rel_bias": nrm(ks[10], (NUM_BUCKETS, A_HEADS), 0.5),
        "final_g": 1.0 + nrm(ks[11], (D_MODEL,), 0.02),
    }

def reference(x, c, w_ada, b_ada, norm_g, w_in, w_alpha_up, b_alpha, gla_g, w_out,
              rel_bias, final_g):
    c_act = jax.nn.silu(c)
    for l in range(DEPTH):
        mod = jnp.einsum('bd,de->be', c_act, w_ada[l]) + b_ada[l]
        shift, scale, gate = jnp.split(mod, 3, axis=-1)
        x = hybrid_layer(x, shift, scale, gate, norm_g[l], w_in[l], w_alpha_up[l],
                         b_alpha[l], gla_g[l], w_out[l], rel_bias)
    return rmsnorm(x, final_g)


_drawn_inputs = setup_inputs


def setup_inputs(seed=0):
    import zlib

    import numpy as np

    out = dict(_drawn_inputs(seed))
    spreads = {}
    factors = {'b_ada': 3.811,
     'norm_g': 7.565,
     'b_alpha': 30.617,
     'gla_g': 33.376,
     'rel_bias': 3.618,
     'final_g': 8.644}
    for name, (base, spread) in spreads.items():
        noise = np.random.default_rng([zlib.crc32(name.encode()), seed]).standard_normal(out[name].shape)
        drawn = base * np.exp(spread * noise) if base else spread * noise
        out[name] = __import__('jax').numpy.asarray(drawn.astype(out[name].dtype))
    for name, factor in factors.items():
        out[name] = (out[name] * factor).astype(out[name].dtype)
    return out
```

```python
from contextlib import ExitStack

import numpy as np
import concourse.bass as bass
from concourse import mybir

ALU = mybir.AluOpType
ACT = mybir.ActivationFunctionType
AX_X = mybir.AxisListType.X
F32 = mybir.dt.float32
F32R = mybir.dt.float32r
U8 = mybir.dt.uint8

P = 128
EPS = 1e-6
TOPK_MAX = 256
BUCKETS, MAX_DISTANCE = 32, 128
GATE_TEMP = 16.0
BLK = 512
CHUNK_KT = 2
RAW, SPLIT = 8, 4
ADA_SLOTS, ADA_KT, ADA_COLS = 5, 8, 256
SHIFT_PE = 6
SIDE_BANK = 4
CAUSAL_FILL = -3.0e38
TAKEN = -3.4e38
TAKEN_BELOW = -3.35e38
UNSELECTED = -1.0e30


def t5_bucket(dist):
    exact = BUCKETS // 2
    d = np.maximum(dist, 0)
    large = exact + (np.log(np.maximum(d, 1).astype(np.float32) / np.float32(exact))
                     / np.log(MAX_DISTANCE / exact) * (BUCKETS - exact)).astype(np.int32)
    return np.where(d < exact, d, np.minimum(large, BUCKETS - 1))


def constants(T):
    i = np.arange(P)
    ident = np.eye(P, dtype=np.float32)
    fill = np.where(i[None, :] > i[:, None], CAUSAL_FILL, 0.0).astype(np.float32)
    square = np.concatenate([ident, ident[::-1], fill], axis=1)
    dist = T - 1 - np.arange(T + P)
    onehot = (t5_bucket(dist)[None, :] == np.arange(BUCKETS)[:, None]).astype(np.float32)
    s, t = i[:, None], i[None, :]
    masks = [s == t] + [(s // (2 * m) == t // (2 * m)) & (s % (2 * m) < m) & (t % (2 * m) >= m)
                        for m in LEVELS]
    return square, onehot, np.stack(masks, 1).astype(np.float32)


LEVELS = (64, 32, 16, 8, 4, 2, 1)


def build(nc, x, c, w_ada, b_ada, norm_g, w_in, w_alpha_up, b_alpha, gla_g, w_out, rel_bias,
          final_g, square, onehot, masks, band_scratch, out):
    T, D = x.shape
    KT = D // P
    NKP = KT // CHUNK_KT
    TT = T // P
    HA, DA = rel_bias.shape[1], P
    A_W = HA * DA
    RANK, B_KW = w_alpha_up.shape
    HB, DK = B_KW // P, P
    DV = gla_g.shape[0]
    B_W = HB * DV
    IH, ID = 16, 64
    TOPK = min(TOPK_MAX, T // 4)
    assert (T, D, DK * HB, TT) == (256, 2048, 512, 2) and A_W == B_W == 1024
    AQ, AK, AV, AG = (n * A_W for n in range(4))
    IQ = 4 * A_W
    IK = IQ + IH * ID
    BQ = IK + ID + IH
    BK = BQ + B_KW
    BV = BK + B_KW
    BG = BV + B_W
    BA = BG + B_W
    NAR = ID + RANK + IH
    NB = RANK + IH
    EARLY = (IQ, IQ + BLK, BK)
    BLOCKS = (BQ, BV, BV + BLK, AQ, AQ + BLK, AK, AK + BLK, AV, AV + BLK, AG, AG + BLK,
              BG, BG + BLK)
    B_BQ, B_BV, B_AQ, B_AK, B_AV, B_AG, B_BG = 0, 1, 3, 5, 7, 9, 11
    NIN, NOUT = len(BLOCKS), D // BLK
    E0 = len(EARLY) * NKP
    CHUNKS = E0 + (NIN + NOUT) * NKP
    HALF = NKP // 2
    STEPS = 2 * (NIN + NOUT)

    def names(stem, n):
        return [f"{stem}{i}" for i in range(n)]

    PLAN = {
        0: [(n, "A") for n in names("T_iq0_", 2) + ["T_nar"]],
        1: [(n, "A") for n in names("T_iq1_", 2) + names("T_bk_", 2)],
        2: [("pre0", "A"), ("pre1", "A"), ("band", "A")],
        3: [(n, "A") for n in names("T_bq_", 2) + ["idx0", "idx1"]],
        4: [(f"idx{j}", "A") for j in range(2, 6)],
        5: [(f"idx{j}", "A") for j in range(6, 10)],
        6: [(f"idx{j}", "A") for j in range(10, 14)],
        7: [("idx14", "A"), ("idx15", "A"), ("diag0", "V"), ("diag1", "V")],
        8: [("cross", "V"), ("L64_0", "V"), ("L64_1", "V")],
        9: [("T_aq0_0", "A"), ("T_aq0_1", "A"), ("L32_0", "V"), ("L32_1", "V")],
        10: [(f"L{m}_{t}", "V") for m in (16, 8) for t in range(2)],
        11: [("T_aq1_0", "A"), ("T_aq1_1", "A"), ("L4_0", "V"), ("L4_1", "V")],
        12: [(f"L{m}_{t}", "V") for m in (2, 1) for t in range(2)],
        13: [("T_ak0_0", "A"), ("T_ak0_1", "A")],
        14: [(n, "A") for n in names("gla_o", 4)],
        15: [("T_ak1_0", "A"), ("T_ak1_1", "A")],
        16: [(f"qk{h}", "V") for h in range(4)],
        17: [(f"qk{h}", "V") for h in range(4, 8)],
        18: [(f"pt{h}", "A") for h in range(4)],
        19: [(f"pt{h}", "A") for h in range(4, 8)],
        20: [("pv0", "V"), ("pv2", "V")],
        21: [("pv4", "V"), ("pv6", "V")],
        24: [(f"mixA{i}", "V") for i in range(4)],
        26: [(f"mixB{i}", "V") for i in range(4)],
    }
    GATE_SUMS = {19: [0], 20: [1, 2], 21: [3], 22: [4], 23: [5], 24: [6], 25: [7], 26: [8], 27: [9], 28: [10, 11],
                 29: [12], 30: [13, 14], 31: [15]}
    sum_step = {n: s for s, ns in GATE_SUMS.items() for n in ns}
    GATE_LOADS = {}
    for n, s in sum_step.items():
        GATE_LOADS.setdefault(18 if n < 3 else max(s - 1, sum_step[n - 3] + 1), []).append(n)
    GATE_STEPS = {21: 0, 22: 1, 25: 2, 27: 3, 28: 4, 29: 5, 31: 6, 32: 7}
    for s, j in GATE_STEPS.items():
        PLAN.setdefault(s, []).append((f"gate{j}", "V"))
    USES = [u for s in sorted(PLAN) for u in PLAN[s]]
    ORDER = {name: i for i, (name, _) in enumerate(USES)}
    DRAINER = dict(USES)

    def drained_count(name):
        return sum(1 for n, d in USES[:ORDER[name] + 1] if d == DRAINER[name])

    with ExitStack() as ctx:
        def sb(name, shape, dt=F32):
            return ctx.enter_context(nc.sbuf_tensor(name, shape, dt))

        def sem(name):
            return ctx.enter_context(nc.semaphore(name))

        raw = sb("raw", [P, RAW, CHUNK_KT, BLK])
        w_hi = sb("w_hi", [P, SPLIT, CHUNK_KT, BLK], F32R)
        w_lo = sb("w_lo", [P, SPLIT, CHUNK_KT, BLK], F32R)
        h_hi = sb("h_hi", [P, KT, T], F32R)
        h_lo = sb("h_lo", [P, KT, T], F32R)
        a_hi = sb("a_hi", [P, KT // 2, T], F32R)
        a_lo = sb("a_lo", [P, KT // 2, T], F32R)
        nar_hi = a_hi[:, :, :].rearrange("p a t -> p (a t)")[:, 0:KT * NAR].rearrange("p (k n) -> p k n", k=KT)
        nar_lo = a_lo[:, :, :].rearrange("p a t -> p (a t)")[:, 0:KT * NAR].rearrange("p (k n) -> p k n", k=KT)
        gate_b = sb("gate_b", [P, D])
        hankel = sb("hankel", [P, HA, T])
        sq = sb("sq", [P, 3 * P])
        ident, flip, fill = sq[:, 0:P], sq[:, P:2 * P], sq[:, 2 * P:3 * P]
        lvl_mask = sb("lvl_mask", [P, 1 + len(LEVELS), P], U8)
        NROWS = 3 * KT + HB
        small = sb("small", [P, 344])
        at = [0]

        def tiny(n):
            at[0] += n
            assert at[0] <= 344
            return small[:, at[0] - n:at[0]]

        c_raw, c_act = tiny(KT), tiny(KT)
        cols = tiny(NROWS)
        mod = tiny(4)
        half = tiny(1)
        stats = tiny(8)
        iws = tiny(TT * IH)
        iws_v = iws.rearrange("p (t j) -> p t j", t=TT)
        top8 = tiny(TT * 8)
        lmax, nmax, rsum, rinv = tiny(16), tiny(16), tiny(16), tiny(16)
        gss, gms, grs = tiny(8), tiny(8), tiny(8)
        zss, zsum, zrs = tiny(8), tiny(2), tiny(2)
        gla_gb = sb("gla_gb", [P, DV])

        KW = 256
        arena = sb("arena", [P, 72 * KW])

        def place(kib, words):
            o = int(kib * KW)
            return arena[:, o:o + words]

        ada = [place(8 * i, ADA_KT * ADA_COLS).rearrange("p (k n) -> p k n", k=ADA_KT) for i in range(ADA_SLOTS)]
        xT = place(40, KT * T).rearrange("p (k t) -> p k t", k=KT)
        acc = [place(56 + i, ADA_COLS) for i in range(8)]
        nar_raw = place(64, KT * NAR).rearrange("p (k n) -> p k n", k=KT)
        x_nat = raw[:, 4:8, :, :].rearrange("p a k n -> p (a k n)").rearrange("p (t d) -> p t d", t=TT)
        x_junk = place(40, D)
        rows = place(70, P)
        onehot_sb = place(68.25, T + P)
        relb = place(69.75, HA)
        stage = [place(4 * i, TT * BLK).rearrange("p (t n) -> p t n", t=TT) for i in range(3)]
        masks_wide = place(36, (1 + len(LEVELS)) * P)
        relu = [place(8 + 1.5 * i, 3 * P) for i in range(2)]
        iqT = place(12, 8 * T).rearrange("p (c t) -> p c t", c=8)
        bkT, bqT = place(20, HB * T), place(24, HB * T)
        cum = place(28, HB * T)
        expo = [place(32, HB * T), place(36, HB * T)]
        qk = [place(40, HB * T), place(44, HB * T)]
        attn = place(48, 3 * BLK).rearrange("p (b n) -> p b n", b=3)
        bv = place(54, TT * B_W).rearrange("p (t n) -> p t n", t=TT)
        score = place(62, 3 * P)
        select = place(63.5, 3 * P)
        narT = place(66.25, T)
        ikT = place(67.25, T)
        band_sb = place(70, T + P)
        qT = place(12, HA * T).rearrange("p (h t) -> p h t", h=HA)
        kT = place(20, HA * T).rearrange("p (h t) -> p h t", h=HA)
        o_b = place(28, TT * B_W).rearrange("p (t n) -> p t n", t=TT)
        prob = place(36, HA * 3 * P).rearrange("p (h n) -> p h n", h=HA)
        v_a = place(54, TT * A_W).rearrange("p (t n) -> p t n", t=TT)
        probT = place(0, HA * 3 * P).rearrange("p (h n) -> p h n", h=HA)
        silu_a = place(12, TT * A_W).rearrange("p (t n) -> p t n", t=TT)
        mix_a = place(20, TT * A_W).rearrange("p (t n) -> p t n", t=TT)
        silu_b = [place(4 * i, TT * BLK).rearrange("p (t n) -> p t n", t=TT) for i in range(2)]
        slot = lambda a: a.rearrange("p (k n) -> p k n", k=ADA_KT)
        hankel_slot = slot(hankel[:, :, :].rearrange("p h t -> p (h t)"))
        gate_first = [slot(place(12, ADA_KT * ADA_COLS)), slot(place(20, ADA_KT * ADA_COLS))]
        gate_late = [slot(place(36, ADA_KT * ADA_COLS)), slot(place(44, ADA_KT * ADA_COLS))]

        def gate_slot(n):
            return hankel_slot if n % 3 == 2 else (gate_first if n < 3 else gate_late)[n % 3]
        gate_acc = [place(62 + i, ADA_COLS) for i in range(8)]
        junk = place(8, D)[:, 0:BLK]
        z = place(12, TT * D).rearrange("p (t d) -> p t d", t=TT)
        fin_g = place(54, D)
        w_alpha = sb("w_alpha", [ID + RANK, B_KW])
        ones = sb("ones", [P, P])

        bank = [ctx.enter_context(nc.psum_tensor(f"bank{i}", [P, BLK], F32)) for i in range(8)]
        ADA_BANK, NAR_BANK = 7, 6

        def side(name):
            return bank[SIDE_BANK + ORDER[name] % 4]

        x_in, c_in, rows_in, square_in, tables_in, nar_in = (
            sem(n) for n in ("x_in", "c_in", "rows_in", "square_in", "tables_in", "nar_in"))
        raw_in = [sem(f"raw_in{i}") for i in range(RAW)]
        ada_in = [sem(f"ada_in{i}") for i in range(ADA_SLOTS)]
        gate_in = [sem(f"gate_in{i}") for i in range(3)]
        bias_tables_in = sem("bias_tables_in")
        band_out, hankel_in, x_again, fin_in, gate_bias_in = (
            sem(n) for n in ("band_out", "hankel_in", "x_again", "fin_in", "gate_bias_in"))
        out_done = sem("out_done")
        hi_made, lo_made, chunk_used = sem("hi_made"), sem("lo_made"), sem("chunk_used")
        nar_hi_made, nar_lo_made, nar_done = sem("nar_hi_made"), sem("nar_lo_made"), sem("nar_done")
        early_drained, block_drained = sem("early_drained"), sem("block_drained")
        x_squared, x_rstd, x_normed, xT_filled, xT_drained = (
            sem(n) for n in ("x_squared", "x_rstd", "x_normed", "xT_filled", "xT_drained"))
        c_acted, cols_filled, cols_made = sem("c_acted"), sem("cols_filled"), sem("cols_made")
        ada_summed, shift_used = sem("ada_summed"), sem("shift_used")
        mod_filled, mod_read = sem("mod_filled"), sem("mod_read")
        h_made, h_hi_made, h_lo_made = sem("h_made"), sem("h_hi_made"), sem("h_lo_made")
        side_filled, drained_act, drained_dve = sem("side_filled"), sem("drained_act"), sem("drained_dve")
        pre_made, cum_made = sem("pre_made"), sem("cum_made")
        ones_made, masks_in, masks_made = sem("ones_made"), sem("masks_in"), sem("masks_made")
        expo_made, decay_made, level_made = sem("expo_made"), sem("decay_made"), sem("level_made")
        relu_used, select_made = sem("relu_used"), sem("select_made")
        gss_made, grs_made, o_b_made = sem("gss_made"), sem("grs_made"), sem("o_b_made")
        nmax_made, prob_made, rinv_made = sem("nmax_made"), sem("prob_made"), sem("rinv_made")
        silu_a_made, mix_a_made, silu_b_made, mix_b_made = (
            sem(n) for n in ("silu_a_made", "mix_a_made", "silu_b_made", "mix_b_made"))
        mixT_hi_made = sem("mixT_hi_made")
        gate_used, gate_summed = sem("gate_used"), sem("gate_summed")
        z_made, z_squared, zsum_made, z_rstd, z_scaled = (
            sem(n) for n in ("z_made", "z_squared", "zsum_made", "z_rstd", "z_scaled"))
        act_step, dve_step, pool_step = sem("act_step"), sem("dve_step"), sem("pool_step")

        def wait_drained(eng, name):
            eng.wait_ge(drained_act if DRAINER[name] == "A" else drained_dve, drained_count(name))

        def wait_filled(eng, name):
            eng.wait_ge(side_filled, ORDER[name] + 1)

        def chunk_source(g):
            if g < E0:
                kp, c0 = g // len(EARLY), EARLY[g % len(EARLY)]
            else:
                blk, kp = divmod(g - E0, NKP)
                c0 = BLOCKS[blk] if blk < NIN else (blk - NIN) * BLK
            w = w_in if g < E0 + NIN * NKP else w_out
            r0 = kp * CHUNK_KT * P
            return w[r0:r0 + CHUNK_KT * P, c0:c0 + BLK].rearrange("(k p) n -> p k n", p=P)

        def ada_source(col0, half_):
            v = w_ada.rearrange("(p k) n -> p k n", k=KT)
            return v[:, half_ * ADA_KT:(half_ + 1) * ADA_KT, col0:col0 + ADA_COLS]

        block = ctx.enter_context(nc.Block())

        @block.sync
        def _(sp):
            sp.dma_start(x_nat, x.rearrange("(t p) d -> p t d", p=P)).then_inc(x_in, 16)
            sp.dma_start(c_raw, c.rearrange("(p k) -> p k", k=KT)).then_inc(c_in, 16)
            sp.dma_start(sq[:, :], square).then_inc(square_in, 16)
            sp.dma_start(rows[0:KT, :], norm_g.rearrange("(k p) -> k p", p=P)).then_inc(rows_in, 16)
            sp.dma_start(rows[KT:3 * KT, :], b_ada[0:2 * D].rearrange("(k p) -> k p", p=P)).then_inc(rows_in, 16)
            sp.dma_start(rows[3 * KT:NROWS, :], b_alpha.rearrange("(k p) -> k p", p=P)).then_inc(rows_in, 16)

            def load_raw(g):
                if g >= RAW:
                    sp.wait_ge(lo_made, g - RAW + 1)
                elif g >= 4:
                    sp.wait_ge(xT_filled, 8)
                sp.dma_start(raw[:, g % RAW, :, :], chunk_source(g)).then_inc(raw_in[g % RAW], 16)

            def load_ada(n):
                kp, r = divmod(n, 4)
                if n >= ADA_SLOTS:
                    sp.wait_ge(ada_summed, n - ADA_SLOTS + 1)
                    pk, pr = divmod(n - ADA_SLOTS, 4)
                    if pr == 3:
                        sp.wait_ge(shift_used, pk + 1)
                col0 = (D if r < 2 else 0) + kp * ADA_COLS
                sp.dma_start(ada[n % ADA_SLOTS], ada_source(col0, r % 2)).then_inc(ada_in[n % ADA_SLOTS], 16)

            for kp in range(NKP):
                for r in range(2):
                    load_ada(4 * kp + r)
                load_raw(len(EARLY) * kp)
                for r in range(2, 4):
                    load_ada(4 * kp + r)
                for j in range(1, len(EARLY)):
                    load_raw(len(EARLY) * kp + j)
                if kp == 0:
                    narrow = ((0, IK, ID), (ID, BA, RANK), (ID + RANK, IK + ID, IH))
                    for o, c0, n in narrow:
                        sp.dma_start(nar_raw[:, :, o:o + n],
                                     w_in[:, c0:c0 + n].rearrange("(k p) n -> p k n", p=P)).then_inc(nar_in, 16)
                    sp.dma_start(w_alpha[ID:ID + RANK, :], w_alpha_up).then_inc(tables_in, 16)
                    sp.dma_start(gla_gb[:, :], gla_g.partition_broadcast(P)).then_inc(tables_in, 16)

            for s in range(STEPS):
                for i in range(HALF):
                    load_raw(E0 + HALF * s + i)
            for i in range(2 * TT):
                t, hf = divmod(i, 2)
                sp.wait_ge(z_scaled, i + 1)
                sp.dma_start(out[t * P:(t + 1) * P, hf * D // 2:(hf + 1) * D // 2],
                             z[:, t, hf * D // 2:(hf + 1) * D // 2]).then_inc(out_done, 16)
            sp.wait_ge(out_done, 16 * 2 * TT)

        @block.gpsimd
        def _(pool):
            pool.memset(ones[:, :], 1.0).then_inc(ones_made, 1)
            pool.memset(half, -0.5).then_inc(pool_step, 1)
            pool.wait_ge(pool_step, 1)
            steps = [1]

            def link(ins):
                steps[0] += 1
                ins.then_inc(pool_step, 1)
                pool.wait_ge(pool_step, steps[0])

            def rsqrt_mean(out_, sums, mean, n, done):
                link(pool.tensor_scalar(mean, sums, 1.0 / n, EPS, ALU.mult, ALU.add))
                w = sums.shape[1]
                pool.tensor_tensor(out_, mean, half.to_broadcast([P, w]), ALU.pow).then_inc(done, 1)

            pool.wait_ge(x_squared, TT)
            rsqrt_mean(stats[:, 4:6], stats[:, 0:2], stats[:, 2:4], D, x_rstd)

            pool.wait_ge(masks_in, 16)
            pool.tensor_copy(lvl_mask[:, :, :].rearrange("p l t -> p (l t)"), masks_wide).then_inc(masks_made, 1)
            pool.wait_ge(masks_made, 1)

            pool.wait_ge(cum_made, 1)
            cv = cum.rearrange("p (h t u) -> p h t u", h=HB, t=TT)
            ev = expo[0].rearrange("p (h t u) -> p h t u", h=HB, t=TT)
            pool.tensor_copy(ev[:, :, 1, :], cv[:, :, 1, :])
            pool.tensor_tensor(ev[:, :, 0, :], cv[:, :, 0, P - 1:P].to_broadcast([P, HB, P]), cv[:, :, 0, :],
                               ALU.subtract).then_inc(expo_made, 1)
            for i, m in enumerate(LEVELS):
                if i >= 1:
                    pool.wait_ge(level_made, i)
                n = HB * T // (2 * m)
                lv = cum.rearrange("p (n two m) -> p n two m", two=2, m=m)
                le = expo[(i + 1) % 2].rearrange("p (n two m) -> p n two m", two=2, m=m)
                last = lv[:, :, 0, m - 1:m].to_broadcast([P, n, m])
                pool.tensor_tensor(le[:, :, 1, :], lv[:, :, 1, :], last, ALU.subtract)
                pool.tensor_tensor(le[:, :, 0, :], last, lv[:, :, 0, :], ALU.subtract).then_inc(expo_made, 1)

            pool.wait_ge(gss_made, TT * HB)
            rsqrt_mean(grs, gss, gms, DV, grs_made)

            pool.wait_ge(zsum_made, 1)
            rsqrt_mean(zrs, zsum, stats[:, 6:8], D, z_rstd)

        @block.scalar
        def _(act):
            steps = [0]

            def link(ins):
                steps[0] += 1
                ins.then_inc(act_step, 1)
                act.wait_ge(act_step, steps[0])

            def make_hi(g):
                act.wait_ge(raw_in[g % RAW], 16 * (g // RAW + 1))
                if g >= SPLIT:
                    act.wait_ge(chunk_used, g - SPLIT + 1)
                act.activation(w_hi[:, g % SPLIT, :, :], raw[:, g % RAW, :, :], ACT.Copy).then_inc(hi_made, 1)

            def drain(name, *pairs, func=ACT.Copy, **kw):
                wait_filled(act, name)
                for d, s in pairs:
                    ins = act.activation(d, s, func, **kw)
                ins.then_inc(drained_act, 1)

            def drain_turned(stem, dst, c0, scale=1.0):
                for i in range(2):
                    name = f"{stem}{i}"
                    drain(name, (dst[:, c0 + 2 * i:c0 + 2 * i + 2, :].rearrange("p c t -> p (c t)"), side(name)[:, :]),
                          scale=scale)

            def drain_block(blk, dst, func=ACT.Copy):
                act.wait_ge(chunk_used, E0 + (blk + 1) * NKP)
                for t in range(TT):
                    ins = act.activation(dst(t), bank[2 * (blk % 2) + t][:, :], func)
                ins.then_inc(block_drained, 1)

            act.wait_ge(c_in, 16)
            act.activation(c_act, c_raw, ACT.Silu).then_inc(c_acted, 1)
            act.wait_ge(x_in, 16)
            for t in range(TT):
                act.activation(x_junk, x_nat[:, t, :], ACT.Square, accum_out=stats[:, t:t + 1]).then_inc(x_squared, 1)
                act.wait_ge(x_squared, t + 1)
            for i in range(8):
                act.wait_ge(xT_filled, i + 1)
                act.activation(xT[:, 2 * i:2 * i + 2, :].rearrange("p k t -> p (k t)"), bank[i][:, :], ACT.Copy
                               ).then_inc(xT_drained, 1)

            for kp in range(NKP):
                make_hi(len(EARLY) * kp)
                act.wait_ge(h_made, kp + 1)
                k0 = kp * CHUNK_KT
                act.activation(h_hi[:, k0:k0 + CHUNK_KT, :], xT[:, k0:k0 + CHUNK_KT, :], ACT.Copy).then_inc(h_hi_made, 1)
                for j in range(1, len(EARLY)):
                    make_hi(len(EARLY) * kp + j)
                if kp == 0:
                    act.wait_ge(nar_in, 48)
                    act.activation(nar_hi, nar_raw, ACT.Copy).then_inc(nar_hi_made, 1)
            for i in range(HALF):
                make_hi(E0 + i)
            act.wait_ge(chunk_used, E0)
            act.wait_ge(nar_done, 1)
            for j, st in ((0, 0), (2, 2)):
                for t in range(TT):
                    act.activation(stage[st][:, t, :], bank[2 * j + t][:, :], ACT.Copy).then_inc(early_drained, 1)
            act.activation(narT[0:NAR, :], bank[NAR_BANK][0:NAR, 0:T], ACT.Copy).then_inc(early_drained, 1)
            for t in range(TT):
                act.activation(stage[1][:, t, :], bank[2 + t][:, :], ACT.Copy).then_inc(early_drained, 1)

            def relus(lo, hi):
                for j in range(lo, hi):
                    if j >= 2:
                        act.wait_ge(relu_used, j - 1)
                    drain(f"idx{j}", (relu[j % 2], side(f"idx{j}")[:, 0:3 * P]), func=ACT.Relu)

            def decay(i):
                act.wait_ge(expo_made, i + 1)
                act.activation(expo[i % 2], expo[i % 2], ACT.Exp, scale=1.0 / GATE_TEMP).then_inc(decay_made, 1)

            def probs(lo, hi):
                act.wait_ge(nmax_made, lo // 4 + 1)
                for h in range(lo, hi):
                    for t, (c0, c1) in enumerate(((0, P), (P, 3 * P))):
                        ins = act.activation(prob[:, h, c0:c1], prob[:, h, c0:c1], ACT.Exp,
                                             bias=nmax[:, 2 * h + t:2 * h + t + 1],
                                             accum_out=rsum[:, 2 * h + t:2 * h + t + 1])
                    ins.then_inc(prob_made, 1)

            def drain_probT(lo, hi):
                for h in range(lo, hi):
                    drain(f"pt{h}", (probT[:, h, :], side(f"pt{h}")[:, 0:3 * P]))

            def mixT_hi(stem, hi_dst, lo_):
                for i in range(lo_, 4):
                    wait_filled(act, f"{stem}{i}")
                    act.activation(hi_dst[:, 2 * i:2 * i + 2, :].rearrange("p c t -> p (c t)"), side(f"{stem}{i}")[:, :],
                                   ACT.Copy).then_inc(mixT_hi_made, 1)

            def z_squares(blk):
                for t in range(TT):
                    act.wait_ge(z_made, 2 * blk + t + 1)
                    ins = act.activation(junk, z[:, t, blk * BLK:(blk + 1) * BLK], ACT.Square,
                                         accum_out=zss[:, 4 * t + blk:4 * t + blk + 1])
                    ins.then_inc(z_squared, 1)
                    act.wait_ge(z_squared, 2 * blk + t + 1)

            for s in range(STEPS):
                if s == 27:
                    act.wait_ge(chunk_used, E0 + NIN * NKP)
                    mixT_hi("mixB", h_hi[:, KT // 2:KT, :], 0)
                if s > 0:
                    for i in range(HALF):
                        make_hi(E0 + HALF * s + i)
                for n in GATE_LOADS.get(s, ()):
                    if n == 0:
                        wait_filled(act, "qk7")
                    if n == 3:
                        wait_filled(act, "pt7")
                    if n >= 3:
                        act.wait_ge(gate_used, n - 2)
                    act.dma_start(gate_slot(n), ada_source(2 * D + n // 2 * ADA_COLS, n % 2)
                                  ).then_inc(gate_in[n % 3], 16)
                if s == 1:
                    act.dma_start(masks_wide, masks.rearrange("s l t -> s (l t)")).then_inc(masks_in, 16)
                    act.dma_start(onehot_sb[0:BUCKETS, :], onehot).then_inc(bias_tables_in, 16)
                    act.dma_start(relb[0:BUCKETS, :], rel_bias).then_inc(bias_tables_in, 16)
                    act.dma_start(gate_b[:, :], b_ada[2 * D:3 * D].partition_broadcast(P)).then_inc(gate_bias_in, 16)
                    drain_turned("T_iq0_", iqT, 0)
                    wait_filled(act, "T_nar")
                    act.activation(ikT, side("T_nar")[:, 0:T], ACT.Copy)
                    act.activation(iws_v, side("T_nar")[:, T:T + TT * NB].rearrange("p (t n) -> p t n", t=TT)[:, :, RANK:NB],
                                   ACT.Copy, scale=IH ** -0.5 * ID ** -0.5).then_inc(drained_act, 1)
                if s == 2:
                    drain_turned("T_iq1_", iqT, 4)
                    drain_turned("T_bk_", bkT.rearrange("p (c t) -> p c t", c=HB), 0)
                    drain_block(B_BQ, lambda t: stage[0][:, t, :])
                if s == 3:
                    for i in range(2):
                        wait_filled(act, f"pre{i}")
                        for j in range(2):
                            hd = 2 * i + j
                            ins = act.activation(cum[:, hd * T:(hd + 1) * T], side(f"pre{i}")[:, j * T:(j + 1) * T],
                                                 ACT.Identity, bias=cols[:, 3 * KT + hd:3 * KT + hd + 1])
                        ins.then_inc(drained_act, 1)
                    wait_drained(act, "pre1")
                    link(act.activation(expo[0], cum, ACT.Abs))
                    link(act.activation(expo[0], expo[0], ACT.Exp, scale=-1.0))
                    act.activation(expo[0], expo[0], ACT.Ln, bias=1.0).then_inc(pre_made, 1)
                    wait_filled(act, "band")
                    act.activation(band_sb[0:HA, :], side("band")[0:HA, 0:T + P], ACT.Copy).then_inc(drained_act, 1)
                    wait_drained(act, "band")
                    act.dma_start(band_scratch, band_sb[0:HA, :]).then_inc(band_out, 16)
                if s == 4:
                    drain_turned("T_bq_", bqT.rearrange("p (c t) -> p c t", c=HB), 0, scale=DK ** -0.5)
                    relus(0, 2)
                    wait_filled(act, "idx1")
                    drain_block(B_BV, lambda t: bv[:, t, 0:BLK])
                if s == 5:
                    act.wait_ge(band_out, 16)
                    act.dma_start(hankel[:, :, :], bass.AP(band_scratch.tensor, 0, [[1, P], [T + P, HA], [1, T]])
                                  ).then_inc(hankel_in, 16)
                    relus(2, 6)
                if s == 6:
                    relus(6, 10)
                    drain_block(B_BV + 1, lambda t: bv[:, t, BLK:])
                if s == 7:
                    decay(0)
                    relus(10, 14)
                if s == 8:
                    relus(14, 16)
                    decay(1)
                    drain_block(B_AQ, lambda t: stage[0][:, t, :])
                if s == 9:
                    decay(2)
                if s == 10:
                    drain_turned("T_aq0_", qT, 0, scale=DA ** -0.5)
                    decay(3)
                    drain_block(B_AQ + 1, lambda t: stage[1][:, t, :])
                    decay(4)
                if s == 11:
                    decay(5)
                if s == 12:
                    drain_turned("T_aq1_", qT, 4, scale=DA ** -0.5)
                    drain_block(B_AK, lambda t: stage[0][:, t, :])
                    decay(6)
                    decay(7)
                if s == 14:
                    act.wait_ge(level_made, 8)
                    wait_filled(act, "L1_1")
                    drain_turned("T_ak0_", kT, 0)
                    drain_block(B_AK + 1, lambda t: stage[1][:, t, :])
                if s == 15:
                    for i in range(4):
                        t, pair = divmod(i, 2)
                        wait_filled(act, f"gla_o{i}")
                        for j in range(2):
                            n = t * HB + 2 * pair + j
                            act.activation(junk[:, 0:DV], side(f"gla_o{i}")[:, j * DV:(j + 1) * DV], ACT.Square,
                                           accum_out=gss[:, n:n + 1]).then_inc(gss_made, 1)
                            act.wait_ge(gss_made, n + 1)
                        act.activation(o_b[:, t, pair * BLK:(pair + 1) * BLK], side(f"gla_o{i}")[:, :], ACT.Copy
                                       ).then_inc(drained_act, 1)
                if s == 16:
                    drain_turned("T_ak1_", kT, 4)
                    drain_block(B_AV, lambda t: v_a[:, t, 0:BLK])
                if s == 18:
                    probs(0, 4)
                    drain_block(B_AV + 1, lambda t: v_a[:, t, BLK:])
                if s == 19:
                    drain_probT(0, 4)
                    probs(4, 8)
                if s == 20:
                    drain_probT(4, 8)
                    act.wait_ge(gate_used, 1)
                    drain_block(B_AG, lambda t: silu_a[:, t, 0:BLK], ACT.Silu)
                if s == 22:
                    drain_block(B_AG + 1, lambda t: silu_a[:, t, BLK:], ACT.Silu)
                if s == 24:
                    wait_drained(act, "pv6")
                    drain_block(B_BG, lambda t: silu_b[0][:, t, :], ACT.Silu)
                if s == 25:
                    act.wait_ge(nar_done, 1)
                    mixT_hi("mixA", a_hi, 0)
                if s == 26:
                    drain_block(B_BG + 1, lambda t: silu_b[1][:, t, :], ACT.Silu)
                    wait_drained(act, "pv6")
                    act.dma_start(fin_g, final_g.partition_broadcast(P)).then_inc(fin_in, 16)
                    wait_filled(act, "mixA3")
                    act.dma_start(z, x.rearrange("(t p) d -> p t d", p=P)).then_inc(x_again, 16)
                if s in (29, 31, 33):
                    z_squares((s - 29) // 2)
            z_squares(NOUT - 1)

        @block.vector
        def _(dve):
            steps = [0]

            def mark(ins):
                steps[0] += 1
                ins.then_inc(dve_step, 1)
                return steps[0]

            def link(ins):
                dve.wait_ge(dve_step, mark(ins))

            def make_lo(g):
                dve.wait_ge(hi_made, g + 1)
                dve.tensor_tensor(w_lo[:, g % SPLIT, :, :], raw[:, g % RAW, :, :], w_hi[:, g % SPLIT, :, :],
                                  ALU.subtract).then_inc(lo_made, 1)

            def sum_rows(slot, accs, half_, used, n=ADA_KT):
                marks = [None, None]
                for i in range(n):
                    k = half_ * ADA_KT + i
                    a = accs[i % 2]
                    if marks[i % 2]:
                        dve.wait_ge(dve_step, marks[i % 2])
                    if k < 2:
                        ins = dve.tensor_scalar(a, slot[:, i, :], c_act[:, k:k + 1], None, ALU.mult)
                    else:
                        ins = dve.scalar_tensor_tensor(out=a, in0=slot[:, i, :], scalar=c_act[:, k:k + 1], in1=a,
                                                       op0=ALU.mult, op1=ALU.add)
                    if i < n - 1:
                        marks[i % 2] = mark(ins)
                    else:
                        ins.then_inc(used, 1)
                dve.wait_ge(dve_step, marks[0])

            def sum_ada(n):
                kp, r = divmod(n, 4)
                dve.wait_ge(ada_in[n % ADA_SLOTS], 16 * (n // ADA_SLOTS + 1))
                a = 4 * (kp % 2) + 2 * (r // 2)
                if kp >= 2 and r == 0:
                    dve.wait_ge(mod_filled, kp - 1)
                if r % 2:
                    dve.wait_ge(ada_summed, n)
                sum_rows(ada[n % ADA_SLOTS], acc[a:a + 2], r % 2, ada_summed, ADA_KT - SHIFT_PE if r == 3 else ADA_KT)

            dve.wait_ge(x_rstd, 1)
            for t in range(TT):
                dve.tensor_scalar(x_nat[:, t, :], x_nat[:, t, :], stats[:, 4 + t:5 + t], None, ALU.mult
                                  ).then_inc(x_normed, 1)
            dve.wait_ge(c_acted, 1)
            for n in range(4):
                sum_ada(n)
            dve.wait_ge(cols_filled, 1)
            dve.tensor_copy(cols[:, 0:KT], bank[ADA_BANK][:, 0:KT])
            dve.tensor_scalar(cols[:, KT:2 * KT], bank[ADA_BANK][:, 2 * KT:3 * KT], 1.0, None, ALU.add)
            dve.tensor_copy(cols[:, 2 * KT:3 * KT], bank[ADA_BANK][:, KT:2 * KT])
            dve.tensor_copy(cols[:, 3 * KT:NROWS], bank[ADA_BANK][:, 3 * KT:NROWS]).then_inc(cols_made, 1)
            dve.wait_ge(cols_made, 1)
            for kp in range(NKP):
                if kp > 0:
                    for r in range(4):
                        sum_ada(4 * kp + r)
                make_lo(len(EARLY) * kp)
                if kp == 0:
                    dve.wait_ge(xT_drained, 8)
                dve.wait_ge(mod_filled, kp + 1)
                pm = bank[ADA_BANK][:, 4 * kp:4 * kp + 4].rearrange("p (a k) -> p a k", a=2)
                bias = cols[:, KT:3 * KT].rearrange("p (a k) -> p a k", a=2)[:, :, 2 * kp:2 * kp + 2]
                dve.tensor_tensor(mod.rearrange("p (a k) -> p a k", a=2), pm, bias, ALU.add).then_inc(mod_read, 1)
                dve.wait_ge(mod_read, kp + 1)
                link(dve.tensor_tensor(mod[:, 0:2], mod[:, 0:2], cols[:, 2 * kp:2 * kp + 2], ALU.mult))
                k0 = kp * CHUNK_KT
                for i in range(CHUNK_KT):
                    ins = dve.tensor_scalar(xT[:, k0 + i, :], xT[:, k0 + i, :], mod[:, i:i + 1], mod[:, 2 + i:3 + i],
                                            ALU.mult, ALU.add)
                ins.then_inc(h_made, 1)
                make_lo(len(EARLY) * kp + 1)
                dve.wait_ge(h_made, kp + 1)
                dve.wait_ge(h_hi_made, kp + 1)
                dve.tensor_tensor(h_lo[:, k0:k0 + CHUNK_KT, :], xT[:, k0:k0 + CHUNK_KT, :],
                                  h_hi[:, k0:k0 + CHUNK_KT, :], ALU.subtract).then_inc(h_lo_made, 1)
                make_lo(len(EARLY) * kp + 2)
                if kp == 0:
                    dve.wait_ge(nar_hi_made, 1)
                    dve.tensor_tensor(nar_lo, nar_raw, nar_hi, ALU.subtract).then_inc(nar_lo_made, 1)

            parts = ((0, 0, P), (1, P, 3 * P))

            def start_scores():
                dve.wait_ge(square_in, 16)
                dve.memset(score[:, P:2 * P], 0.0)
                dve.tensor_copy(score[:, 0:P], fill)
                link(dve.tensor_copy(score[:, 2 * P:3 * P], fill))

            def add_heads(lo, hi):
                for j in range(lo, hi):
                    wait_drained(dve, f"idx{j}")
                    if j > 0:
                        dve.wait_ge(relu_used, j)
                    for t, c0, c1 in parts:
                        ins = dve.scalar_tensor_tensor(out=score[:, c0:c1], in0=relu[j % 2][:, c0:c1],
                                                       scalar=iws_v[:, t, j:j + 1], in1=score[:, c0:c1],
                                                       op0=ALU.mult, op1=ALU.add)
                    ins.then_inc(relu_used, 1)

            def topk_rounds(n):
                for _ in range(n):
                    for t, c0, c1 in parts:
                        m1 = mark(dve.max(top8[:, 8 * t:8 * t + 8], score[:, c0:c1]))
                    dve.wait_ge(dve_step, m1)
                    for t, c0, c1 in parts:
                        m2 = mark(dve.match_replace(score[:, c0:c1], top8[:, 8 * t:8 * t + 8], score[:, c0:c1], TAKEN))
                    dve.wait_ge(dve_step, m2)

            def make_select():
                link(dve.tensor_scalar(select, score, TAKEN_BELOW, UNSELECTED, ALU.is_gt, ALU.mult))
                dve.tensor_tensor(select[:, 0:P], select[:, 0:P], fill, ALU.min)
                dve.tensor_tensor(select[:, 2 * P:3 * P], select[:, 2 * P:3 * P], fill, ALU.min).then_inc(select_made, 1)

            def cumulate():
                dve.wait_ge(pre_made, 1)
                resets = qk[0]
                link(dve.memset(resets, 1.0))
                dve.memset(resets.rearrange("p (n u) -> p n u", u=P)[:, :, 0:1], 0.0)
                link(dve.scalar_tensor_tensor(out=qk[1], in0=cum, scalar=0.0, in1=expo[0], op0=ALU.min,
                                              op1=ALU.subtract))
                dve.tensor_tensor_scan(cum, resets, qk[1], 0.0, ALU.mult, ALU.add).then_inc(cum_made, 1)
                dve.wait_ge(cum_made, 1)
                link(dve.memset(attn, 0.0))

            def level(i):
                m = P if i == 0 else LEVELS[i - 1]
                dve.wait_ge(decay_made, i + 1)
                if i >= 2:
                    wait_filled(dve, "cross" if i == 2 else f"L{LEVELS[i - 3]}_1")
                if i == 0:
                    wait_drained(dve, "T_bq_1")
                v = lambda a: a.rearrange("p (n two m) -> p n two m", two=2, m=m)
                dve.tensor_tensor(v(qk[i % 2])[:, :, 1, :], v(bqT)[:, :, 1, :], v(expo[i % 2])[:, :, 1, :], ALU.mult)
                dve.tensor_tensor(v(qk[i % 2])[:, :, 0, :], v(bkT)[:, :, 0, :], v(expo[i % 2])[:, :, 0, :], ALU.mult
                                  ).then_inc(level_made, 1)

            def take_level(name, t, lvl):
                wait_filled(dve, name)
                hv = lambda a: a.rearrange("p (h t) -> p h t", h=HB)
                dve.copy_predicated(hv(attn[:, t, :]), lvl_mask[:, lvl, :].unsqueeze(1).to_broadcast([P, HB, P]),
                                    hv(side(name)[:, :])).then_inc(drained_dve, 1)
                wait_drained(dve, name)

            def norm_b():
                dve.wait_ge(tables_in, 16 * 2)
                dve.wait_ge(grs_made, 1)
                wait_drained(dve, "gla_o3")
                for t in range(TT):
                    for hd in range(HB):
                        n = t * HB + hd
                        v = o_b[:, t, hd * DV:(hd + 1) * DV]
                        ins = dve.scalar_tensor_tensor(out=v, in0=v, scalar=grs[:, n:n + 1], in1=gla_gb[:, :],
                                                       op0=ALU.mult, op1=ALU.mult)
                ins.then_inc(o_b_made, 1)

            def logits(lo, hi):
                for h in range(lo, hi):
                    wait_filled(dve, f"qk{h}")
                    for t, c0, c1 in parts:
                        ins = dve.tensor_tensor_reduce(prob[:, h, c0:c1], side(f"qk{h}")[:, c0:c1], select[:, c0:c1], 1.0,
                                                       TAKEN, ALU.add, ALU.max, lmax[:, 2 * h + t:2 * h + t + 1])
                    ins.then_inc(drained_dve, 1)
                wait_drained(dve, f"qk{hi - 1}")
                dve.tensor_scalar(nmax[:, 2 * lo:2 * hi], lmax[:, 2 * lo:2 * hi], -1.0, None, ALU.mult
                                  ).then_inc(nmax_made, 1)

            def take_outputs(lo, hi):
                for h in range(lo, hi, 2):
                    wait_filled(dve, f"pv{h}")
                    for j in range(2):
                        for t in range(TT):
                            n = 2 * (h + j) + t
                            ins = dve.tensor_scalar(mix_a[:, t, (h + j) * DA:(h + j + 1) * DA],
                                                    side(f"pv{h}")[:, j * T + t * P:j * T + (t + 1) * P],
                                                    rinv[:, n:n + 1], None, ALU.mult)
                    ins.then_inc(drained_dve, 1)

            def mixT_lo(stem, hi_dst, lo_dst, before):
                for i in range(4):
                    dve.wait_ge(mixT_hi_made, before + i + 1)
                    dve.tensor_tensor(lo_dst[:, 2 * i:2 * i + 2, :].rearrange("p c t -> p (c t)"), side(f"{stem}{i}")[:, :],
                                      hi_dst[:, 2 * i:2 * i + 2, :].rearrange("p c t -> p (c t)"), ALU.subtract
                                      ).then_inc(drained_dve, 1)

            def sum_gate(n):
                j, hf = divmod(n, 2)
                dve.wait_ge(gate_in[n % 3], 16 * (n // 3 + 1))
                if hf == 0 and j >= 4:
                    wait_filled(dve, f"gate{j - 4}")
                if hf == 1:
                    dve.wait_ge(gate_used, n)
                sum_rows(gate_slot(n), gate_acc[2 * (j % 4):2 * (j % 4) + 2], hf, gate_used)

            def take_gate(j):
                wait_filled(dve, f"gate{j}")
                g = gate_b[:, j * ADA_COLS:(j + 1) * ADA_COLS]
                dve.tensor_tensor(g, side(f"gate{j}")[:, 0:ADA_COLS], g, ALU.add).then_inc(drained_dve, 1)

            def residual(blk):
                dve.wait_ge(chunk_used, E0 + (NIN + blk + 1) * NKP)
                if blk == 0:
                    dve.wait_ge(x_again, 16)
                wait_drained(dve, f"gate{2 * blk + 1}")
                cs = slice(blk * BLK, (blk + 1) * BLK)
                for t in range(TT):
                    b = 2 * ((NIN + blk) % 2) + t
                    tmp = silu_b[0][:, t, :]
                    if t == TT - 1:
                        mk = mark(dve.tensor_tensor(tmp, bank[b][:, :], gate_b[:, cs], ALU.mult))
                    else:
                        dve.tensor_tensor(tmp, bank[b][:, :], gate_b[:, cs], ALU.mult)
                dve.wait_ge(dve_step, mk)
                for t in range(TT):
                    dve.tensor_tensor(z[:, t, cs], z[:, t, cs], silu_b[0][:, t, :], ALU.add).then_inc(z_made, 1)
                dve.wait_ge(z_made, 2 * blk + 2)

            for s in range(STEPS):
                if s == 27:
                    mixT_lo("mixB", h_hi[:, KT // 2:KT, :], h_lo[:, KT // 2:KT, :], 4)
                for i in range(HALF):
                    make_lo(E0 + HALF * s + i)
                if s == 1:
                    start_scores()
                if s == 4:
                    cumulate()
                    add_heads(0, 2)
                if s == 5:
                    add_heads(2, 6)
                if s == 6:
                    add_heads(6, 10)
                if s == 7:
                    level(0)
                    add_heads(10, 14)
                if s == 8:
                    dve.wait_ge(masks_made, 1)
                    take_level("diag0", 0, 0)
                    take_level("diag1", 1, 0)
                    level(1)
                    add_heads(14, 16)
                    dve.wait_ge(relu_used, IH)
                if s == 9:
                    wait_filled(dve, "cross")
                    dve.tensor_copy(attn[:, 2, :], side("cross")[:, :]).then_inc(drained_dve, 1)
                    take_level("L64_0", 0, 1)
                    take_level("L64_1", 1, 1)
                    level(2)
                    topk_rounds(1)
                if s == 10:
                    take_level("L32_0", 0, 2)
                    take_level("L32_1", 1, 2)
                    level(3)
                    level(4)
                    topk_rounds(1)
                if s == 11:
                    for m in (16, 8):
                        for t in range(TT):
                            take_level(f"L{m}_{t}", t, 1 + LEVELS.index(m))
                    level(5)
                    topk_rounds(1)
                if s == 12:
                    take_level("L4_0", 0, 5)
                    take_level("L4_1", 1, 5)
                    level(6)
                    level(7)
                    topk_rounds(1)
                if s == 13:
                    for m in (2, 1):
                        for t in range(TT):
                            take_level(f"L{m}_{t}", t, 1 + LEVELS.index(m))
                    topk_rounds(1)
                if s in (14, 15, 16):
                    topk_rounds(1)
                if s == 16:
                    make_select()
                    dve.wait_ge(select_made, 1)
                    norm_b()
                if s == 17:
                    logits(0, 4)
                if s == 18:
                    logits(4, 8)
                if s == 20:
                    dve.wait_ge(prob_made, HA)
                    dve.reciprocal(rinv, rsum).then_inc(rinv_made, 1)
                    dve.wait_ge(rinv_made, 1)
                if s == 21:
                    take_outputs(0, 4)
                if s == 22:
                    take_outputs(4, 8)
                if s == 23:
                    dve.wait_ge(block_drained, B_AG + 2)
                    wait_drained(dve, "pv6")
                    for t in range(TT):
                        dve.tensor_tensor(mix_a[:, t, :], mix_a[:, t, :], silu_a[:, t, :], ALU.mult).then_inc(mix_a_made, 1)
                if s == 25:
                    mixT_lo("mixA", a_hi, a_lo, 0)
                if s in (25, 26):
                    j = s - 25
                    dve.wait_ge(block_drained, B_BG + 1 + j)
                    dve.wait_ge(o_b_made, 1)
                    for t in range(TT):
                        v = o_b[:, t, j * BLK:(j + 1) * BLK]
                        dve.tensor_tensor(v, v, silu_b[j][:, t, :], ALU.mult).then_inc(mix_b_made, 1)
                for j, ps in ((j, ps) for ps, j in GATE_STEPS.items() if ps + 1 == s):
                    take_gate(j)
                for n in GATE_SUMS.get(s, ()):
                    sum_gate(n)
                if s in (29, 31, 33):
                    residual((s - 29) // 2)
            residual(NOUT - 1)
            dve.wait_ge(z_squared, 2 * NOUT)
            dve.tensor_reduce(zsum, zss.rearrange("p (t n) -> p t n", t=TT), AX_X, ALU.add).then_inc(zsum_made, 1)
            dve.wait_ge(z_rstd, 1)
            dve.wait_ge(fin_in, 16)
            for t in range(TT):
                for hf in range(2):
                    cs = slice(hf * D // 2, (hf + 1) * D // 2)
                    dve.scalar_tensor_tensor(out=z[:, t, cs], in0=z[:, t, cs], scalar=zrs[:, t:t + 1], in1=fin_g[:, cs],
                                             op0=ALU.mult, op1=ALU.mult).then_inc(z_scaled, 1)

        @block.tensor
        def _(pe):
            def three(out_, hi, lo, whi, wlo, first, last):
                pe.matmul(out_, hi, whi, start=first, stop=False, skip_group_check=True)
                pe.matmul(out_, hi, wlo, start=False, stop=False, skip_group_check=True)
                return pe.matmul(out_, lo, whi, start=False, stop=last, skip_group_check=True)

            def use_chunk(g, kp, banks, s_hi, s_lo):
                pe.wait_ge(lo_made, g + 1)
                for i in range(CHUNK_KT):
                    k = kp * CHUNK_KT + i
                    for t in range(TT):
                        ts = slice(t * P, (t + 1) * P)
                        ins = three(bank[banks + t][:, :], s_hi(k)[:, ts], s_lo(k)[:, ts],
                                    w_hi[:, g % SPLIT, i, :], w_lo[:, g % SPLIT, i, :], k == 0, k == KT - 1)
                ins.then_inc(chunk_used, 1)

            def fill_side(name):
                if ORDER[name] >= 4:
                    wait_drained(pe, USES[ORDER[name] - 4][0])
                return side(name)

            def turn(stem, st, idn=ident):
                for i in range(2):
                    b = fill_side(f"{stem}{i}")
                    for j in range(2):
                        for t in range(TT):
                            c0 = (2 * i + j) * P
                            ins = pe.transpose(b[:, (2 * j + t) * P:(2 * j + t + 1) * P], st[:, t, c0:c0 + P], idn)
                    ins.then_inc(side_filled, 1)

            pe.wait_ge(square_in, 16)
            pe.wait_ge(x_normed, TT)
            for i in range(8):
                for j in range(2):
                    for t in range(TT):
                        k = 2 * i + j
                        ins = pe.transpose(bank[i][:, (2 * j + t) * P:(2 * j + t + 1) * P],
                                           x_nat[:, t, k * P:(k + 1) * P], ident)
                ins.then_inc(xT_filled, 1)
            pe.wait_ge(rows_in, 48)
            pe.wait_ge(xT_drained, 8)
            pe.transpose(bank[ADA_BANK][:, 0:NROWS], rows[0:NROWS, :], ident[0:NROWS, 0:NROWS]).then_inc(cols_filled, 1)
            pe.wait_ge(cols_made, 1)
            pe.wait_ge(c_acted, 1)

            def modulation(kp):
                pb = bank[ADA_BANK]
                if kp > 0:
                    pe.wait_ge(mod_read, kp)
                n = 4 * kp + 3
                pe.wait_ge(ada_in[n % ADA_SLOTS], 16 * (n // ADA_SLOTS + 1))
                for ct in range(2):
                    for i in range(ADA_KT - SHIFT_PE, ADA_KT):
                        ins = pe.matmul(pb[:, 4 * kp + 2 + ct:4 * kp + 3 + ct],
                                        ada[n % ADA_SLOTS][:, i, ct * P:(ct + 1) * P],
                                        c_act[:, ADA_KT + i:ADA_KT + i + 1],
                                        start=(ct == 0 and i == ADA_KT - SHIFT_PE), stop=False, skip_group_check=True)
                ins.then_inc(shift_used, 1)
                pe.wait_ge(ones_made, 1)
                for r in range(2):
                    pe.wait_ge(ada_summed, 4 * kp + 2 * r + 2)
                    for ct in range(2):
                        for i in range(2):
                            o = 4 * kp + 2 * r + ct
                            ins = pe.matmul(pb[:, o:o + 1], acc[4 * (kp % 2) + 2 * r + i][:, ct * P:(ct + 1) * P],
                                            ones[:, 0:1], start=False, stop=(i == 1), skip_group_check=True)
                ins.then_inc(mod_filled, 1)

            modulation(0)
            for kp in range(NKP):
                pe.wait_ge(h_lo_made, kp + 1)
                for j in range(len(EARLY)):
                    if j == 2 and kp < NKP - 1:
                        modulation(kp + 1)
                    use_chunk(len(EARLY) * kp + j, kp, 2 * j, lambda k: h_hi[:, k, :], lambda k: h_lo[:, k, :])
                if kp == 0:
                    pe.wait_ge(nar_lo_made, 1)
                for i in range(CHUNK_KT):
                    k = kp * CHUNK_KT + i
                    ins = three(bank[NAR_BANK][0:NAR, 0:T], nar_hi[:, k, :], nar_lo[:, k, :], h_hi[:, k, :], h_lo[:, k, :],
                                k == 0, k == KT - 1)
            ins.then_inc(nar_done, 1)

            def index_heads(lo, hi):
                for j in range(lo, hi):
                    b = fill_side(f"idx{j}")
                    r = slice((j % 2) * ID, (j % 2 + 1) * ID)
                    pe.matmul(b[:, 0:P], iqT[r, j // 2, 0:P], ikT[r, 0:P], start=True, stop=True)
                    pe.matmul(b[:, P:3 * P], iqT[r, j // 2, P:T], ikT[r, :], start=True, stop=True
                              ).then_inc(side_filled, 1)

            bqv, bkv = (a.rearrange("p (h t) -> p h t", h=HB) for a in (bqT, bkT))
            qkv = [a.rearrange("p (h t) -> p h t", h=HB) for a in qk]

            def pair_products(name, left, right):
                b = fill_side(name)
                for hd in range(HB):
                    ins = pe.matmul(b[:, hd * P:(hd + 1) * P], left(hd), right(hd), start=True, stop=True)
                ins.then_inc(side_filled, 1)

            def level_products(i):
                pe.wait_ge(level_made, i + 1)
                for t in range(TT):
                    tile = lambda hd: qkv[i % 2][:, hd, t * P:(t + 1) * P]
                    pair_products(f"L{LEVELS[i - 1]}_{t}", tile, tile)

            def turn_mix(stem, src):
                for i in range(4):
                    b = fill_side(f"{stem}{i}")
                    for j in range(2):
                        for t in range(TT):
                            c0 = (2 * i + j) * P
                            ins = pe.transpose(b[:, (2 * j + t) * P:(2 * j + t + 1) * P], src[:, t, c0:c0 + P], ident)
                    ins.then_inc(side_filled, 1)

            for s in range(STEPS):
                blk, second = divmod(s, 2)
                if second == 0:
                    if blk >= 2:
                        if blk - 2 < NIN:
                            pe.wait_ge(block_drained, blk - 1)
                        else:
                            pe.wait_ge(z_made, 2 * (blk - 2 - NIN + 1))
                    elif blk == 0:
                        pe.wait_ge(early_drained, 2)
                    else:
                        pe.wait_ge(early_drained, 7)
                if s == 26:
                    wait_drained(pe, "mixA3")
                if s == 27:
                    wait_drained(pe, "mixB3")
                if blk < NIN:
                    s_hi, s_lo = (lambda k: h_hi[:, k, :]), (lambda k: h_lo[:, k, :])
                else:
                    s_hi = lambda k: a_hi[:, k, :] if k < KT // 2 else h_hi[:, k, :]
                    s_lo = lambda k: a_lo[:, k, :] if k < KT // 2 else h_lo[:, k, :]
                for i in range(HALF):
                    use_chunk(E0 + s * HALF + i, second * HALF + i, 2 * (blk % 2), s_hi, s_lo)

                if s == 0:
                    pe.wait_ge(early_drained, 7)
                    pe.wait_ge(mod_read, NKP)
                    turn("T_iq0_", stage[0])
                    b = fill_side("T_nar")
                    for r in range(2):
                        pe.matmul(b[r * ID:(r + 1) * ID, 0:T], ident[0:ID, 0:ID], narT[0:ID, :], start=True, stop=True)
                    for t in range(TT):
                        ins = pe.transpose(b[:, T + t * NB:T + (t + 1) * NB], narT[ID:NAR, t * P:(t + 1) * P],
                                           ident[ID:NAR, ID:NAR])
                    ins.then_inc(side_filled, 1)
                if s == 1:
                    turn("T_iq1_", stage[1])
                    turn("T_bk_", stage[2])
                if s == 2:
                    pe.wait_ge(tables_in, 16 * 2)
                    pe.wait_ge(bias_tables_in, 16 * 2)
                    for i in range(2):
                        b = fill_side(f"pre{i}")
                        for j in range(2):
                            hd = 2 * i + j
                            ins = pe.matmul(b[:, j * T:(j + 1) * T], w_alpha[ID:ID + RANK, hd * DK:(hd + 1) * DK],
                                            narT[ID:ID + RANK, :], start=True, stop=True)
                        ins.then_inc(side_filled, 1)
                    b = fill_side("band")
                    pe.matmul(b[0:HA, 0:T + P], relb[0:BUCKETS, :], onehot_sb[0:BUCKETS, :], start=True, stop=True
                              ).then_inc(side_filled, 1)
                if s == 3:
                    pe.wait_ge(block_drained, B_BQ + 1)
                    turn("T_bq_", stage[0])
                    wait_drained(pe, "T_iq1_1")
                    index_heads(0, 2)
                if s in (4, 5, 6):
                    index_heads(4 * s - 14, 4 * s - 10)
                if s == 7:
                    index_heads(14, 16)
                    for t in range(TT):
                        pair_products(f"diag{t}", lambda hd: bkv[:, hd, t * P:(t + 1) * P],
                                      lambda hd: bqv[:, hd, t * P:(t + 1) * P])
                if s == 8:
                    pe.wait_ge(level_made, 1)
                    pair_products("cross", lambda hd: qkv[0][:, hd, 0:P], lambda hd: qkv[0][:, hd, P:T])
                    level_products(1)
                if s == 9:
                    pe.wait_ge(block_drained, B_AQ + 1)
                    turn("T_aq0_", stage[0])
                    level_products(2)
                if s == 10:
                    level_products(3)
                    level_products(4)
                if s == 11:
                    pe.wait_ge(block_drained, B_AQ + 2)
                    turn("T_aq1_", stage[1])
                    level_products(5)
                if s == 12:
                    level_products(6)
                    level_products(7)
                if s == 13:
                    pe.wait_ge(block_drained, B_AK + 1)
                    turn("T_ak0_", stage[0])
                if s == 14:
                    wait_drained(pe, "L1_1")
                    for i in range(4):
                        t, pair = divmod(i, 2)
                        b = fill_side(f"gla_o{i}")
                        for j in range(2):
                            hd = 2 * pair + j
                            o, vs, hs = b[:, j * DV:(j + 1) * DV], slice(hd * DV, (hd + 1) * DV), slice(hd * P, (hd + 1) * P)
                            if t == 1:
                                pe.matmul(o, attn[:, 2, hs], bv[:, 0, vs], start=True, stop=False)
                            ins = pe.matmul(o, attn[:, t, hs], bv[:, t, vs], start=(t == 0), stop=True)
                        ins.then_inc(side_filled, 1)
                if s == 15:
                    pe.wait_ge(block_drained, B_AK + 2)
                    turn("T_ak1_", stage[1])
                if s in (16, 17):
                    wait_drained(pe, "T_ak1_1")
                    pe.wait_ge(hankel_in, 16)
                    for h in range(4 * (s - 16), 4 * (s - 15)):
                        b = fill_side(f"qk{h}")
                        for t, c0, c1 in ((0, 0, P), (1, P, 3 * P)):
                            pe.matmul(b[:, c0:c1], qT[:, h, t * P:(t + 1) * P], kT[:, h, 0:c1 - c0], start=True, stop=False)
                            ins = pe.matmul(b[:, c0:c1], flip, hankel[:, h, T - (c1 - c0):T], start=False, stop=True)
                        ins.then_inc(side_filled, 1)
                if s in (18, 19):
                    for h in range(4 * (s - 18), 4 * (s - 17)):
                        b = fill_side(f"pt{h}")
                        pe.wait_ge(prob_made, h + 1)
                        for i in range(3):
                            ins = pe.transpose(b[:, i * P:(i + 1) * P], prob[:, h, i * P:(i + 1) * P], ident)
                        ins.then_inc(side_filled, 1)
                if s in (20, 21):
                    pe.wait_ge(block_drained, B_AV + 2)
                    for h in range(4 * (s - 20), 4 * (s - 19), 2):
                        b = fill_side(f"pv{h}")
                        wait_drained(pe, f"pt{h + 1}")
                        for hd in (h, h + 1):
                            o, vs = (hd - h) * T, slice(hd * DA, (hd + 1) * DA)
                            pe.matmul(b[:, o:o + P], probT[:, hd, 0:P], v_a[:, 0, vs], start=True, stop=True)
                            pe.matmul(b[:, o + P:o + T], probT[:, hd, P:2 * P], v_a[:, 0, vs], start=True, stop=False)
                            ins = pe.matmul(b[:, o + P:o + T], probT[:, hd, 2 * P:3 * P], v_a[:, 1, vs], start=False,
                                            stop=True)
                        ins.then_inc(side_filled, 1)
                if s == 24:
                    pe.wait_ge(mix_a_made, TT)
                    turn_mix("mixA", mix_a)
                if s == 26:
                    pe.wait_ge(mix_b_made, 2 * TT)
                    turn_mix("mixB", o_b)
                if s in GATE_STEPS:
                    j = GATE_STEPS[s]
                    b = fill_side(f"gate{j}")
                    pe.wait_ge(gate_used, 2 * j + 2)
                    pe.wait_ge(gate_bias_in, 16)
                    for i in range(2):
                        ins = pe.matmul(b[:, 0:ADA_COLS], ones[:, :], gate_acc[2 * (j % 4) + i], start=(i == 0), stop=(i == 1))
                    ins.then_inc(side_filled, 1)


_INS = ["x", "c", "w_ada", "b_ada", "norm_g", "w_in", "w_alpha_up", "b_alpha", "gla_g", "w_out", "rel_bias", "final_g"]


def kernel(**inputs):
    import numpy as _np
    import concourse.bacc as _bacc
    from concourse import mybir as _mybir
    from concourse.bass_utils import run_bass_kernel_spmd as _run

    nc = _bacc.Bacc("TRN2", target_bir_lowering=False, num_devices=1)
    arrays, args = {}, []
    for name in _INS:
        a = _np.ascontiguousarray(inputs[name])
        if name not in ("rel_bias", "final_g"):
            a = a[0]
        arrays[f"in_{name}"] = a
        args.append(nc.dram_tensor(f"in_{name}", a.shape, _mybir.dt.from_np(a.dtype), kind="ExternalInput").ap())
    T, D = inputs["x"].shape[1:]
    for name, a in zip(("square", "onehot", "masks"), constants(T)):
        arrays[f"const_{name}"] = a
        args.append(nc.dram_tensor(f"const_{name}", a.shape, _mybir.dt.from_np(a.dtype), kind="ExternalInput").ap())
    args.append(nc.dram_tensor("band_scratch", (inputs["rel_bias"].shape[1], T + P), _mybir.dt.float32,
                               kind="Internal").ap())
    args.append(nc.dram_tensor("out", (T, D), _mybir.dt.float32, kind="ExternalOutput").ap())
    build(nc, *args)
    r = _run(nc, [arrays], core_ids=[0])
    return r.results[0]["out"].reshape(1, T, D)
```

```python
from contextlib import ExitStack

import numpy as np
import concourse.bass as bass
from concourse import mybir

ALU = mybir.AluOpType
ACT = mybir.ActivationFunctionType
AX_X = mybir.AxisListType.X
F32 = mybir.dt.float32
F32R = mybir.dt.float32r
U8 = mybir.dt.uint8

P = 128
EPS = 1e-6
TOPK_MAX = 256
BUCKETS, MAX_DISTANCE = 32, 128
GATE_TEMP = 16.0
BLK = 512
CHUNK_KT = 2
RAW, SPLIT = 8, 4
ADA_SLOTS, ADA_KT, ADA_COLS = 5, 8, 256
SHIFT_PE = 6
SIDE_BANK = 4
CAUSAL_FILL = -3.0e38
TAKEN = -3.4e38
TAKEN_BELOW = -3.35e38
UNSELECTED = -1.0e30


def t5_bucket(dist):
    exact = BUCKETS // 2
    d = np.maximum(dist, 0)
    large = exact + (np.log(np.maximum(d, 1).astype(np.float32) / np.float32(exact))
                     / np.log(MAX_DISTANCE / exact) * (BUCKETS - exact)).astype(np.int32)
    return np.where(d < exact, d, np.minimum(large, BUCKETS - 1))


def constants(T):
    i = np.arange(P)
    ident = np.eye(P, dtype=np.float32)
    fill = np.where(i[None, :] > i[:, None], CAUSAL_FILL, 0.0).astype(np.float32)
    square = np.concatenate([ident, ident[::-1], fill], axis=1)
    dist = T - 1 - np.arange(T + P)
    onehot = (t5_bucket(dist)[None, :] == np.arange(BUCKETS)[:, None]).astype(np.float32)
    s, t = i[:, None], i[None, :]
    masks = [s == t] + [(s // (2 * m) == t // (2 * m)) & (s % (2 * m) < m) & (t % (2 * m) >= m)
                        for m in LEVELS]
    return square, onehot, np.stack(masks, 1).astype(np.float32)


LEVELS = (64, 32, 16, 8, 4, 2, 1)


def build(nc, x, c, w_ada, b_ada, norm_g, w_in, w_alpha_up, b_alpha, gla_g, w_out, rel_bias,
          final_g, square, onehot, masks, band_scratch, out):
    T, D = x.shape
    KT = D // P
    NKP = KT // CHUNK_KT
    TT = T // P
    HA, DA = rel_bias.shape[1], P
    A_W = HA * DA
    RANK, B_KW = w_alpha_up.shape
    HB, DK = B_KW // P, P
    DV = gla_g.shape[0]
    B_W = HB * DV
    IH, ID = 16, 64
    TOPK = min(TOPK_MAX, T // 4)
    assert (T, D, DK * HB, TT) == (256, 2048, 512, 2) and A_W == B_W == 1024
    AQ, AK, AV, AG = (n * A_W for n in range(4))
    IQ = 4 * A_W
    IK = IQ + IH * ID
    BQ = IK + ID + IH
    BK = BQ + B_KW
    BV = BK + B_KW
    BG = BV + B_W
    BA = BG + B_W
    NAR = ID + RANK + IH
    NB = RANK + IH
    EARLY = (IQ, IQ + BLK, BK)
    BLOCKS = (BQ, BV, BV + BLK, AQ, AQ + BLK, AK, AK + BLK, AV, AV + BLK, AG, AG + BLK,
              BG, BG + BLK)
    B_BQ, B_BV, B_AQ, B_AK, B_AV, B_AG, B_BG = 0, 1, 3, 5, 7, 9, 11
    NIN, NOUT = len(BLOCKS), D // BLK
    E0 = len(EARLY) * NKP
    CHUNKS = E0 + (NIN + NOUT) * NKP
    HALF = NKP // 2
    STEPS = 2 * (NIN + NOUT)

    def names(stem, n):
        return [f"{stem}{i}" for i in range(n)]

    PLAN = {
        0: [(n, "A") for n in names("T_iq0_", 2) + ["T_nar"]],
        1: [(n, "A") for n in names("T_iq1_", 2) + names("T_bk_", 2)],
        2: [("pre0", "A"), ("pre1", "A"), ("band", "A")],
        3: [(n, "A") for n in names("T_bq_", 2) + ["idx0", "idx1"]],
        4: [(f"idx{j}", "A") for j in range(2, 6)],
        5: [(f"idx{j}", "A") for j in range(6, 10)],
        6: [(f"idx{j}", "A") for j in range(10, 14)],
        7: [("idx14", "A"), ("idx15", "A"), ("diag0", "V"), ("diag1", "V")],
        8: [("cross", "V"), ("L64_0", "V"), ("L64_1", "V")],
        9: [("T_aq0_0", "A"), ("T_aq0_1", "A"), ("L32_0", "V"), ("L32_1", "V")],
        10: [(f"L{m}_{t}", "V") for m in (16, 8) for t in range(2)],
        11: [("T_aq1_0", "A"), ("T_aq1_1", "A"), ("L4_0", "V"), ("L4_1", "V")],
        12: [(f"L{m}_{t}", "V") for m in (2, 1) for t in range(2)],
        13: [("T_ak0_0", "A"), ("T_ak0_1", "A")],
        14: [(n, "A") for n in names("gla_o", 4)],
        15: [("T_ak1_0", "A"), ("T_ak1_1", "A")],
        16: [(f"qk{h}", "V") for h in range(4)],
        17: [(f"qk{h}", "V") for h in range(4, 8)],
        18: [(f"pt{h}", "A") for h in range(4)],
        19: [(f"pt{h}", "A") for h in range(4, 8)],
        20: [("pv0", "V"), ("pv2", "V")],
        21: [("pv4", "V"), ("pv6", "V")],
        24: [(f"mixA{i}", "V") for i in range(4)],
        26: [(f"mixB{i}", "V") for i in range(4)],
    }
    GATE_SUMS = {19: [0], 20: [1, 2], 21: [3], 22: [4], 23: [5], 24: [6], 25: [7], 26: [8], 27: [9], 28: [10, 11],
                 29: [12], 30: [13, 14], 31: [15]}
    sum_step = {n: s for s, ns in GATE_SUMS.items() for n in ns}
    GATE_LOADS = {}
    for n, s in sum_step.items():
        GATE_LOADS.setdefault(18 if n < 3 else max(s - 1, sum_step[n - 3] + 1), []).append(n)
    GATE_STEPS = {21: 0, 22: 1, 25: 2, 27: 3, 28: 4, 29: 5, 31: 6, 32: 7}
    for s, j in GATE_STEPS.items():
        PLAN.setdefault(s, []).append((f"gate{j}", "V"))
    USES = [u for s in sorted(PLAN) for u in PLAN[s]]
    ORDER = {name: i for i, (name, _) in enumerate(USES)}
    DRAINER = dict(USES)

    def drained_count(name):
        return sum(1 for n, d in USES[:ORDER[name] + 1] if d == DRAINER[name])

    with ExitStack() as ctx:
        def sb(name, shape, dt=F32):
            return ctx.enter_context(nc.sbuf_tensor(name, shape, dt))

        def sem(name):
            return ctx.enter_context(nc.semaphore(name))

        raw = sb("raw", [P, RAW, CHUNK_KT, BLK])
        w_hi = sb("w_hi", [P, SPLIT, CHUNK_KT, BLK], F32R)
        w_lo = sb("w_lo", [P, SPLIT, CHUNK_KT, BLK], F32R)
        h_hi = sb("h_hi", [P, KT, T], F32R)
        h_lo = sb("h_lo", [P, KT, T], F32R)
        a_hi = sb("a_hi", [P, KT // 2, T], F32R)
        a_lo = sb("a_lo", [P, KT // 2, T], F32R)
        nar_hi = a_hi[:, :, :].rearrange("p a t -> p (a t)")[:, 0:KT * NAR].rearrange("p (k n) -> p k n", k=KT)
        nar_lo = a_lo[:, :, :].rearrange("p a t -> p (a t)")[:, 0:KT * NAR].rearrange("p (k n) -> p k n", k=KT)
        gate_b = sb("gate_b", [P, D])
        hankel = sb("hankel", [P, HA, T])
        sq = sb("sq", [P, 3 * P])
        ident, flip, fill = sq[:, 0:P], sq[:, P:2 * P], sq[:, 2 * P:3 * P]
        lvl_mask = sb("lvl_mask", [P, 1 + len(LEVELS), P], U8)
        NROWS = 3 * KT + HB
        small = sb("small", [P, 344])
        at = [0]

        def tiny(n):
            at[0] += n
            assert at[0] <= 344
            return small[:, at[0] - n:at[0]]

        c_raw, c_act = tiny(KT), tiny(KT)
        cols = tiny(NROWS)
        mod = tiny(4)
        half = tiny(1)
        stats = tiny(8)
        iws = tiny(TT * IH)
        iws_v = iws.rearrange("p (t j) -> p t j", t=TT)
        top8 = tiny(TT * 8)
        lmax, nmax, rsum, rinv = tiny(16), tiny(16), tiny(16), tiny(16)
        gss, gms, grs = tiny(8), tiny(8), tiny(8)
        zss, zsum, zrs = tiny(8), tiny(2), tiny(2)
        gla_gb = sb("gla_gb", [P, DV])

        KW = 256
        arena = sb("arena", [P, 72 * KW])

        def place(kib, words):
            o = int(kib * KW)
            return arena[:, o:o + words]

        ada = [place(8 * i, ADA_KT * ADA_COLS).rearrange("p (k n) -> p k n", k=ADA_KT) for i in range(ADA_SLOTS)]
        xT = place(40, KT * T).rearrange("p (k t) -> p k t", k=KT)
        acc = [place(56 + i, ADA_COLS) for i in range(8)]
        rstd_diag = acc[4].rearrange("p (t n) -> p t n", t=TT)
        nar_raw = place(64, KT * NAR).rearrange("p (k n) -> p k n", k=KT)
        x_nat = raw[:, 4:8, :, :].rearrange("p a k n -> p (a k n)").rearrange("p (t d) -> p t d", t=TT)
        x_junk = place(40, D)
        rows = place(70, P)
        onehot_sb = place(68.25, T + P)
        relb = place(69.75, HA)
        stage = [place(4 * i, TT * BLK).rearrange("p (t n) -> p t n", t=TT) for i in range(3)]
        masks_wide = place(36, (1 + len(LEVELS)) * P)
        relu = [place(8 + 1.5 * i, 3 * P) for i in range(2)]
        iqT = place(12, 8 * T).rearrange("p (c t) -> p c t", c=8)
        bkT, bqT = place(20, HB * T), place(24, HB * T)
        cum = place(28, HB * T)
        expo = [place(32, HB * T), place(36, HB * T)]
        qk = [place(40, HB * T), place(44, HB * T)]
        attn = place(48, 3 * BLK).rearrange("p (b n) -> p b n", b=3)
        bv = place(54, TT * B_W).rearrange("p (t n) -> p t n", t=TT)
        score = place(62, 3 * P)
        select = place(63.5, 3 * P)
        narT = place(66.25, T)
        ikT = place(67.25, T)
        band_sb = place(70, T + P)
        qT = place(12, HA * T).rearrange("p (h t) -> p h t", h=HA)
        kT = place(20, HA * T).rearrange("p (h t) -> p h t", h=HA)
        o_b = place(28, TT * B_W).rearrange("p (t n) -> p t n", t=TT)
        prob = place(36, HA * 3 * P).rearrange("p (h n) -> p h n", h=HA)
        v_a = place(54, TT * A_W).rearrange("p (t n) -> p t n", t=TT)
        probT = place(0, HA * 3 * P).rearrange("p (h n) -> p h n", h=HA)
        silu_a = place(12, TT * A_W).rearrange("p (t n) -> p t n", t=TT)
        mix_a = place(20, TT * A_W).rearrange("p (t n) -> p t n", t=TT)
        silu_b = [place(4 * i, TT * BLK).rearrange("p (t n) -> p t n", t=TT) for i in range(2)]
        slot = lambda a: a.rearrange("p (k n) -> p k n", k=ADA_KT)
        hankel_slot = slot(hankel[:, :, :].rearrange("p h t -> p (h t)"))
        gate_first = [slot(place(12, ADA_KT * ADA_COLS)), slot(place(20, ADA_KT * ADA_COLS))]
        gate_late = [slot(place(36, ADA_KT * ADA_COLS)), slot(place(44, ADA_KT * ADA_COLS))]

        def gate_slot(n):
            return hankel_slot if n % 3 == 2 else (gate_first if n < 3 else gate_late)[n % 3]
        gate_acc = [place(62 + i, ADA_COLS) for i in range(8)]
        junk = place(8, D)[:, 0:BLK]
        z = place(12, TT * D).rearrange("p (t d) -> p t d", t=TT)
        fin_g = place(54, D)
        ACT_COLS = 3 * D // 8

        def z_part(blk, t):
            return silu_b[1][:, t, :] if blk == NOUT - 1 else z[:, t, blk * BLK:(blk + 1) * BLK]
        w_alpha = sb("w_alpha", [ID + RANK, B_KW])
        ones = sb("ones", [P, P])

        bank = [ctx.enter_context(nc.psum_tensor(f"bank{i}", [P, BLK], F32)) for i in range(8)]
        ADA_BANK, NAR_BANK = 7, 6

        def side(name):
            return bank[SIDE_BANK + ORDER[name] % 4]

        x_in = [sem(f"x_in{t}") for t in range(TT)]
        c_in, rows_in, square_in, tables_in, nar_in = (
            sem(n) for n in ("c_in", "rows_in", "square_in", "tables_in", "nar_in"))
        raw_in = [sem(f"raw_in{i}") for i in range(RAW)]
        ada_in = [sem(f"ada_in{i}") for i in range(ADA_SLOTS)]
        gate_in = [sem(f"gate_in{i}") for i in range(3)]
        bias_tables_in = sem("bias_tables_in")
        band_out, hankel_in, x_again, fin_in, gate_bias_in = (
            sem(n) for n in ("band_out", "hankel_in", "x_again", "fin_in", "gate_bias_in"))
        out_done = sem("out_done")
        hi_made, lo_made, chunk_used = sem("hi_made"), sem("lo_made"), sem("chunk_used")
        nar_hi_made, nar_lo_made, nar_done = sem("nar_hi_made"), sem("nar_lo_made"), sem("nar_done")
        early_drained, block_drained = sem("early_drained"), sem("block_drained")
        x_squared, x_rstd, diag_made, xT_filled, xT_drained = (
            sem(n) for n in ("x_squared", "x_rstd", "diag_made", "xT_filled", "xT_drained"))
        c_acted, cols_filled, cols_made = sem("c_acted"), sem("cols_filled"), sem("cols_made")
        ada_summed, shift_used, acc_folded = sem("ada_summed"), sem("shift_used"), sem("acc_folded")
        mod_filled, mod_read, mod_made = sem("mod_filled"), sem("mod_read"), sem("mod_made")
        h_made, h_hi_made, h_lo_made = sem("h_made"), sem("h_hi_made"), sem("h_lo_made")
        side_filled, drained_act, drained_dve = sem("side_filled"), sem("drained_act"), sem("drained_dve")
        pre_made, cum_made = sem("pre_made"), sem("cum_made")
        ones_made, masks_in, masks_made = sem("ones_made"), sem("masks_in"), sem("masks_made")
        expo_made, decay_made, level_made = sem("expo_made"), sem("decay_made"), sem("level_made")
        relu_used, select_made = sem("relu_used"), sem("select_made")
        gss_made, grs_made, o_b_made = sem("gss_made"), sem("grs_made"), sem("o_b_made")
        nmax_made, prob_made, rinv_made = sem("nmax_made"), sem("prob_made"), sem("rinv_made")
        silu_a_made, mix_a_made, silu_b_made, mix_b_made = (
            sem(n) for n in ("silu_a_made", "mix_a_made", "silu_b_made", "mix_b_made"))
        mixT_hi_made = sem("mixT_hi_made")
        gate_used, gate_folded = sem("gate_used"), sem("gate_folded")
        y_gated, last_filled = sem("y_gated"), sem("last_filled")
        z_made, z_squared, z_weighted, zsum_made, z_rstd, scaled_act, scaled_dve = (
            sem(n) for n in ("z_made", "z_squared", "z_weighted", "zsum_made", "z_rstd", "scaled_act", "scaled_dve"))
        act_step, dve_step, pool_step = sem("act_step"), sem("dve_step"), sem("pool_step")

        def wait_drained(eng, name):
            eng.wait_ge(drained_act if DRAINER[name] == "A" else drained_dve, drained_count(name))

        def wait_filled(eng, name):
            eng.wait_ge(side_filled, ORDER[name] + 1)

        def block_of(s):
            return {2 * NIN + 1: (NIN + 1, 0), 2 * NIN + 2: (NIN, 1)}.get(s, divmod(s, 2))

        OUT_DONE = [2 * NIN + 2, 2 * NIN + 3, 2 * NIN + 5, 2 * NIN + 7]

        def chunk_source(g):
            if g < E0:
                kp, c0 = g // len(EARLY), EARLY[g % len(EARLY)]
            else:
                step, i = divmod(g - E0, HALF)
                blk, second = block_of(step)
                kp = second * HALF + i
                c0 = BLOCKS[blk] if blk < NIN else (blk - NIN) * BLK
            w = w_in if g < E0 + NIN * NKP else w_out
            r0 = kp * CHUNK_KT * P
            return w[r0:r0 + CHUNK_KT * P, c0:c0 + BLK].rearrange("(k p) n -> p k n", p=P)

        def ada_source(col0, half_):
            v = w_ada.rearrange("(p k) n -> p k n", k=KT)
            return v[:, half_ * ADA_KT:(half_ + 1) * ADA_KT, col0:col0 + ADA_COLS]

        block = ctx.enter_context(nc.Block())

        @block.sync
        def _(sp):
            sp.dma_start(c_raw, c.rearrange("(p k) -> p k", k=KT)).then_inc(c_in, 16)

            def load_raw(g):
                if g >= RAW:
                    sp.wait_ge(lo_made, g - RAW + 1)
                elif g >= 4:
                    sp.wait_ge(xT_filled, 8)
                sp.dma_start(raw[:, g % RAW, :, :], chunk_source(g)).then_inc(raw_in[g % RAW], 16)

            def load_ada(n):
                kp, r = divmod(n, 4)
                if n >= ADA_SLOTS:
                    sp.wait_ge(ada_summed, n - ADA_SLOTS + 1)
                    pk, pr = divmod(n - ADA_SLOTS, 4)
                    if pr == 3:
                        sp.wait_ge(shift_used, pk + 1)
                col0 = (D if r < 2 else 0) + kp * ADA_COLS
                sp.dma_start(ada[n % ADA_SLOTS], ada_source(col0, r % 2)).then_inc(ada_in[n % ADA_SLOTS], 16)

            load_ada(0)
            for t in range(TT):
                sp.dma_start(x_nat[:, t, :], x[t * P:(t + 1) * P, :]).then_inc(x_in[t], 16)
            sp.dma_start(sq[:, :], square).then_inc(square_in, 16)
            for r in range(1, 4):
                load_ada(r)
            sp.dma_start(rows[0:KT, :], norm_g.rearrange("(k p) -> k p", p=P)).then_inc(rows_in, 16)
            sp.dma_start(rows[KT:3 * KT, :], b_ada[0:2 * D].rearrange("(k p) -> k p", p=P)).then_inc(rows_in, 16)
            sp.dma_start(rows[3 * KT:NROWS, :], b_alpha.rearrange("(k p) -> k p", p=P)).then_inc(rows_in, 16)
            for j in range(len(EARLY)):
                load_raw(j)
            for kp in range(NKP):
                if kp > 0:
                    for j in range(len(EARLY)):
                        load_ada(4 * kp + j)
                        load_raw(len(EARLY) * kp + j)
                    load_ada(4 * kp + 3)
                if kp == 1:
                    narrow = ((0, IK, ID), (ID, BA, RANK), (ID + RANK, IK + ID, IH))
                    for o, c0, n in narrow:
                        sp.dma_start(nar_raw[:, :, o:o + n],
                                     w_in[:, c0:c0 + n].rearrange("(k p) n -> p k n", p=P)).then_inc(nar_in, 16)
                    sp.dma_start(w_alpha[ID:ID + RANK, :], w_alpha_up).then_inc(tables_in, 16)
                    sp.dma_start(gla_gb[:, :], gla_g.partition_broadcast(P)).then_inc(tables_in, 16)

            for s in range(STEPS):
                for i in range(HALF):
                    load_raw(E0 + HALF * s + i)
            for t in range(TT):
                for scaled, c0, c1 in ((scaled_dve, ACT_COLS, D), (scaled_act, 0, ACT_COLS)):
                    sp.wait_ge(scaled, t + 1)
                    sp.dma_start(out[t * P:(t + 1) * P, c0:c1], z[:, t, c0:c1]).then_inc(out_done, 16)
            sp.wait_ge(out_done, 16 * 2 * TT)

        @block.gpsimd
        def _(pool):
            pool.memset(ones[:, :], 1.0).then_inc(ones_made, 1)
            pool.memset(half, -0.5).then_inc(pool_step, 1)
            pool.wait_ge(pool_step, 1)
            steps = [1]

            def link(ins):
                steps[0] += 1
                ins.then_inc(pool_step, 1)
                pool.wait_ge(pool_step, steps[0])

            def rsqrt_mean(out_, sums, mean, n, done):
                link(pool.tensor_scalar(mean, sums, 1.0 / n, EPS, ALU.mult, ALU.add))
                w = sums.shape[1]
                pool.tensor_tensor(out_, mean, half.to_broadcast([P, w]), ALU.pow).then_inc(done, 1)

            for t in range(TT):
                pool.wait_ge(x_squared, t + 1)
                rsqrt_mean(stats[:, 4 + t:5 + t], stats[:, t:t + 1], stats[:, 2 + t:3 + t], D, x_rstd)

            for kp in range(NKP):
                for r in range(2):
                    pool.wait_ge(ada_summed, 4 * kp + 2 * r + 2)
                    even, odd = acc[4 * (kp % 2) + 2 * r:4 * (kp % 2) + 2 * r + 2]
                    pool.tensor_tensor(even, even, odd, ALU.add).then_inc(acc_folded, 1)

            pool.wait_ge(masks_in, 16)
            pool.tensor_copy(lvl_mask[:, :, :].rearrange("p l t -> p (l t)"), masks_wide).then_inc(masks_made, 1)
            pool.wait_ge(masks_made, 1)

            pool.wait_ge(cum_made, 1)
            cv = cum.rearrange("p (h t u) -> p h t u", h=HB, t=TT)
            ev = expo[0].rearrange("p (h t u) -> p h t u", h=HB, t=TT)
            pool.tensor_copy(ev[:, :, 1, :], cv[:, :, 1, :])
            pool.tensor_tensor(ev[:, :, 0, :], cv[:, :, 0, P - 1:P].to_broadcast([P, HB, P]), cv[:, :, 0, :],
                               ALU.subtract).then_inc(expo_made, 1)
            for i, m in enumerate(LEVELS):
                if i >= 1:
                    pool.wait_ge(level_made, i)
                n = HB * T // (2 * m)
                lv = cum.rearrange("p (n two m) -> p n two m", two=2, m=m)
                le = expo[(i + 1) % 2].rearrange("p (n two m) -> p n two m", two=2, m=m)
                last = lv[:, :, 0, m - 1:m].to_broadcast([P, n, m])
                pool.tensor_tensor(le[:, :, 1, :], lv[:, :, 1, :], last, ALU.subtract)
                pool.tensor_tensor(le[:, :, 0, :], last, lv[:, :, 0, :], ALU.subtract).then_inc(expo_made, 1)

            pool.wait_ge(gss_made, TT * HB)
            rsqrt_mean(grs, gss, gms, DV, grs_made)

            for j in range(D // ADA_COLS):
                pool.wait_ge(gate_used, 2 * j + 2)
                even, odd = gate_acc[2 * (j % 4):2 * (j % 4) + 2]
                pool.tensor_tensor(even, even, odd, ALU.add).then_inc(gate_folded, 1)

            pool.wait_ge(fin_in, 16)
            for blk in range(NOUT - 1):
                pool.wait_ge(z_squared, TT * (blk + 1))
                cs = slice(blk * BLK, (blk + 1) * BLK)
                for t in range(TT):
                    pool.tensor_tensor(z[:, t, cs], z[:, t, cs], fin_g[:, cs], ALU.mult).then_inc(z_weighted, 1)
            for t in range(TT):
                pool.wait_ge(zsum_made, t + 1)
                rsqrt_mean(zrs[:, t:t + 1], zsum[:, t:t + 1], stats[:, 6 + t:7 + t], D, z_rstd)

        @block.scalar
        def _(act):
            steps = [0]

            def link(ins):
                steps[0] += 1
                ins.then_inc(act_step, 1)
                act.wait_ge(act_step, steps[0])

            def make_hi(g):
                act.wait_ge(raw_in[g % RAW], 16 * (g // RAW + 1))
                if g >= SPLIT:
                    act.wait_ge(chunk_used, g - SPLIT + 1)
                act.activation(w_hi[:, g % SPLIT, :, :], raw[:, g % RAW, :, :], ACT.Copy).then_inc(hi_made, 1)

            def drain(name, *pairs, func=ACT.Copy, **kw):
                wait_filled(act, name)
                for d, s in pairs:
                    ins = act.activation(d, s, func, **kw)
                ins.then_inc(drained_act, 1)

            def drain_turned(stem, dst, c0, scale=1.0):
                for i in range(2):
                    name = f"{stem}{i}"
                    drain(name, (dst[:, c0 + 2 * i:c0 + 2 * i + 2, :].rearrange("p c t -> p (c t)"), side(name)[:, :]),
                          scale=scale)

            def drain_block(blk, dst, func=ACT.Copy):
                act.wait_ge(chunk_used, E0 + (blk + 1) * NKP)
                for t in range(TT):
                    ins = act.activation(dst(t), bank[2 * (blk % 2) + t][:, :], func)
                ins.then_inc(block_drained, 1)

            act.wait_ge(c_in, 16)
            act.activation(c_act, c_raw, ACT.Silu).then_inc(c_acted, 1)
            for t in range(TT):
                act.wait_ge(x_in[t], 16)
                act.activation(x_junk, x_nat[:, t, :], ACT.Square, accum_out=stats[:, t:t + 1]).then_inc(x_squared, 1)
                act.wait_ge(x_squared, t + 1)
            for i in range(8):
                act.wait_ge(xT_filled, i + 1)
                act.activation(xT[:, 2 * i:2 * i + 2, :].rearrange("p k t -> p (k t)"), bank[i % 6][:, :], ACT.Copy
                               ).then_inc(xT_drained, 1)
            act.wait_ge(xT_drained, 8)

            for kp in range(NKP):
                ahead = len(EARLY) if kp == NKP - 1 else 2
                for j in range(ahead):
                    make_hi(len(EARLY) * kp + j)
                k0 = kp * CHUNK_KT
                act.wait_ge(mod_made, kp + 1)
                for i in range(CHUNK_KT):
                    act.activation(xT[:, k0 + i, :], xT[:, k0 + i, :], ACT.Identity, scale=mod[:, i:i + 1],
                                   bias=mod[:, 2 + i:3 + i]).then_inc(h_made, 1)
                act.wait_ge(h_made, CHUNK_KT * (kp + 1))
                act.activation(h_hi[:, k0:k0 + CHUNK_KT, :], xT[:, k0:k0 + CHUNK_KT, :], ACT.Copy).then_inc(h_hi_made, 1)
                for j in range(ahead, len(EARLY)):
                    make_hi(len(EARLY) * kp + j)
                if kp == 1:
                    act.wait_ge(nar_in, 48)
                    act.activation(nar_hi, nar_raw, ACT.Copy).then_inc(nar_hi_made, 1)
            make_hi(E0)
            act.wait_ge(chunk_used, E0 - 2)
            for t in range(TT):
                act.activation(stage[0][:, t, :], bank[t][:, :], ACT.Copy).then_inc(early_drained, 1)
            make_hi(E0 + 1)
            act.wait_ge(chunk_used, E0)
            act.wait_ge(nar_done, 1)
            for t in range(TT):
                act.activation(stage[2][:, t, :], bank[4 + t][:, :], ACT.Copy).then_inc(early_drained, 1)
            act.activation(narT[0:NAR, :], bank[NAR_BANK][0:NAR, 0:T], ACT.Copy).then_inc(early_drained, 1)
            for t in range(TT):
                act.activation(stage[1][:, t, :], bank[2 + t][:, :], ACT.Copy).then_inc(early_drained, 1)
            for i in range(2, HALF):
                make_hi(E0 + i)

            def relus(lo, hi):
                for j in range(lo, hi):
                    if j >= 2:
                        act.wait_ge(relu_used, j - 1)
                    drain(f"idx{j}", (relu[j % 2], side(f"idx{j}")[:, 0:3 * P]), func=ACT.Relu)

            def decay(i):
                act.wait_ge(expo_made, i + 1)
                act.activation(expo[i % 2], expo[i % 2], ACT.Exp, scale=1.0 / GATE_TEMP).then_inc(decay_made, 1)

            def probs(lo, hi):
                act.wait_ge(nmax_made, lo // 4 + 1)
                for h in range(lo, hi):
                    for t, (c0, c1) in enumerate(((0, P), (P, 3 * P))):
                        ins = act.activation(prob[:, h, c0:c1], prob[:, h, c0:c1], ACT.Exp,
                                             bias=nmax[:, 2 * h + t:2 * h + t + 1],
                                             accum_out=rsum[:, 2 * h + t:2 * h + t + 1])
                    ins.then_inc(prob_made, 1)

            def drain_probT(lo, hi):
                for h in range(lo, hi):
                    drain(f"pt{h}", (probT[:, h, :], side(f"pt{h}")[:, 0:3 * P]))

            def mixT_hi(stem, hi_dst, lo_):
                for i in range(lo_, 4):
                    wait_filled(act, f"{stem}{i}")
                    act.activation(hi_dst[:, 2 * i:2 * i + 2, :].rearrange("p c t -> p (c t)"), side(f"{stem}{i}")[:, :],
                                   ACT.Copy).then_inc(mixT_hi_made, 1)

            def z_square(blk, t):
                act.wait_ge(z_made, TT * blk + t + 1)
                if blk + t > 0:
                    act.wait_ge(z_squared, TT * blk + t)
                act.activation(junk, z_part(blk, t), ACT.Square,
                               accum_out=zss[:, NOUT * t + blk:NOUT * t + blk + 1]).then_inc(z_squared, 1)

            for s in range(STEPS):
                if s > 0:
                    for i in range(HALF):
                        make_hi(E0 + HALF * s + i)
                if s == 27:
                    act.wait_ge(chunk_used, E0 + NIN * NKP)
                    mixT_hi("mixB", h_hi[:, KT // 2:KT, :], 0)
                for n in GATE_LOADS.get(s, ()):
                    if n == 0:
                        wait_filled(act, "qk7")
                    if n == 3:
                        wait_filled(act, "pt7")
                    if n >= 3:
                        act.wait_ge(gate_used, n - 2)
                    act.dma_start(gate_slot(n), ada_source(2 * D + n // 2 * ADA_COLS, n % 2)
                                  ).then_inc(gate_in[n % 3], 16)
                if s == 1:
                    act.dma_start(masks_wide, masks.rearrange("s l t -> s (l t)")).then_inc(masks_in, 16)
                    act.dma_start(onehot_sb[0:BUCKETS, :], onehot).then_inc(bias_tables_in, 16)
                    act.dma_start(relb[0:BUCKETS, :], rel_bias).then_inc(bias_tables_in, 16)
                    act.dma_start(gate_b[:, :], b_ada[2 * D:3 * D].partition_broadcast(P)).then_inc(gate_bias_in, 16)
                    drain_turned("T_iq0_", iqT, 0)
                    wait_filled(act, "T_nar")
                    act.activation(ikT, side("T_nar")[:, 0:T], ACT.Copy)
                    act.activation(iws_v, side("T_nar")[:, T:T + TT * NB].rearrange("p (t n) -> p t n", t=TT)[:, :, RANK:NB],
                                   ACT.Copy, scale=IH ** -0.5 * ID ** -0.5).then_inc(drained_act, 1)
                if s == 2:
                    drain_turned("T_iq1_", iqT, 4)
                    drain_turned("T_bk_", bkT.rearrange("p (c t) -> p c t", c=HB), 0)
                    drain_block(B_BQ, lambda t: stage[0][:, t, :])
                if s == 3:
                    for i in range(2):
                        wait_filled(act, f"pre{i}")
                        for j in range(2):
                            hd = 2 * i + j
                            ins = act.activation(cum[:, hd * T:(hd + 1) * T], side(f"pre{i}")[:, j * T:(j + 1) * T],
                                                 ACT.Identity, bias=cols[:, 3 * KT + hd:3 * KT + hd + 1])
                        ins.then_inc(drained_act, 1)
                    wait_drained(act, "pre1")
                    link(act.activation(expo[0], cum, ACT.Abs))
                    link(act.activation(expo[0], expo[0], ACT.Exp, scale=-1.0))
                    act.activation(expo[0], expo[0], ACT.Ln, bias=1.0).then_inc(pre_made, 1)
                    wait_filled(act, "band")
                    act.activation(band_sb[0:HA, :], side("band")[0:HA, 0:T + P], ACT.Copy).then_inc(drained_act, 1)
                    wait_drained(act, "band")
                    act.dma_start(band_scratch, band_sb[0:HA, :]).then_inc(band_out, 16)
                if s == 4:
                    drain_turned("T_bq_", bqT.rearrange("p (c t) -> p c t", c=HB), 0, scale=DK ** -0.5)
                    relus(0, 2)
                    wait_filled(act, "idx1")
                    drain_block(B_BV, lambda t: bv[:, t, 0:BLK])
                if s == 5:
                    act.wait_ge(band_out, 16)
                    act.dma_start(hankel[:, :, :], bass.AP(band_scratch.tensor, 0, [[1, P], [T + P, HA], [1, T]])
                                  ).then_inc(hankel_in, 16)
                    relus(2, 6)
                if s == 6:
                    relus(6, 10)
                    drain_block(B_BV + 1, lambda t: bv[:, t, BLK:])
                if s == 7:
                    decay(0)
                    relus(10, 14)
                if s == 8:
                    relus(14, 16)
                    decay(1)
                    drain_block(B_AQ, lambda t: stage[0][:, t, :])
                if s == 9:
                    decay(2)
                if s == 10:
                    drain_turned("T_aq0_", qT, 0, scale=DA ** -0.5)
                    decay(3)
                    drain_block(B_AQ + 1, lambda t: stage[1][:, t, :])
                    decay(4)
                if s == 11:
                    decay(5)
                if s == 12:
                    drain_turned("T_aq1_", qT, 4, scale=DA ** -0.5)
                    drain_block(B_AK, lambda t: stage[0][:, t, :])
                    decay(6)
                    decay(7)
                if s == 14:
                    act.wait_ge(level_made, 8)
                    wait_filled(act, "L1_1")
                    drain_turned("T_ak0_", kT, 0)
                    drain_block(B_AK + 1, lambda t: stage[1][:, t, :])
                if s == 15:
                    for i in range(4):
                        t, pair = divmod(i, 2)
                        wait_filled(act, f"gla_o{i}")
                        for j in range(2):
                            n = t * HB + 2 * pair + j
                            act.activation(junk[:, 0:DV], side(f"gla_o{i}")[:, j * DV:(j + 1) * DV], ACT.Square,
                                           accum_out=gss[:, n:n + 1]).then_inc(gss_made, 1)
                            act.wait_ge(gss_made, n + 1)
                        act.activation(o_b[:, t, pair * BLK:(pair + 1) * BLK], side(f"gla_o{i}")[:, :], ACT.Copy
                                       ).then_inc(drained_act, 1)
                if s == 16:
                    drain_turned("T_ak1_", kT, 4)
                    drain_block(B_AV, lambda t: v_a[:, t, 0:BLK])
                if s == 18:
                    probs(0, 4)
                    drain_block(B_AV + 1, lambda t: v_a[:, t, BLK:])
                if s == 19:
                    drain_probT(0, 4)
                    probs(4, 8)
                if s == 20:
                    drain_probT(4, 8)
                    act.wait_ge(gate_used, 1)
                    drain_block(B_AG, lambda t: silu_a[:, t, 0:BLK], ACT.Silu)
                if s == 22:
                    drain_block(B_AG + 1, lambda t: silu_a[:, t, BLK:], ACT.Silu)
                if s == 24:
                    wait_drained(act, "pv6")
                    drain_block(B_BG, lambda t: silu_b[0][:, t, :], ACT.Silu)
                if s == 25:
                    act.wait_ge(nar_done, 1)
                    mixT_hi("mixA", a_hi, 0)
                if s == 26:
                    drain_block(B_BG + 1, lambda t: silu_b[1][:, t, :], ACT.Silu)
                    wait_drained(act, "pv6")
                    act.dma_start(fin_g, final_g.partition_broadcast(P)).then_inc(fin_in, 16)
                    wait_filled(act, "mixA3")
                    act.dma_start(z, x.rearrange("(t p) d -> p t d", p=P)).then_inc(x_again, 16)
                for blk in range(NOUT - 1):
                    if s == min(OUT_DONE[blk] + 2, STEPS - 1):
                        for t in range(TT):
                            z_square(blk, t)
            for t in range(TT):
                z_square(NOUT - 1, t)
                act.wait_ge(z_weighted, TT * (NOUT - 1))
                act.wait_ge(z_rstd, t + 1)
                act.activation(z[:, t, 0:ACT_COLS], z[:, t, 0:ACT_COLS], ACT.Copy, scale=zrs[:, t:t + 1]
                               ).then_inc(scaled_act, 1)

        @block.vector
        def _(dve):
            steps = [0]

            def mark(ins):
                steps[0] += 1
                ins.then_inc(dve_step, 1)
                return steps[0]

            def link(ins):
                dve.wait_ge(dve_step, mark(ins))

            def make_lo(g):
                dve.wait_ge(hi_made, g + 1)
                dve.tensor_tensor(w_lo[:, g % SPLIT, :, :], raw[:, g % RAW, :, :], w_hi[:, g % SPLIT, :, :],
                                  ALU.subtract).then_inc(lo_made, 1)

            def sum_rows(slot, accs, half_, used, n=ADA_KT):
                marks = [None, None]
                for i in range(n):
                    k = half_ * ADA_KT + i
                    a = accs[i % 2]
                    if marks[i % 2]:
                        dve.wait_ge(dve_step, marks[i % 2])
                    if k < 2:
                        ins = dve.tensor_scalar(a, slot[:, i, :], c_act[:, k:k + 1], None, ALU.mult)
                    else:
                        ins = dve.scalar_tensor_tensor(out=a, in0=slot[:, i, :], scalar=c_act[:, k:k + 1], in1=a,
                                                       op0=ALU.mult, op1=ALU.add)
                    if i < n - 1:
                        marks[i % 2] = mark(ins)
                    else:
                        ins.then_inc(used, 1)
                dve.wait_ge(dve_step, marks[0])

            def sum_ada(n):
                kp, r = divmod(n, 4)
                dve.wait_ge(ada_in[n % ADA_SLOTS], 16 * (n // ADA_SLOTS + 1))
                a = 4 * (kp % 2) + 2 * (r // 2)
                if kp >= 2 and r == 0:
                    dve.wait_ge(mod_filled, kp - 1)
                if r % 2:
                    dve.wait_ge(ada_summed, n)
                sum_rows(ada[n % ADA_SLOTS], acc[a:a + 2], r % 2, ada_summed, ADA_KT - SHIFT_PE if r == 3 else ADA_KT)

            dve.wait_ge(c_acted, 1)
            sum_ada(0)
            dve.wait_ge(square_in, 16)
            for t in range(TT):
                dve.wait_ge(x_rstd, t + 1)
                dve.tensor_scalar(rstd_diag[:, t, :], ident, stats[:, 4 + t:5 + t], None, ALU.mult
                                  ).then_inc(diag_made, 1)
            for n in range(1, 4):
                sum_ada(n)
            dve.wait_ge(cols_filled, 1)
            dve.tensor_copy(cols[:, 0:KT], bank[ADA_BANK][:, 0:KT])
            dve.tensor_scalar(cols[:, KT:2 * KT], bank[ADA_BANK][:, 2 * KT:3 * KT], 1.0, None, ALU.add)
            dve.tensor_copy(cols[:, 2 * KT:3 * KT], bank[ADA_BANK][:, KT:2 * KT])
            dve.tensor_copy(cols[:, 3 * KT:NROWS], bank[ADA_BANK][:, 3 * KT:NROWS]).then_inc(cols_made, 1)
            dve.wait_ge(cols_made, 1)
            dve.wait_ge(xT_filled, 8)
            for kp in range(NKP):
                if kp > 0 and kp < NKP - 1:
                    sum_ada(4 * kp + 4)
                ahead = len(EARLY) if kp == NKP - 1 else 1
                for j in range(ahead):
                    make_lo(len(EARLY) * kp + j)
                dve.wait_ge(mod_filled, kp + 1)
                pm = bank[ADA_BANK][:, 4 * kp:4 * kp + 4].rearrange("p (a k) -> p a k", a=2)
                bias = cols[:, KT:3 * KT].rearrange("p (a k) -> p a k", a=2)[:, :, 2 * kp:2 * kp + 2]
                dve.tensor_tensor(mod.rearrange("p (a k) -> p a k", a=2), pm, bias, ALU.add).then_inc(mod_read, 1)
                dve.wait_ge(mod_read, kp + 1)
                dve.tensor_tensor(mod[:, 0:2], mod[:, 0:2], cols[:, 2 * kp:2 * kp + 2], ALU.mult).then_inc(mod_made, 1)
                k0 = kp * CHUNK_KT
                if kp < NKP - 1:
                    make_lo(len(EARLY) * kp + 1)
                dve.wait_ge(h_hi_made, kp + 1)
                dve.tensor_tensor(h_lo[:, k0:k0 + CHUNK_KT, :], xT[:, k0:k0 + CHUNK_KT, :],
                                  h_hi[:, k0:k0 + CHUNK_KT, :], ALU.subtract).then_inc(h_lo_made, 1)
                if kp == 0:
                    make_lo(2)
                    for n in range(4, 8):
                        sum_ada(n)
                elif kp < NKP - 1:
                    sum_ada(4 * kp + 5)
                    sum_ada(4 * kp + 6)
                    if kp == NKP - 2:
                        make_lo(len(EARLY) * kp + 2)
                    sum_ada(4 * kp + 7)
                    if kp < NKP - 2:
                        make_lo(len(EARLY) * kp + 2)
                if kp == 1:
                    dve.wait_ge(nar_hi_made, 1)
                    dve.tensor_tensor(nar_lo, nar_raw, nar_hi, ALU.subtract).then_inc(nar_lo_made, 1)

            parts = ((0, 0, P), (1, P, 3 * P))

            def start_scores():
                dve.wait_ge(square_in, 16)
                dve.memset(score[:, P:2 * P], 0.0)
                dve.tensor_copy(score[:, 0:P], fill)
                link(dve.tensor_copy(score[:, 2 * P:3 * P], fill))

            def add_heads(lo, hi):
                for j in range(lo, hi):
                    wait_drained(dve, f"idx{j}")
                    if j > 0:
                        dve.wait_ge(relu_used, j)
                    for t, c0, c1 in parts:
                        ins = dve.scalar_tensor_tensor(out=score[:, c0:c1], in0=relu[j % 2][:, c0:c1],
                                                       scalar=iws_v[:, t, j:j + 1], in1=score[:, c0:c1],
                                                       op0=ALU.mult, op1=ALU.add)
                    ins.then_inc(relu_used, 1)

            def topk_rounds(n):
                for _ in range(n):
                    for t, c0, c1 in parts:
                        m1 = mark(dve.max(top8[:, 8 * t:8 * t + 8], score[:, c0:c1]))
                    dve.wait_ge(dve_step, m1)
                    for t, c0, c1 in parts:
                        m2 = mark(dve.match_replace(score[:, c0:c1], top8[:, 8 * t:8 * t + 8], score[:, c0:c1], TAKEN))
                    dve.wait_ge(dve_step, m2)

            def make_select():
                link(dve.tensor_scalar(select, score, TAKEN_BELOW, UNSELECTED, ALU.is_gt, ALU.mult))
                dve.tensor_tensor(select[:, 0:P], select[:, 0:P], fill, ALU.min)
                dve.tensor_tensor(select[:, 2 * P:3 * P], select[:, 2 * P:3 * P], fill, ALU.min).then_inc(select_made, 1)

            def cumulate():
                dve.wait_ge(pre_made, 1)
                resets = qk[0]
                link(dve.memset(resets, 1.0))
                dve.memset(resets.rearrange("p (n u) -> p n u", u=P)[:, :, 0:1], 0.0)
                link(dve.scalar_tensor_tensor(out=qk[1], in0=cum, scalar=0.0, in1=expo[0], op0=ALU.min,
                                              op1=ALU.subtract))
                dve.tensor_tensor_scan(cum, resets, qk[1], 0.0, ALU.mult, ALU.add).then_inc(cum_made, 1)
                dve.wait_ge(cum_made, 1)
                link(dve.memset(attn, 0.0))

            def level(i):
                m = P if i == 0 else LEVELS[i - 1]
                dve.wait_ge(decay_made, i + 1)
                if i >= 2:
                    wait_filled(dve, "cross" if i == 2 else f"L{LEVELS[i - 3]}_1")
                if i == 0:
                    wait_drained(dve, "T_bq_1")
                v = lambda a: a.rearrange("p (n two m) -> p n two m", two=2, m=m)
                dve.tensor_tensor(v(qk[i % 2])[:, :, 1, :], v(bqT)[:, :, 1, :], v(expo[i % 2])[:, :, 1, :], ALU.mult)
                dve.tensor_tensor(v(qk[i % 2])[:, :, 0, :], v(bkT)[:, :, 0, :], v(expo[i % 2])[:, :, 0, :], ALU.mult
                                  ).then_inc(level_made, 1)

            def take_level(name, t, lvl):
                wait_filled(dve, name)
                hv = lambda a: a.rearrange("p (h t) -> p h t", h=HB)
                if lvl == 0:
                    dve.copy_predicated(hv(attn[:, t, :]), lvl_mask[:, lvl, :].unsqueeze(1).to_broadcast([P, HB, P]),
                                        hv(side(name)[:, :])).then_inc(drained_dve, 1)
                else:
                    m = LEVELS[lvl - 1]
                    n = P // (2 * m)
                    dst = attn[:, t, :].rearrange("p (h n two m) -> p h n two m", h=HB, two=2, m=m)[:, :, :, 1, :]
                    msk = lvl_mask[:, lvl, :].rearrange("p (n two m) -> p n two m", two=2, m=m)[:, :, 1, :]
                    src = side(name)[:, 0:HB * P // 2].rearrange("p (h n m) -> p h n m", h=HB, m=m)
                    dve.copy_predicated(dst, msk.unsqueeze(1).to_broadcast([P, HB, n, m]), src).then_inc(drained_dve, 1)
                wait_drained(dve, name)

            def norm_b():
                dve.wait_ge(tables_in, 16 * 2)
                dve.wait_ge(grs_made, 1)
                wait_drained(dve, "gla_o3")
                for t in range(TT):
                    for hd in range(HB):
                        n = t * HB + hd
                        v = o_b[:, t, hd * DV:(hd + 1) * DV]
                        ins = dve.scalar_tensor_tensor(out=v, in0=v, scalar=grs[:, n:n + 1], in1=gla_gb[:, :],
                                                       op0=ALU.mult, op1=ALU.mult)
                ins.then_inc(o_b_made, 1)

            def logits(lo, hi):
                for h in range(lo, hi):
                    wait_filled(dve, f"qk{h}")
                    for t, c0, c1 in parts:
                        ins = dve.tensor_tensor_reduce(prob[:, h, c0:c1], side(f"qk{h}")[:, c0:c1], select[:, c0:c1], 1.0,
                                                       TAKEN, ALU.add, ALU.max, lmax[:, 2 * h + t:2 * h + t + 1])
                    ins.then_inc(drained_dve, 1)
                wait_drained(dve, f"qk{hi - 1}")
                dve.tensor_scalar(nmax[:, 2 * lo:2 * hi], lmax[:, 2 * lo:2 * hi], -1.0, None, ALU.mult
                                  ).then_inc(nmax_made, 1)

            def take_outputs(lo, hi):
                for h in range(lo, hi, 2):
                    wait_filled(dve, f"pv{h}")
                    for j in range(2):
                        for t in range(TT):
                            n = 2 * (h + j) + t
                            ins = dve.tensor_scalar(mix_a[:, t, (h + j) * DA:(h + j + 1) * DA],
                                                    side(f"pv{h}")[:, j * T + t * P:j * T + (t + 1) * P],
                                                    rinv[:, n:n + 1], None, ALU.mult)
                    ins.then_inc(drained_dve, 1)

            def mixT_lo(stem, hi_dst, lo_dst, before):
                for i in range(4):
                    dve.wait_ge(mixT_hi_made, before + i + 1)
                    dve.tensor_tensor(lo_dst[:, 2 * i:2 * i + 2, :].rearrange("p c t -> p (c t)"), side(f"{stem}{i}")[:, :],
                                      hi_dst[:, 2 * i:2 * i + 2, :].rearrange("p c t -> p (c t)"), ALU.subtract
                                      ).then_inc(drained_dve, 1)

            def sum_gate(n):
                j, hf = divmod(n, 2)
                dve.wait_ge(gate_in[n % 3], 16 * (n // 3 + 1))
                if hf == 0 and j >= 4:
                    wait_filled(dve, f"gate{j - 4}")
                if hf == 1:
                    dve.wait_ge(gate_used, n)
                sum_rows(gate_slot(n), gate_acc[2 * (j % 4):2 * (j % 4) + 2], hf, gate_used)

            def take_gate(j):
                wait_filled(dve, f"gate{j}")
                g = gate_b[:, j * ADA_COLS:(j + 1) * ADA_COLS]
                dve.tensor_tensor(g, side(f"gate{j}")[:, 0:ADA_COLS], g, ALU.add).then_inc(drained_dve, 1)

            def residual(blk):
                dve.wait_ge(chunk_used, E0 + HALF * (OUT_DONE[blk] + 1))
                dve.wait_ge(x_again, 16)
                wait_drained(dve, f"gate{2 * blk + 1}")
                cs = slice(blk * BLK, (blk + 1) * BLK)
                for t in range(TT):
                    dve.tensor_tensor(silu_b[0][:, t, :], bank[2 * ((NIN + blk) % 2) + t][:, :], gate_b[:, cs], ALU.mult
                                      ).then_inc(y_gated, 1)
                dve.wait_ge(y_gated, TT * (blk + 1))
                for t in range(TT):
                    dve.tensor_tensor(z[:, t, cs], z[:, t, cs], silu_b[0][:, t, :], ALU.add).then_inc(z_made, 1)
                dve.wait_ge(z_made, TT * (blk + 1))

            def last_residual(t):
                blk = NOUT - 1
                dve.wait_ge(last_filled, t + 1)
                wait_drained(dve, f"gate{2 * blk + 1}")
                cs = slice(blk * BLK, (blk + 1) * BLK)
                link(dve.tensor_tensor(silu_b[0][:, t, :], bank[2 * ((NIN + blk) % 2) + t][:, :], gate_b[:, cs], ALU.mult))
                dve.tensor_tensor(z_part(blk, t), z[:, t, cs], silu_b[0][:, t, :], ALU.add).then_inc(z_made, 1)
                dve.wait_ge(z_made, TT * blk + t + 1)
                dve.wait_ge(fin_in, 16)
                link(dve.tensor_tensor(z[:, t, cs], z_part(blk, t), fin_g[:, cs], ALU.mult))

            for s in range(STEPS):
                for i in range(HALF):
                    make_lo(E0 + HALF * s + i)
                if s == 27:
                    mixT_lo("mixB", h_hi[:, KT // 2:KT, :], h_lo[:, KT // 2:KT, :], 4)
                if s == 1:
                    start_scores()
                if s == 4:
                    cumulate()
                    add_heads(0, 2)
                if s == 5:
                    add_heads(2, 6)
                if s == 6:
                    add_heads(6, 10)
                if s == 7:
                    level(0)
                    add_heads(10, 14)
                if s == 8:
                    dve.wait_ge(masks_made, 1)
                    take_level("diag0", 0, 0)
                    take_level("diag1", 1, 0)
                    level(1)
                    add_heads(14, 16)
                    dve.wait_ge(relu_used, IH)
                if s == 9:
                    wait_filled(dve, "cross")
                    dve.tensor_copy(attn[:, 2, :], side("cross")[:, :]).then_inc(drained_dve, 1)
                    take_level("L64_0", 0, 1)
                    take_level("L64_1", 1, 1)
                    level(2)
                    topk_rounds(1)
                if s == 10:
                    take_level("L32_0", 0, 2)
                    take_level("L32_1", 1, 2)
                    level(3)
                    level(4)
                    topk_rounds(1)
                if s == 11:
                    for m in (16, 8):
                        for t in range(TT):
                            take_level(f"L{m}_{t}", t, 1 + LEVELS.index(m))
                    level(5)
                    topk_rounds(1)
                if s == 12:
                    take_level("L4_0", 0, 5)
                    take_level("L4_1", 1, 5)
                    level(6)
                    level(7)
                    topk_rounds(1)
                if s == 13:
                    for m in (2, 1):
                        for t in range(TT):
                            take_level(f"L{m}_{t}", t, 1 + LEVELS.index(m))
                    topk_rounds(1)
                if s in (14, 15, 16):
                    topk_rounds(1)
                if s == 16:
                    make_select()
                    dve.wait_ge(select_made, 1)
                    norm_b()
                if s == 17:
                    logits(0, 4)
                if s == 18:
                    logits(4, 8)
                if s == 20:
                    dve.wait_ge(prob_made, HA)
                    dve.reciprocal(rinv, rsum).then_inc(rinv_made, 1)
                    dve.wait_ge(rinv_made, 1)
                if s == 21:
                    take_outputs(0, 4)
                if s == 22:
                    take_outputs(4, 8)
                if s == 23:
                    dve.wait_ge(block_drained, B_AG + 2)
                    wait_drained(dve, "pv6")
                    for t in range(TT):
                        dve.tensor_tensor(mix_a[:, t, :], mix_a[:, t, :], silu_a[:, t, :], ALU.mult).then_inc(mix_a_made, 1)
                if s == 25:
                    mixT_lo("mixA", a_hi, a_lo, 0)
                if s in (25, 26):
                    j = s - 25
                    dve.wait_ge(block_drained, B_BG + 1 + j)
                    dve.wait_ge(o_b_made, 1)
                    for t in range(TT):
                        v = o_b[:, t, j * BLK:(j + 1) * BLK]
                        dve.tensor_tensor(v, v, silu_b[j][:, t, :], ALU.mult).then_inc(mix_b_made, 1)
                for blk in range(NOUT - 1):
                    if s == OUT_DONE[blk] + 1:
                        residual(blk)
                for j, ps in ((j, ps) for ps, j in GATE_STEPS.items() if ps + 1 == s):
                    take_gate(j)
                for n in GATE_SUMS.get(s, ()):
                    sum_gate(n)
            for t in range(TT):
                last_residual(t)
                dve.wait_ge(z_squared, TT * (NOUT - 1) + t + 1)
                dve.tensor_reduce(zsum[:, t:t + 1], zss[:, NOUT * t:NOUT * (t + 1)], AX_X, ALU.add).then_inc(zsum_made, 1)
                dve.wait_ge(z_weighted, TT * (NOUT - 1))
                dve.wait_ge(z_rstd, t + 1)
                dve.tensor_scalar(z[:, t, ACT_COLS:], z[:, t, ACT_COLS:], zrs[:, t:t + 1], None, ALU.mult
                                  ).then_inc(scaled_dve, 1)

        @block.tensor
        def _(pe):
            def three(out_, hi, lo, whi, wlo, first, last):
                pe.matmul(out_, hi, whi, start=first, stop=False, skip_group_check=True)
                pe.matmul(out_, hi, wlo, start=False, stop=False, skip_group_check=True)
                return pe.matmul(out_, lo, whi, start=False, stop=last, skip_group_check=True)

            def use_chunk(g, kp, banks, s_hi, s_lo):
                pe.wait_ge(lo_made, g + 1)
                for i in range(CHUNK_KT):
                    k = kp * CHUNK_KT + i
                    for t in range(TT):
                        ts = slice(t * P, (t + 1) * P)
                        ins = three(bank[banks + t][:, :], s_hi(k)[:, ts], s_lo(k)[:, ts],
                                    w_hi[:, g % SPLIT, i, :], w_lo[:, g % SPLIT, i, :], k == 0, k == KT - 1)
                ins.then_inc(chunk_used, 1)

            def fill_side(name):
                if ORDER[name] >= 4:
                    wait_drained(pe, USES[ORDER[name] - 4][0])
                return side(name)

            def turn(stem, st, idn=ident):
                for i in range(2):
                    b = fill_side(f"{stem}{i}")
                    for j in range(2):
                        for t in range(TT):
                            c0 = (2 * i + j) * P
                            ins = pe.transpose(b[:, (2 * j + t) * P:(2 * j + t + 1) * P], st[:, t, c0:c0 + P], idn)
                    ins.then_inc(side_filled, 1)

            pe.wait_ge(diag_made, TT)
            for i in range(8):
                if i >= 6:
                    pe.wait_ge(xT_drained, i - 5)
                for j in range(2):
                    for t in range(TT):
                        k = 2 * i + j
                        ins = pe.matmul(bank[i % 6][:, (2 * j + t) * P:(2 * j + t + 1) * P],
                                        x_nat[:, t, k * P:(k + 1) * P], rstd_diag[:, t, :], start=True, stop=True)
                ins.then_inc(xT_filled, 1)
            pe.wait_ge(square_in, 16)
            pe.wait_ge(rows_in, 48)
            pe.transpose(bank[ADA_BANK][:, 0:NROWS], rows[0:NROWS, :], ident[0:NROWS, 0:NROWS]).then_inc(cols_filled, 1)
            pe.wait_ge(cols_made, 1)
            pe.wait_ge(c_acted, 1)

            def modulation(kp):
                pb = bank[ADA_BANK]
                if kp > 0:
                    pe.wait_ge(mod_read, kp)
                n = 4 * kp + 3
                pe.wait_ge(ada_in[n % ADA_SLOTS], 16 * (n // ADA_SLOTS + 1))
                for ct in range(2):
                    for i in range(ADA_KT - SHIFT_PE, ADA_KT):
                        ins = pe.matmul(pb[:, 4 * kp + 2 + ct:4 * kp + 3 + ct],
                                        ada[n % ADA_SLOTS][:, i, ct * P:(ct + 1) * P],
                                        c_act[:, ADA_KT + i:ADA_KT + i + 1],
                                        start=(ct == 0 and i == ADA_KT - SHIFT_PE), stop=False, skip_group_check=True)
                ins.then_inc(shift_used, 1)
                pe.wait_ge(ones_made, 1)
                for r in range(2):
                    pe.wait_ge(acc_folded, 2 * kp + r + 1)
                    for ct in range(2):
                        o = 4 * kp + 2 * r + ct
                        ins = pe.matmul(pb[:, o:o + 1], acc[4 * (kp % 2) + 2 * r][:, ct * P:(ct + 1) * P],
                                        ones[:, 0:1], start=False, stop=True, skip_group_check=True)
                ins.then_inc(mod_filled, 1)

            modulation(0)
            pe.wait_ge(xT_drained, 8)
            for kp in range(NKP):
                pe.wait_ge(h_lo_made, kp + 1)
                for j in range(len(EARLY)):
                    if j == 2 and kp < NKP - 1:
                        modulation(kp + 1)
                    use_chunk(len(EARLY) * kp + j, kp, 2 * j, lambda k: h_hi[:, k, :], lambda k: h_lo[:, k, :])
                if kp == 1:
                    pe.wait_ge(nar_lo_made, 1)
                for k in [] if kp == 0 else range(2 * CHUNK_KT) if kp == 1 else range(kp * CHUNK_KT, (kp + 1) * CHUNK_KT):
                    ins = three(bank[NAR_BANK][0:NAR, 0:T], nar_hi[:, k, :], nar_lo[:, k, :], h_hi[:, k, :], h_lo[:, k, :],
                                k == 0, k == KT - 1)
            ins.then_inc(nar_done, 1)

            def index_heads(lo, hi):
                for j in range(lo, hi):
                    b = fill_side(f"idx{j}")
                    r = slice((j % 2) * ID, (j % 2 + 1) * ID)
                    pe.matmul(b[:, 0:P], iqT[r, j // 2, 0:P], ikT[r, 0:P], start=True, stop=True)
                    pe.matmul(b[:, P:3 * P], iqT[r, j // 2, P:T], ikT[r, :], start=True, stop=True
                              ).then_inc(side_filled, 1)

            bqv, bkv = (a.rearrange("p (h t) -> p h t", h=HB) for a in (bqT, bkT))
            qkv = [a.rearrange("p (h t) -> p h t", h=HB) for a in qk]

            def pair_products(name, left, right, n=P):
                b = fill_side(name)
                for hd in range(HB):
                    ins = pe.matmul(b[:, hd * n:(hd + 1) * n], left(hd), right(hd), start=True, stop=True)
                ins.then_inc(side_filled, 1)

            def level_products(i):
                pe.wait_ge(level_made, i + 1)
                for t in range(TT):
                    tile = lambda hd: qkv[i % 2][:, hd, t * P:(t + 1) * P]
                    targets = lambda hd: tile(hd).rearrange("p (n two m) -> p n two m", two=2, m=LEVELS[i - 1])[:, :, 1, :]
                    pair_products(f"L{LEVELS[i - 1]}_{t}", tile, targets, P // 2)

            def turn_mix(stem, src):
                for i in range(4):
                    b = fill_side(f"{stem}{i}")
                    for j in range(2):
                        for t in range(TT):
                            c0 = (2 * i + j) * P
                            ins = pe.transpose(b[:, (2 * j + t) * P:(2 * j + t + 1) * P], src[:, t, c0:c0 + P], ident)
                    ins.then_inc(side_filled, 1)

            for s in range(STEPS):
                blk, second = block_of(s)
                if second == 0:
                    if blk >= 2:
                        if blk - 2 < NIN:
                            pe.wait_ge(block_drained, blk - 1)
                        else:
                            pe.wait_ge(y_gated, TT * (blk - 2 - NIN + 1))
                    elif blk == 0:
                        pe.wait_ge(early_drained, 2)
                    else:
                        pe.wait_ge(early_drained, 7)
                if s == 26:
                    wait_drained(pe, "mixA3")
                if s == 28:
                    wait_drained(pe, "mixB3")
                if blk < NIN:
                    s_hi, s_lo = (lambda k: h_hi[:, k, :]), (lambda k: h_lo[:, k, :])
                else:
                    s_hi = lambda k: a_hi[:, k, :] if k < KT // 2 else h_hi[:, k, :]
                    s_lo = lambda k: a_lo[:, k, :] if k < KT // 2 else h_lo[:, k, :]
                if s < STEPS - 1:
                    for i in range(HALF):
                        use_chunk(E0 + s * HALF + i, second * HALF + i, 2 * (blk % 2), s_hi, s_lo)
                else:
                    for t in range(TT):
                        for i in range(HALF):
                            g = E0 + s * HALF + i
                            pe.wait_ge(lo_made, g + 1)
                            for j in range(CHUNK_KT):
                                k = (second * HALF + i) * CHUNK_KT + j
                                ins = three(bank[2 * (blk % 2) + t][:, :], s_hi(k)[:, t * P:(t + 1) * P],
                                            s_lo(k)[:, t * P:(t + 1) * P], w_hi[:, g % SPLIT, j, :], w_lo[:, g % SPLIT, j, :],
                                            k == 0, k == KT - 1)
                        ins.then_inc(last_filled, 1)

                if s == 0:
                    pe.wait_ge(early_drained, 7)
                    pe.wait_ge(mod_read, NKP)
                    turn("T_iq0_", stage[0])
                    b = fill_side("T_nar")
                    for r in range(2):
                        pe.matmul(b[r * ID:(r + 1) * ID, 0:T], ident[0:ID, 0:ID], narT[0:ID, :], start=True, stop=True)
                    for t in range(TT):
                        ins = pe.transpose(b[:, T + t * NB:T + (t + 1) * NB], narT[ID:NAR, t * P:(t + 1) * P],
                                           ident[ID:NAR, ID:NAR])
                    ins.then_inc(side_filled, 1)
                if s == 1:
                    turn("T_iq1_", stage[1])
                    turn("T_bk_", stage[2])
                if s == 2:
                    pe.wait_ge(tables_in, 16 * 2)
                    pe.wait_ge(bias_tables_in, 16 * 2)
                    for i in range(2):
                        b = fill_side(f"pre{i}")
                        for j in range(2):
                            hd = 2 * i + j
                            ins = pe.matmul(b[:, j * T:(j + 1) * T], w_alpha[ID:ID + RANK, hd * DK:(hd + 1) * DK],
                                            narT[ID:ID + RANK, :], start=True, stop=True)
                        ins.then_inc(side_filled, 1)
                    b = fill_side("band")
                    pe.matmul(b[0:HA, 0:T + P], relb[0:BUCKETS, :], onehot_sb[0:BUCKETS, :], start=True, stop=True
                              ).then_inc(side_filled, 1)
                if s == 3:
                    pe.wait_ge(block_drained, B_BQ + 1)
                    turn("T_bq_", stage[0])
                    wait_drained(pe, "T_iq1_1")
                    index_heads(0, 2)
                if s in (4, 5, 6):
                    index_heads(4 * s - 14, 4 * s - 10)
                if s == 7:
                    index_heads(14, 16)
                    for t in range(TT):
                        pair_products(f"diag{t}", lambda hd: bkv[:, hd, t * P:(t + 1) * P],
                                      lambda hd: bqv[:, hd, t * P:(t + 1) * P])
                if s == 8:
                    pe.wait_ge(level_made, 1)
                    pair_products("cross", lambda hd: qkv[0][:, hd, 0:P], lambda hd: qkv[0][:, hd, P:T])
                    level_products(1)
                if s == 9:
                    pe.wait_ge(block_drained, B_AQ + 1)
                    turn("T_aq0_", stage[0])
                    level_products(2)
                if s == 10:
                    level_products(3)
                    level_products(4)
                if s == 11:
                    pe.wait_ge(block_drained, B_AQ + 2)
                    turn("T_aq1_", stage[1])
                    level_products(5)
                if s == 12:
                    level_products(6)
                    level_products(7)
                if s == 13:
                    pe.wait_ge(block_drained, B_AK + 1)
                    turn("T_ak0_", stage[0])
                if s == 14:
                    wait_drained(pe, "L1_1")
                    for i in range(4):
                        t, pair = divmod(i, 2)
                        b = fill_side(f"gla_o{i}")
                        for j in range(2):
                            hd = 2 * pair + j
                            o, vs, hs = b[:, j * DV:(j + 1) * DV], slice(hd * DV, (hd + 1) * DV), slice(hd * P, (hd + 1) * P)
                            if t == 1:
                                pe.matmul(o, attn[:, 2, hs], bv[:, 0, vs], start=True, stop=False)
                            ins = pe.matmul(o, attn[:, t, hs], bv[:, t, vs], start=(t == 0), stop=True)
                        ins.then_inc(side_filled, 1)
                if s == 15:
                    pe.wait_ge(block_drained, B_AK + 2)
                    turn("T_ak1_", stage[1])
                if s in (16, 17):
                    wait_drained(pe, "T_ak1_1")
                    pe.wait_ge(hankel_in, 16)
                    for h in range(4 * (s - 16), 4 * (s - 15)):
                        b = fill_side(f"qk{h}")
                        for t, c0, c1 in ((0, 0, P), (1, P, 3 * P)):
                            pe.matmul(b[:, c0:c1], qT[:, h, t * P:(t + 1) * P], kT[:, h, 0:c1 - c0], start=True, stop=False)
                            ins = pe.matmul(b[:, c0:c1], flip, hankel[:, h, T - (c1 - c0):T], start=False, stop=True)
                        ins.then_inc(side_filled, 1)
                if s in (18, 19):
                    for h in range(4 * (s - 18), 4 * (s - 17)):
                        b = fill_side(f"pt{h}")
                        pe.wait_ge(prob_made, h + 1)
                        for i in range(3):
                            ins = pe.transpose(b[:, i * P:(i + 1) * P], prob[:, h, i * P:(i + 1) * P], ident)
                        ins.then_inc(side_filled, 1)
                if s in (20, 21):
                    pe.wait_ge(block_drained, B_AV + 2)
                    for h in range(4 * (s - 20), 4 * (s - 19), 2):
                        b = fill_side(f"pv{h}")
                        wait_drained(pe, f"pt{h + 1}")
                        for hd in (h, h + 1):
                            o, vs = (hd - h) * T, slice(hd * DA, (hd + 1) * DA)
                            pe.matmul(b[:, o:o + P], probT[:, hd, 0:P], v_a[:, 0, vs], start=True, stop=True)
                            pe.matmul(b[:, o + P:o + T], probT[:, hd, P:2 * P], v_a[:, 0, vs], start=True, stop=False)
                            ins = pe.matmul(b[:, o + P:o + T], probT[:, hd, 2 * P:3 * P], v_a[:, 1, vs], start=False,
                                            stop=True)
                        ins.then_inc(side_filled, 1)
                if s == 24:
                    pe.wait_ge(mix_a_made, TT)
                    turn_mix("mixA", mix_a)
                if s == 26:
                    pe.wait_ge(mix_b_made, 2 * TT)
                    turn_mix("mixB", o_b)
                if s in GATE_STEPS:
                    j = GATE_STEPS[s]
                    b = fill_side(f"gate{j}")
                    pe.wait_ge(gate_folded, j + 1)
                    pe.wait_ge(gate_bias_in, 16)
                    pe.matmul(b[:, 0:ADA_COLS], ones[:, :], gate_acc[2 * (j % 4)], start=True, stop=True
                              ).then_inc(side_filled, 1)


_INS = ["x", "c", "w_ada", "b_ada", "norm_g", "w_in", "w_alpha_up", "b_alpha", "gla_g", "w_out", "rel_bias", "final_g"]


def kernel(**inputs):
    import numpy as _np
    import concourse.bacc as _bacc
    from concourse import mybir as _mybir
    from concourse.bass_utils import run_bass_kernel_spmd as _run

    nc = _bacc.Bacc("TRN2", target_bir_lowering=False, num_devices=1)
    arrays, args = {}, []
    for name in _INS:
        a = _np.ascontiguousarray(inputs[name])
        if name not in ("rel_bias", "final_g"):
            a = a[0]
        arrays[f"in_{name}"] = a
        args.append(nc.dram_tensor(f"in_{name}", a.shape, _mybir.dt.from_np(a.dtype), kind="ExternalInput").ap())
    T, D = inputs["x"].shape[1:]
    for name, a in zip(("square", "onehot", "masks"), constants(T)):
        arrays[f"const_{name}"] = a
        args.append(nc.dram_tensor(f"const_{name}", a.shape, _mybir.dt.from_np(a.dtype), kind="ExternalInput").ap())
    args.append(nc.dram_tensor("band_scratch", (inputs["rel_bias"].shape[1], T + P), _mybir.dt.float32,
                               kind="Internal").ap())
    args.append(nc.dram_tensor("out", (T, D), _mybir.dt.float32, kind="ExternalOutput").ap())
    build(nc, *args)
    r = _run(nc, [arrays], core_ids=[0])
    return r.results[0]["out"].reshape(1, T, D)
```

```python
from contextlib import ExitStack

import numpy as np
import concourse.bass as bass
from concourse import mybir

ALU = mybir.AluOpType
ACT = mybir.ActivationFunctionType
AX_X = mybir.AxisListType.X
F32 = mybir.dt.float32
F32R = mybir.dt.float32r
U8 = mybir.dt.uint8

P = 128
EPS = 1e-6
TOPK_MAX = 256
BUCKETS, MAX_DISTANCE = 32, 128
GATE_TEMP = 16.0
BLK = 512
CHUNK_KT = 2
RAW, SPLIT = 8, 4
ADA_SLOTS, ADA_KT, ADA_COLS = 5, 8, 256
SHIFT_PE = 6
SIDE_BANK = 4
CAUSAL_FILL = -3.0e38
TAKEN = -3.4e38
TAKEN_BELOW = -3.35e38
UNSELECTED = -1.0e30


def t5_bucket(dist):
    exact = BUCKETS // 2
    d = np.maximum(dist, 0)
    large = exact + (np.log(np.maximum(d, 1).astype(np.float32) / np.float32(exact))
                     / np.log(MAX_DISTANCE / exact) * (BUCKETS - exact)).astype(np.int32)
    return np.where(d < exact, d, np.minimum(large, BUCKETS - 1))


def constants(T):
    i = np.arange(P)
    ident = np.eye(P, dtype=np.float32)
    fill = np.where(i[None, :] > i[:, None], CAUSAL_FILL, 0.0).astype(np.float32)
    square = np.concatenate([ident, ident[::-1], fill], axis=1)
    dist = T - 1 - np.arange(T + P)
    onehot = (t5_bucket(dist)[None, :] == np.arange(BUCKETS)[:, None]).astype(np.float32)
    s, t = i[:, None], i[None, :]
    masks = [s == t] + [(s // (2 * m) == t // (2 * m)) & (s % (2 * m) < m) & (t % (2 * m) >= m)
                        for m in LEVELS]
    return square, onehot, np.stack(masks, 1).astype(np.float32)


LEVELS = (64, 32, 16, 8, 4, 2, 1)


def build(nc, x, c, w_ada, b_ada, norm_g, w_in, w_alpha_up, b_alpha, gla_g, w_out, rel_bias,
          final_g, square, onehot, masks, band_scratch, out):
    T, D = x.shape
    KT = D // P
    NKP = KT // CHUNK_KT
    TT = T // P
    HA, DA = rel_bias.shape[1], P
    A_W = HA * DA
    RANK, B_KW = w_alpha_up.shape
    HB, DK = B_KW // P, P
    DV = gla_g.shape[0]
    B_W = HB * DV
    IH, ID = 16, 64
    TOPK = min(TOPK_MAX, T // 4)
    assert (T, D, DK * HB, TT) == (256, 2048, 512, 2) and A_W == B_W == 1024
    AQ, AK, AV, AG = (n * A_W for n in range(4))
    IQ = 4 * A_W
    IK = IQ + IH * ID
    BQ = IK + ID + IH
    BK = BQ + B_KW
    BV = BK + B_KW
    BG = BV + B_W
    BA = BG + B_W
    NAR = ID + RANK + IH
    NARROW = ((slice(0, ID), slice(0, ID)), (slice(ID, ID + RANK), slice(ID + IH, NAR)),
              (slice(ID + RANK, NAR), slice(ID, ID + IH)))
    NB = RANK + IH
    EARLY = (IQ, BQ, IQ + BLK, BK)
    E_IQ0, E_BQ, E_IQ1, E_BK = range(len(EARLY))
    EARLY_BANK = {E_IQ0: 0, E_IQ1: 2, E_BK: 4}
    BLOCKS = (BV, BV + BLK, AQ, AQ + BLK, AK, AK + BLK, AV, AV + BLK, AG, AG + BLK, BG, BG + BLK)
    B_BV, B_AQ, B_AK, B_AV, B_AG, B_BG = 0, 2, 4, 6, 8, 10
    NIN, NOUT = len(BLOCKS), D // BLK
    E0 = len(EARLY) * NKP

    HALF = NKP // 2
    STEPS = 2 * (NIN + NOUT)

    def names(stem, n):
        return [f"{stem}{i}" for i in range(n)]

    PLAN = {
        0: [(n, "A") for n in names("T_iq0_", 2) + ["T_nar"]],
        1: [(n, "A") for n in names("T_iq1_", 2) + names("T_bq_", 2)],
        2: [(n, "A") for n in names("T_bk_", 2) + names("pre", 2)],
        3: [(n, "A") for n in ["band", "idx0", "idx1", "idx2"]],
        4: [(f"idx{j}", "A") for j in range(3, 7)],
        5: [(f"idx{j}", "A") for j in range(7, 11)],
        6: [(f"idx{j}", "A") for j in range(11, 15)],
        7: [("idx15", "A"), ("T_aq0_0", "A"), ("T_aq0_1", "A"), ("cross", "V")],
        8: [("L64", "V"), ("L32", "V"), ("diag0", "V"), ("diag1", "V")],
        9: [("T_aq1_0", "A"), ("T_aq1_1", "A"), ("L16", "V"), ("L8", "V")],
        10: [("L4", "V"), ("L2", "V")],
        11: [("T_ak0_0", "A"), ("T_ak0_1", "A"), ("L1", "V")],
        12: [(n, "A") for n in names("gla_o", 4)],
        13: [("T_ak1_0", "A"), ("T_ak1_1", "A")],
        14: [(f"qk{h}", "V") for h in range(4)],
        15: [(f"qk{h}", "V") for h in range(4, 8)],
        16: [(f"pt{h}", "A") for h in range(4)],
        17: [(f"pt{h}", "A") for h in range(4, 8)],
        18: [("pv0", "V"), ("pv2", "V")],
        19: [("pv4", "V"), ("pv6", "V")],
        22: [(f"mixA{i}", "V") for i in range(4)],
        24: [(f"mixB{i}", "V") for i in range(4)],
    }
    HEADS = {3: (0, 3), 4: (3, 7), 5: (7, 11), 6: (11, 15), 7: (15, 16)}
    ROUNDS = {9: 1, 10: 1, 11: 2, 12: 1, 13: 1, 14: 2}
    assert 8 * sum(ROUNDS.values()) == TOPK
    LEVEL_FACTORS = {6: (0,), 7: (1,), 8: (2,), 9: (3, 4), 10: (5, 6), 11: (7,)}
    LEVEL_DECAYS = {6: (0, 1), 7: (2,), 8: (3,), 9: (4,), 10: (5, 6), 11: (7,)}
    GATE_SUMS = {17: [0], 18: [1, 2], 19: [3], 20: [4], 21: [5], 22: [6], 23: [7], 24: [8], 25: [9], 26: [10, 11],
                 27: [12], 28: [13], 29: [14, 15]}
    sum_step = {n: s for s, ns in GATE_SUMS.items() for n in ns}
    GATE_LOADS = {}
    for n, s in sum_step.items():
        GATE_LOADS.setdefault(16 if n < 3 else max(s - 1, sum_step[n - 3] + 1), []).append(n)
    GATE_STEPS = {19: 0, 20: 1, 23: 2, 25: 3, 26: 4, 27: 5, 29: 6, 30: 7}
    for s, j in GATE_STEPS.items():
        PLAN.setdefault(s, []).append((f"gate{j}", "V"))
    USES = [u for s in sorted(PLAN) for u in PLAN[s]]
    ORDER = {name: i for i, (name, _) in enumerate(USES)}
    DRAINER = dict(USES)

    def drained_count(name):
        return sum(1 for n, d in USES[:ORDER[name] + 1] if d == DRAINER[name])

    with ExitStack() as ctx:
        def sb(name, shape, dt=F32):
            return ctx.enter_context(nc.sbuf_tensor(name, shape, dt))

        def sem(name):
            return ctx.enter_context(nc.semaphore(name))

        raw = sb("raw", [P, RAW, CHUNK_KT, BLK])
        w_hi = sb("w_hi", [P, SPLIT, CHUNK_KT, BLK], F32R)
        w_lo = sb("w_lo", [P, SPLIT, CHUNK_KT, BLK], F32R)
        h_hi = sb("h_hi", [P, KT, T], F32R)
        h_lo = sb("h_lo", [P, KT, T], F32R)
        a_hi = sb("a_hi", [P, KT // 2, T], F32R)
        a_lo = sb("a_lo", [P, KT // 2, T], F32R)
        nar_hi = a_hi[:, :, :].rearrange("p a t -> p (a t)")[:, 0:KT * NAR].rearrange("p (k n) -> p k n", k=KT)
        nar_lo = a_lo[:, :, :].rearrange("p a t -> p (a t)")[:, 0:KT * NAR].rearrange("p (k n) -> p k n", k=KT)
        gate_b = sb("gate_b", [P, D])
        hankel = sb("hankel", [P, HA, T])
        sq = sb("sq", [P, 3 * P])
        ident, flip, fill = sq[:, 0:P], sq[:, P:2 * P], sq[:, 2 * P:3 * P]
        lvl_mask = sb("lvl_mask", [P, 1 + len(LEVELS), P], U8)
        NROWS = 3 * KT + HB
        small = sb("small", [P, 344])
        at = [0]

        def tiny(n):
            at[0] += n
            assert at[0] <= 344
            return small[:, at[0] - n:at[0]]

        c_raw, c_act = tiny(KT), tiny(KT)
        cols = tiny(NROWS)
        mod = tiny(4)
        half = tiny(1)
        stats = tiny(8)
        iws = tiny(TT * IH)
        iws_v = iws.rearrange("p (t j) -> p t j", t=TT)
        top8 = tiny(TT * 8)
        lmax, nmax, rsum, rinv = tiny(16), tiny(16), tiny(16), tiny(16)
        gss, gms, grs = tiny(8), tiny(8), tiny(8)
        zss, zsum, zrs = tiny(8), tiny(2), tiny(2)
        gla_gb = sb("gla_gb", [P, DV])

        KW = 256
        arena = sb("arena", [P, 72 * KW])

        def place(kib, words):
            o = int(kib * KW)
            return arena[:, o:o + words]

        ada = [place(8 * i, ADA_KT * ADA_COLS).rearrange("p (k n) -> p k n", k=ADA_KT) for i in range(ADA_SLOTS)]
        xT = place(40, KT * T).rearrange("p (k t) -> p k t", k=KT)
        acc = [place(56 + i, ADA_COLS) for i in range(8)]
        rstd_diag = acc[4].rearrange("p (t n) -> p t n", t=TT)
        nar_raw = place(64, KT * NAR).rearrange("p (k n) -> p k n", k=KT)
        x_nat = raw[:, 4:8, :, :].rearrange("p a k n -> p (a k n)").rearrange("p (t d) -> p t d", t=TT)
        x_junk = place(40, D)
        rows = place(70, P)
        onehot_sb = place(68.25, T + P)
        relb = place(69.75, HA)
        stage = [place(4 * i, TT * BLK).rearrange("p (t n) -> p t n", t=TT) for i in range(3)]
        masks_wide = place(36, (1 + len(LEVELS)) * P)
        relu = [place(8 + 1.5 * i, 3 * P) for i in range(2)]
        iqT = place(12, 8 * T).rearrange("p (c t) -> p c t", c=8)
        bkT, bqT = place(20, HB * T), place(24, HB * T)
        cum = place(28, HB * T)
        expo = [place(32, HB * T), place(36, HB * T)]
        qk = [place(40, HB * T), place(44, HB * T)]
        attn = place(48, 3 * BLK).rearrange("p (b n) -> p b n", b=3)
        bv = place(54, TT * B_W).rearrange("p (t n) -> p t n", t=TT)
        score = place(62, 3 * P)
        select = place(63.5, 3 * P)
        narT = place(66.25, T)
        ikT = place(67.25, T)
        band_sb = place(70, T + P)
        qT = place(12, HA * T).rearrange("p (h t) -> p h t", h=HA)
        kT = place(20, HA * T).rearrange("p (h t) -> p h t", h=HA)
        o_b = place(28, TT * B_W).rearrange("p (t n) -> p t n", t=TT)
        prob = place(36, HA * 3 * P).rearrange("p (h n) -> p h n", h=HA)
        v_a = place(54, TT * A_W).rearrange("p (t n) -> p t n", t=TT)
        probT = place(0, HA * 3 * P).rearrange("p (h n) -> p h n", h=HA)
        silu_a = place(12, TT * A_W).rearrange("p (t n) -> p t n", t=TT)
        mix_a = place(20, TT * A_W).rearrange("p (t n) -> p t n", t=TT)
        silu_b = [place(4 * i, TT * BLK).rearrange("p (t n) -> p t n", t=TT) for i in range(2)]
        slot = lambda a: a.rearrange("p (k n) -> p k n", k=ADA_KT)
        bq_sum, bq_part = (hankel[:, o:o + TT * BLK // T, :].rearrange("p h t -> p (h t)").rearrange("p (t n) -> p t n", t=TT)
                           for o in (0, HA // 2))
        hankel_slot = slot(hankel[:, :, :].rearrange("p h t -> p (h t)"))
        gate_first = [slot(place(12, ADA_KT * ADA_COLS)), slot(place(20, ADA_KT * ADA_COLS))]
        gate_late = [slot(place(36, ADA_KT * ADA_COLS)), slot(place(44, ADA_KT * ADA_COLS))]

        def gate_slot(n):
            return hankel_slot if n % 3 == 2 else (gate_first if n < 3 else gate_late)[n % 3]
        gate_acc = [place(62 + i, ADA_COLS) for i in range(8)]
        junk = place(8, D)[:, 0:BLK]
        z = place(12, TT * D).rearrange("p (t d) -> p t d", t=TT)
        fin_g = place(54, D)
        ACT_COLS = 3 * D // 8

        def z_part(blk, t):
            return silu_b[1][:, t, :] if blk == NOUT - 1 else z[:, t, blk * BLK:(blk + 1) * BLK]
        w_alpha = sb("w_alpha", [ID + RANK, B_KW])
        ones = sb("ones", [P, P])

        bank = [ctx.enter_context(nc.psum_tensor(f"bank{i}", [P, BLK], F32)) for i in range(8)]
        BQ_BANK, ADA_BANK = 6, 7
        nar_out = bank[ADA_BANK][0:NAR, BLK - T:BLK]

        def side(name):
            return bank[SIDE_BANK + ORDER[name] % 4]

        x_in = [sem(f"x_in{t}") for t in range(TT)]
        c_in, rows_in, square_in, tables_in, nar_in = (
            sem(n) for n in ("c_in", "rows_in", "square_in", "tables_in", "nar_in"))
        raw_in = [sem(f"raw_in{i}") for i in range(RAW)]
        ada_in = [sem(f"ada_in{i}") for i in range(ADA_SLOTS)]
        gate_in = [sem(f"gate_in{i}") for i in range(3)]
        bias_tables_in = sem("bias_tables_in")
        band_out, hankel_in, x_again, fin_in, gate_bias_in = (
            sem(n) for n in ("band_out", "hankel_in", "x_again", "fin_in", "gate_bias_in"))
        out_done = sem("out_done")
        hi_made, lo_made, chunk_used = sem("hi_made"), sem("lo_made"), sem("chunk_used")
        nar_hi_made, nar_lo_made, nar_done = sem("nar_hi_made"), sem("nar_lo_made"), sem("nar_done")
        early_drained, block_drained = sem("early_drained"), sem("block_drained")
        bq_filled, bq_copied, bq_added = sem("bq_filled"), sem("bq_copied"), sem("bq_added")
        x_squared, x_rstd, diag_made, xT_filled, xT_drained = (
            sem(n) for n in ("x_squared", "x_rstd", "diag_made", "xT_filled", "xT_drained"))
        c_acted, cols_filled, cols_made = sem("c_acted"), sem("cols_filled"), sem("cols_made")
        ada_summed, shift_used, acc_folded = sem("ada_summed"), sem("shift_used"), sem("acc_folded")
        mod_filled, mod_read, mod_made = sem("mod_filled"), sem("mod_read"), sem("mod_made")
        h_made, h_hi_made, h_lo_made = sem("h_made"), sem("h_hi_made"), sem("h_lo_made")
        side_filled, drained_act, drained_dve = sem("side_filled"), sem("drained_act"), sem("drained_dve")
        pre_made, cum_made = sem("pre_made"), sem("cum_made")
        ones_made, masks_in, masks_made = sem("ones_made"), sem("masks_in"), sem("masks_made")
        expo_made, decay_made, level_made = sem("expo_made"), sem("decay_made"), sem("level_made")
        relu_used, select_made = sem("relu_used"), sem("select_made")
        gss_made, grs_made, o_b_made = sem("gss_made"), sem("grs_made"), sem("o_b_made")
        nmax_made, prob_made, rinv_made = sem("nmax_made"), sem("prob_made"), sem("rinv_made")
        mix_a_made, mix_b_made = sem("mix_a_made"), sem("mix_b_made")
        mixT_hi_made = sem("mixT_hi_made")
        gate_used, gate_folded = sem("gate_used"), sem("gate_folded")
        y_gated, last_filled = sem("y_gated"), sem("last_filled")
        z_made, z_squared, z_weighted, zsum_made, z_rstd, scaled_act, scaled_dve = (
            sem(n) for n in ("z_made", "z_squared", "z_weighted", "zsum_made", "z_rstd", "scaled_act", "scaled_dve"))
        act_step, dve_step, pool_step = sem("act_step"), sem("dve_step"), sem("pool_step")

        def wait_drained(eng, name):
            eng.wait_ge(drained_act if DRAINER[name] == "A" else drained_dve, drained_count(name))

        def wait_filled(eng, name):
            eng.wait_ge(side_filled, ORDER[name] + 1)

        def block_of(s):
            return {2 * NIN + 1: (NIN + 1, 0), 2 * NIN + 2: (NIN, 1)}.get(s, divmod(s, 2))

        OUT_DONE = [2 * NIN + 2, 2 * NIN + 3, 2 * NIN + 5, 2 * NIN + 7]

        def chunk_source(g):
            if g < E0:
                kp, c0 = g // len(EARLY), EARLY[g % len(EARLY)]
            else:
                step, i = divmod(g - E0, HALF)
                blk, second = block_of(step)
                kp = second * HALF + i
                c0 = BLOCKS[blk] if blk < NIN else (blk - NIN) * BLK
            w = w_in if g < E0 + NIN * NKP else w_out
            r0 = kp * CHUNK_KT * P
            return w[r0:r0 + CHUNK_KT * P, c0:c0 + BLK].rearrange("(k p) n -> p k n", p=P)

        def ada_source(col0, half_):
            v = w_ada.rearrange("(p k) n -> p k n", k=KT)
            return v[:, half_ * ADA_KT:(half_ + 1) * ADA_KT, col0:col0 + ADA_COLS]

        block = ctx.enter_context(nc.Block())

        @block.sync
        def _(sp):
            sp.dma_start(c_raw, c.rearrange("(p k) -> p k", k=KT)).then_inc(c_in, 16)

            def load_raw(g):
                if g >= RAW:
                    sp.wait_ge(lo_made, g - RAW + 1)
                elif g >= 4:
                    sp.wait_ge(xT_filled, 8)
                sp.dma_start(raw[:, g % RAW, :, :], chunk_source(g)).then_inc(raw_in[g % RAW], 16)

            def load_ada(n):
                kp, r = divmod(n, 4)
                if n >= ADA_SLOTS:
                    sp.wait_ge(ada_summed, n - ADA_SLOTS + 1)
                    pk, pr = divmod(n - ADA_SLOTS, 4)
                    if pr == 0:
                        sp.wait_ge(shift_used, pk + 1)
                col0 = (0 if r < 2 else D) + kp * ADA_COLS
                sp.dma_start(ada[n % ADA_SLOTS], ada_source(col0, r % 2)).then_inc(ada_in[n % ADA_SLOTS], 16)

            load_ada(0)
            for t in range(TT):
                sp.dma_start(x_nat[:, t, :], x[t * P:(t + 1) * P, :]).then_inc(x_in[t], 16)
            sp.dma_start(sq[:, :], square).then_inc(square_in, 16)
            for r in range(1, 4):
                load_ada(r)
            sp.dma_start(rows[0:KT, :], norm_g.rearrange("(k p) -> k p", p=P)).then_inc(rows_in, 16)
            sp.dma_start(rows[KT:3 * KT, :], b_ada[0:2 * D].rearrange("(k p) -> k p", p=P)).then_inc(rows_in, 16)
            sp.dma_start(rows[3 * KT:NROWS, :], b_alpha.rearrange("(k p) -> k p", p=P)).then_inc(rows_in, 16)
            for j in range(len(EARLY)):
                load_raw(j)
            for kp in range(NKP):
                if kp > 0:
                    for j in range(len(EARLY)):
                        load_ada(4 * kp + j)
                        load_raw(len(EARLY) * kp + j)
                if kp == 1:
                    for o, c0, n in ((0, IK, ID + IH), (ID + IH, BA, RANK)):
                        sp.dma_start(nar_raw[:, :, o:o + n],
                                     w_in[:, c0:c0 + n].rearrange("(k p) n -> p k n", p=P)).then_inc(nar_in, 16)
                    sp.dma_start(w_alpha[ID:ID + RANK, :], w_alpha_up).then_inc(tables_in, 16)
                    sp.dma_start(gla_gb[:, :], gla_g.partition_broadcast(P)).then_inc(tables_in, 16)

            for s in range(STEPS):
                for i in range(HALF):
                    load_raw(E0 + HALF * s + i)
            for t in range(TT):
                for scaled, c0, c1 in ((scaled_dve, ACT_COLS, D), (scaled_act, 0, ACT_COLS)):
                    sp.wait_ge(scaled, t + 1)
                    sp.dma_start(out[t * P:(t + 1) * P, c0:c1], z[:, t, c0:c1]).then_inc(out_done, 16)
            sp.wait_ge(out_done, 16 * 2 * TT)

        @block.gpsimd
        def _(pool):
            pool.memset(ones[:, :], 1.0).then_inc(ones_made, 1)
            pool.memset(half, -0.5).then_inc(pool_step, 1)
            pool.wait_ge(pool_step, 1)
            steps = [1]

            def link(ins):
                steps[0] += 1
                ins.then_inc(pool_step, 1)
                pool.wait_ge(pool_step, steps[0])

            def rsqrt_mean(out_, sums, mean, n, done):
                link(pool.tensor_scalar(mean, sums, 1.0 / n, EPS, ALU.mult, ALU.add))
                w = sums.shape[1]
                pool.tensor_tensor(out_, mean, half.to_broadcast([P, w]), ALU.pow).then_inc(done, 1)

            for t in range(TT):
                pool.wait_ge(x_squared, t + 1)
                rsqrt_mean(stats[:, 4 + t:5 + t], stats[:, t:t + 1], stats[:, 2 + t:3 + t], D, x_rstd)

            def fold_ada(kp, r):
                pool.wait_ge(ada_summed, 4 * kp + 2 * r + 2)
                even, odd = acc[4 * (kp % 2) + 2 * r:4 * (kp % 2) + 2 * r + 2]
                pool.tensor_tensor(even, even, odd, ALU.add).then_inc(acc_folded, 1)

            for r in range(2):
                fold_ada(0, r)
            for kp in range(NKP):
                for t in range(TT):
                    if t == 1:
                        g = len(EARLY) * kp + E_BK
                        pool.wait_ge(hi_made, g + 1)
                        pool.wait_ge(lo_made, g)
                        pool.tensor_tensor(w_lo[:, g % SPLIT, :, :], raw[:, g % RAW, :, :], w_hi[:, g % SPLIT, :, :],
                                           ALU.subtract).then_inc(lo_made, 1)
                        if kp < NKP - 1:
                            for r in range(2):
                                fold_ada(kp + 1, r)
                    if kp > 0:
                        pool.wait_ge(bq_copied, TT * kp + t + 1)
                        if kp > 1:
                            pool.wait_ge(bq_added, TT * (kp - 2) + t + 1)
                        pool.tensor_tensor(bq_sum[:, t, :], bq_part[:, t, :], bq_sum[:, t, :], ALU.add
                                           ).then_inc(bq_added, 1)

            pool.wait_ge(masks_in, 16)
            pool.tensor_copy(lvl_mask[:, :, :].rearrange("p l t -> p (l t)"), masks_wide).then_inc(masks_made, 1)
            pool.wait_ge(masks_made, 1)

            pool.wait_ge(cum_made, 1)
            cv = cum.rearrange("p (h t u) -> p h t u", h=HB, t=TT)
            ev = expo[0].rearrange("p (h t u) -> p h t u", h=HB, t=TT)
            pool.tensor_copy(ev[:, :, 1, :], cv[:, :, 1, :])
            pool.tensor_tensor(ev[:, :, 0, :], cv[:, :, 0, P - 1:P].to_broadcast([P, HB, P]), cv[:, :, 0, :],
                               ALU.subtract).then_inc(expo_made, 1)
            for i, m in enumerate(LEVELS):
                if i >= 1:
                    pool.wait_ge(level_made, i)
                n = HB * T // (2 * m)
                lv = cum.rearrange("p (n two m) -> p n two m", two=2, m=m)
                le = expo[(i + 1) % 2].rearrange("p (n two m) -> p n two m", two=2, m=m)
                last = lv[:, :, 0, m - 1:m].to_broadcast([P, n, m])
                pool.tensor_tensor(le[:, :, 1, :], lv[:, :, 1, :], last, ALU.subtract)
                pool.tensor_tensor(le[:, :, 0, :], last, lv[:, :, 0, :], ALU.subtract).then_inc(expo_made, 1)

            pool.wait_ge(gss_made, TT * HB)
            rsqrt_mean(grs, gss, gms, DV, grs_made)

            for j in range(D // ADA_COLS):
                pool.wait_ge(gate_used, 2 * j + 2)
                even, odd = gate_acc[2 * (j % 4):2 * (j % 4) + 2]
                pool.tensor_tensor(even, even, odd, ALU.add).then_inc(gate_folded, 1)

            pool.wait_ge(fin_in, 16)
            for blk in range(NOUT - 1):
                pool.wait_ge(z_squared, TT * (blk + 1))
                cs = slice(blk * BLK, (blk + 1) * BLK)
                for t in range(TT):
                    pool.tensor_tensor(z[:, t, cs], z[:, t, cs], fin_g[:, cs], ALU.mult).then_inc(z_weighted, 1)
            for t in range(TT):
                pool.wait_ge(zsum_made, t + 1)
                rsqrt_mean(zrs[:, t:t + 1], zsum[:, t:t + 1], stats[:, 6 + t:7 + t], D, z_rstd)

        @block.scalar
        def _(act):
            steps = [0]

            def link(ins):
                steps[0] += 1
                ins.then_inc(act_step, 1)
                act.wait_ge(act_step, steps[0])

            def make_hi(g):
                act.wait_ge(raw_in[g % RAW], 16 * (g // RAW + 1))
                if g >= SPLIT:
                    act.wait_ge(chunk_used, g - SPLIT + 1)
                act.activation(w_hi[:, g % SPLIT, :, :], raw[:, g % RAW, :, :], ACT.Copy).then_inc(hi_made, 1)

            def drain(name, *pairs, func=ACT.Copy, **kw):
                wait_filled(act, name)
                for d, s in pairs:
                    ins = act.activation(d, s, func, **kw)
                ins.then_inc(drained_act, 1)

            def drain_turned(stem, dst, c0, scale=1.0):
                for i in range(2):
                    name = f"{stem}{i}"
                    drain(name, (dst[:, c0 + 2 * i:c0 + 2 * i + 2, :].rearrange("p c t -> p (c t)"), side(name)[:, :]),
                          scale=scale)

            def drain_block(blk, dst, func=ACT.Copy):
                act.wait_ge(chunk_used, E0 + (blk + 1) * NKP)
                for t in range(TT):
                    ins = act.activation(dst(t), bank[2 * (blk % 2) + t][:, :], func)
                ins.then_inc(block_drained, 1)

            act.wait_ge(c_in, 16)
            act.activation(c_act, c_raw, ACT.Silu).then_inc(c_acted, 1)
            for t in range(TT):
                act.wait_ge(x_in[t], 16)
                act.activation(x_junk, x_nat[:, t, :], ACT.Square, accum_out=stats[:, t:t + 1]).then_inc(x_squared, 1)
                act.wait_ge(x_squared, t + 1)
            for i in range(8):
                act.wait_ge(xT_filled, i + 1)
                act.activation(xT[:, 2 * i:2 * i + 2, :].rearrange("p k t -> p (k t)"), bank[i % 6][:, :], ACT.Copy
                               ).then_inc(xT_drained, 1)
            act.wait_ge(xT_drained, 8)

            def modulate(kp):
                k0 = kp * CHUNK_KT
                act.wait_ge(mod_made, kp + 1)
                for i in range(CHUNK_KT):
                    act.activation(xT[:, k0 + i, :], xT[:, k0 + i, :], ACT.Identity, scale=mod[:, i:i + 1],
                                   bias=mod[:, 2 + i:3 + i]).then_inc(h_made, 1)
                act.wait_ge(h_made, CHUNK_KT * (kp + 1))
                act.activation(h_hi[:, k0:k0 + CHUNK_KT, :], xT[:, k0:k0 + CHUNK_KT, :], ACT.Copy).then_inc(h_hi_made, 1)

            make_hi(0)
            modulate(0)
            for kp in range(NKP):
                for j in range(1, len(EARLY)):
                    make_hi(len(EARLY) * kp + j)
                if kp == 2:
                    act.wait_ge(nar_in, 32)
                    for cs, src in NARROW:
                        ins = act.activation(nar_hi[:, :, cs], nar_raw[:, :, src], ACT.Copy)
                    ins.then_inc(nar_hi_made, 1)
                for t in range(TT):
                    if t == 0:
                        act.wait_ge(bq_filled, kp + 1)
                    else:
                        act.wait_ge(chunk_used, len(EARLY) * kp + E_IQ1 + 1)
                    if kp > 1:
                        act.wait_ge(bq_added, TT * (kp - 2) + t + 1)
                    act.activation((bq_part if kp > 0 else bq_sum)[:, t, :], bank[BQ_BANK][:, :], ACT.Copy
                                   ).then_inc(bq_copied, 1)
                    if t == 0:
                        make_hi(len(EARLY) * (kp + 1))
                        if kp < NKP - 1:
                            modulate(kp + 1)

            act.wait_ge(chunk_used, E0 - 3)
            for t in range(TT):
                act.activation(stage[0][:, t, :], bank[t][:, :], ACT.Copy).then_inc(early_drained, 1)
            make_hi(E0 + 1)
            act.wait_ge(chunk_used, E0)
            act.wait_ge(nar_done, 1)
            for t in range(TT):
                act.activation(stage[2][:, t, :], bank[4 + t][:, :], ACT.Copy).then_inc(early_drained, 1)
            act.activation(narT[0:NAR, :], nar_out, ACT.Copy).then_inc(early_drained, 1)
            for t in range(TT):
                act.activation(stage[1][:, t, :], bank[2 + t][:, :], ACT.Copy).then_inc(early_drained, 1)
            for i in range(2, HALF):
                make_hi(E0 + i)

            def relus(lo, hi):
                for j in range(lo, hi):
                    if j >= 2:
                        act.wait_ge(relu_used, j - 1)
                    drain(f"idx{j}", (relu[j % 2], side(f"idx{j}")[:, 0:3 * P]), func=ACT.Relu)

            def decay(i):
                act.wait_ge(expo_made, i + 1)
                act.activation(expo[i % 2], expo[i % 2], ACT.Exp, scale=1.0 / GATE_TEMP).then_inc(decay_made, 1)

            def probs(lo, hi):
                act.wait_ge(nmax_made, lo // 4 + 1)
                for h in range(lo, hi):
                    for t, (c0, c1) in enumerate(((0, P), (P, 3 * P))):
                        ins = act.activation(prob[:, h, c0:c1], prob[:, h, c0:c1], ACT.Exp,
                                             bias=nmax[:, 2 * h + t:2 * h + t + 1],
                                             accum_out=rsum[:, 2 * h + t:2 * h + t + 1])
                    ins.then_inc(prob_made, 1)

            def drain_probT(lo, hi):
                for h in range(lo, hi):
                    drain(f"pt{h}", (probT[:, h, :], side(f"pt{h}")[:, 0:3 * P]))

            def mixT_hi(stem, hi_dst, lo_):
                for i in range(lo_, 4):
                    wait_filled(act, f"{stem}{i}")
                    act.activation(hi_dst[:, 2 * i:2 * i + 2, :].rearrange("p c t -> p (c t)"), side(f"{stem}{i}")[:, :],
                                   ACT.Copy).then_inc(mixT_hi_made, 1)

            def z_square(blk, t):
                act.wait_ge(z_made, TT * blk + t + 1)
                if blk + t > 0:
                    act.wait_ge(z_squared, TT * blk + t)
                act.activation(junk, z_part(blk, t), ACT.Square,
                               accum_out=zss[:, NOUT * t + blk:NOUT * t + blk + 1]).then_inc(z_squared, 1)

            for s in range(STEPS):
                if s > 0:
                    for i in range(HALF):
                        make_hi(E0 + HALF * s + i)
                if s == 25:
                    act.wait_ge(chunk_used, E0 + NIN * NKP)
                    mixT_hi("mixB", h_hi[:, KT // 2:KT, :], 0)
                for n in GATE_LOADS.get(s, ()):
                    if n == 0:
                        wait_filled(act, "qk7")
                    if n == 3:
                        wait_filled(act, "pt7")
                    if n >= 3:
                        act.wait_ge(gate_used, n - 2)
                    act.dma_start(gate_slot(n), ada_source(2 * D + n // 2 * ADA_COLS, n % 2)
                                  ).then_inc(gate_in[n % 3], 16)
                if s == 1:
                    act.dma_start(masks_wide, masks.rearrange("s l t -> s (l t)")).then_inc(masks_in, 16)
                    act.dma_start(onehot_sb[0:BUCKETS, :], onehot).then_inc(bias_tables_in, 16)
                    act.dma_start(relb[0:BUCKETS, :], rel_bias).then_inc(bias_tables_in, 16)
                    act.dma_start(gate_b[:, :], b_ada[2 * D:3 * D].partition_broadcast(P)).then_inc(gate_bias_in, 16)
                    drain_turned("T_iq0_", iqT, 0)
                    wait_filled(act, "T_nar")
                    act.activation(ikT, side("T_nar")[:, 0:T], ACT.Copy)
                    act.activation(iws_v, side("T_nar")[:, T:T + TT * NB].rearrange("p (t n) -> p t n", t=TT)[:, :, RANK:NB],
                                   ACT.Copy, scale=IH ** -0.5 * ID ** -0.5).then_inc(drained_act, 1)
                if s == 2:
                    drain_turned("T_iq1_", iqT, 4)
                    drain_turned("T_bq_", bqT.rearrange("p (c t) -> p c t", c=HB), 0, scale=DK ** -0.5)
                    drain_block(B_BV, lambda t: bv[:, t, 0:BLK])
                if s == 3:
                    drain_turned("T_bk_", bkT.rearrange("p (c t) -> p c t", c=HB), 0)
                    for i in range(2):
                        wait_filled(act, f"pre{i}")
                        for j in range(2):
                            hd = 2 * i + j
                            ins = act.activation(cum[:, hd * T:(hd + 1) * T], side(f"pre{i}")[:, j * T:(j + 1) * T],
                                                 ACT.Identity, bias=cols[:, 3 * KT + hd:3 * KT + hd + 1])
                        ins.then_inc(drained_act, 1)
                    wait_drained(act, "pre1")
                    link(act.activation(expo[0], cum, ACT.Abs))
                    link(act.activation(expo[0], expo[0], ACT.Exp, scale=-1.0))
                    act.activation(expo[0], expo[0], ACT.Ln, bias=1.0).then_inc(pre_made, 1)
                if s == 4:
                    wait_filled(act, "band")
                    act.activation(band_sb[0:HA, :], side("band")[0:HA, 0:T + P], ACT.Copy).then_inc(drained_act, 1)
                    wait_drained(act, "band")
                    act.dma_start(band_scratch, band_sb[0:HA, :]).then_inc(band_out, 16)
                if s == 5:
                    act.wait_ge(band_out, 16)
                    wait_filled(act, "T_bq_1")
                    act.dma_start(hankel[:, :, :], bass.AP(band_scratch.tensor, 0, [[1, P], [T + P, HA], [1, T]])
                                  ).then_inc(hankel_in, 16)
                if s - 1 in HEADS:
                    relus(*HEADS[s - 1])
                if s == 4:
                    drain_block(B_BV + 1, lambda t: bv[:, t, BLK:])
                if s == 8:
                    drain_turned("T_aq0_", qT, 0, scale=DA ** -0.5)
                if s == 10:
                    drain_turned("T_aq1_", qT, 4, scale=DA ** -0.5)
                for i in LEVEL_DECAYS.get(s, ()):
                    decay(i)
                if s == 6:
                    drain_block(B_AQ, lambda t: stage[0][:, t, :])
                if s == 8:
                    drain_block(B_AQ + 1, lambda t: stage[1][:, t, :])
                if s == 10:
                    drain_block(B_AK, lambda t: stage[0][:, t, :])
                if s == 12:
                    act.wait_ge(level_made, 8)
                    wait_filled(act, "L1")
                    drain_turned("T_ak0_", kT, 0)
                    drain_block(B_AK + 1, lambda t: stage[1][:, t, :])
                if s == 13:
                    for i in range(4):
                        t, pair = divmod(i, 2)
                        wait_filled(act, f"gla_o{i}")
                        for j in range(2):
                            n = t * HB + 2 * pair + j
                            act.activation(junk[:, 0:DV], side(f"gla_o{i}")[:, j * DV:(j + 1) * DV], ACT.Square,
                                           accum_out=gss[:, n:n + 1]).then_inc(gss_made, 1)
                            act.wait_ge(gss_made, n + 1)
                        act.activation(o_b[:, t, pair * BLK:(pair + 1) * BLK], side(f"gla_o{i}")[:, :], ACT.Copy
                                       ).then_inc(drained_act, 1)
                if s == 14:
                    drain_turned("T_ak1_", kT, 4)
                    drain_block(B_AV, lambda t: v_a[:, t, 0:BLK])
                if s == 16:
                    probs(0, 4)
                    drain_block(B_AV + 1, lambda t: v_a[:, t, BLK:])
                if s == 17:
                    drain_probT(0, 4)
                    probs(4, 8)
                if s == 18:
                    drain_probT(4, 8)
                    act.wait_ge(gate_used, 1)
                    drain_block(B_AG, lambda t: silu_a[:, t, 0:BLK], ACT.Silu)
                if s == 20:
                    drain_block(B_AG + 1, lambda t: silu_a[:, t, BLK:], ACT.Silu)
                if s == 22:
                    wait_drained(act, "pv6")
                    drain_block(B_BG, lambda t: silu_b[0][:, t, :], ACT.Silu)
                if s == 23:
                    act.wait_ge(nar_done, 1)
                    mixT_hi("mixA", a_hi, 0)
                if s == 24:
                    drain_block(B_BG + 1, lambda t: silu_b[1][:, t, :], ACT.Silu)
                    wait_drained(act, "pv6")
                    act.dma_start(fin_g, final_g.partition_broadcast(P)).then_inc(fin_in, 16)
                    wait_filled(act, "mixA3")
                    act.dma_start(z, x.rearrange("(t p) d -> p t d", p=P)).then_inc(x_again, 16)
                for blk in range(NOUT - 1):
                    if s == min(OUT_DONE[blk] + 2, STEPS - 1):
                        for t in range(TT):
                            z_square(blk, t)
            for t in range(TT):
                z_square(NOUT - 1, t)
                act.wait_ge(z_weighted, TT * (NOUT - 1))
                act.wait_ge(z_rstd, t + 1)
                act.activation(z[:, t, 0:ACT_COLS], z[:, t, 0:ACT_COLS], ACT.Copy, scale=zrs[:, t:t + 1]
                               ).then_inc(scaled_act, 1)

        @block.vector
        def _(dve):
            steps = [0]

            def mark(ins):
                steps[0] += 1
                ins.then_inc(dve_step, 1)
                return steps[0]

            def link(ins):
                dve.wait_ge(dve_step, mark(ins))

            def make_lo(g):
                if 0 < g <= E0 and g % len(EARLY) == 0:
                    dve.wait_ge(lo_made, g)
                dve.wait_ge(hi_made, g + 1)
                dve.tensor_tensor(w_lo[:, g % SPLIT, :, :], raw[:, g % RAW, :, :], w_hi[:, g % SPLIT, :, :],
                                  ALU.subtract).then_inc(lo_made, 1)

            def sum_rows(slot, accs, half_, used, n=ADA_KT):
                marks = [None, None]
                for i in range(n):
                    k = half_ * ADA_KT + i
                    a = accs[i % 2]
                    if marks[i % 2]:
                        dve.wait_ge(dve_step, marks[i % 2])
                    if k < 2:
                        ins = dve.tensor_scalar(a, slot[:, i, :], c_act[:, k:k + 1], None, ALU.mult)
                    else:
                        ins = dve.scalar_tensor_tensor(out=a, in0=slot[:, i, :], scalar=c_act[:, k:k + 1], in1=a,
                                                       op0=ALU.mult, op1=ALU.add)
                    if i < n - 1:
                        marks[i % 2] = mark(ins)
                    else:
                        ins.then_inc(used, 1)
                dve.wait_ge(dve_step, marks[0])

            def sum_ada(n):
                kp, r = divmod(n, 4)
                dve.wait_ge(ada_in[n % ADA_SLOTS], 16 * (n // ADA_SLOTS + 1))
                a = 4 * (kp % 2) + 2 * (r // 2)
                if kp >= 2 and r == 0:
                    dve.wait_ge(mod_filled, kp - 1)
                if r % 2:
                    dve.wait_ge(ada_summed, n)
                sum_rows(ada[n % ADA_SLOTS], acc[a:a + 2], r % 2, ada_summed, ADA_KT - SHIFT_PE if r == 0 else ADA_KT)

            dve.wait_ge(c_acted, 1)
            sum_ada(0)
            dve.wait_ge(square_in, 16)
            for t in range(TT):
                dve.wait_ge(x_rstd, t + 1)
                dve.tensor_scalar(rstd_diag[:, t, :], ident, stats[:, 4 + t:5 + t], None, ALU.mult
                                  ).then_inc(diag_made, 1)
            for n in range(1, 4):
                sum_ada(n)
            dve.wait_ge(cols_filled, 1)
            dve.tensor_copy(cols[:, 0:KT], bank[ADA_BANK][:, 0:KT])
            dve.tensor_scalar(cols[:, KT:2 * KT], bank[ADA_BANK][:, 2 * KT:3 * KT], 1.0, None, ALU.add)
            dve.tensor_copy(cols[:, 2 * KT:3 * KT], bank[ADA_BANK][:, KT:2 * KT])
            dve.tensor_copy(cols[:, 3 * KT:NROWS], bank[ADA_BANK][:, 3 * KT:NROWS]).then_inc(cols_made, 1)
            dve.wait_ge(cols_made, 1)
            dve.wait_ge(xT_filled, 8)
            for kp in range(NKP):
                if kp > 1 and kp < NKP - 1:
                    sum_ada(4 * kp + 4)
                dve.wait_ge(mod_filled, kp + 1)
                pm = bank[ADA_BANK][:, 4 * kp:4 * kp + 4].rearrange("p (a k) -> p a k", a=2)
                bias = cols[:, KT:3 * KT].rearrange("p (a k) -> p a k", a=2)[:, :, 2 * kp:2 * kp + 2]
                dve.tensor_tensor(mod.rearrange("p (a k) -> p a k", a=2), pm, bias, ALU.add).then_inc(mod_read, 1)
                dve.wait_ge(mod_read, kp + 1)
                dve.tensor_tensor(mod[:, 0:2], mod[:, 0:2], cols[:, 2 * kp:2 * kp + 2], ALU.mult).then_inc(mod_made, 1)
                k0 = kp * CHUNK_KT
                make_lo(len(EARLY) * kp)
                dve.wait_ge(h_hi_made, kp + 1)
                dve.tensor_tensor(h_lo[:, k0:k0 + CHUNK_KT, :], xT[:, k0:k0 + CHUNK_KT, :],
                                  h_hi[:, k0:k0 + CHUNK_KT, :], ALU.subtract).then_inc(h_lo_made, 1)
                make_lo(len(EARLY) * kp + 1)
                make_lo(len(EARLY) * kp + 2)
                if kp < NKP - 1:
                    for n in range(4 * kp + (4 if kp < 2 else 5), 4 * kp + 8):
                        sum_ada(n)
                if kp == 2:
                    dve.wait_ge(nar_hi_made, 1)
                    for cs, src in NARROW:
                        ins = dve.tensor_tensor(nar_lo[:, :, cs], nar_raw[:, :, src], nar_hi[:, :, cs], ALU.subtract)
                    ins.then_inc(nar_lo_made, 1)

            parts = ((0, 0, P), (1, P, 3 * P))

            def start_scores():
                dve.wait_ge(square_in, 16)
                dve.memset(score[:, P:2 * P], 0.0)
                dve.tensor_copy(score[:, 0:P], fill)
                link(dve.tensor_copy(score[:, 2 * P:3 * P], fill))

            def add_heads(lo, hi):
                for j in range(lo, hi):
                    wait_drained(dve, f"idx{j}")
                    if j > 0:
                        dve.wait_ge(relu_used, j)
                    for t, c0, c1 in parts:
                        ins = dve.scalar_tensor_tensor(out=score[:, c0:c1], in0=relu[j % 2][:, c0:c1],
                                                       scalar=iws_v[:, t, j:j + 1], in1=score[:, c0:c1],
                                                       op0=ALU.mult, op1=ALU.add)
                    ins.then_inc(relu_used, 1)

            def topk_rounds(n):
                for _ in range(n):
                    for t, c0, c1 in parts:
                        m1 = mark(dve.max(top8[:, 8 * t:8 * t + 8], score[:, c0:c1]))
                    dve.wait_ge(dve_step, m1)
                    for t, c0, c1 in parts:
                        m2 = mark(dve.match_replace(score[:, c0:c1], top8[:, 8 * t:8 * t + 8], score[:, c0:c1], TAKEN))
                    dve.wait_ge(dve_step, m2)

            def make_select():
                link(dve.tensor_scalar(select, score, TAKEN_BELOW, UNSELECTED, ALU.is_gt, ALU.mult))
                dve.tensor_tensor(select[:, 0:P], select[:, 0:P], fill, ALU.min)
                dve.tensor_tensor(select[:, 2 * P:3 * P], select[:, 2 * P:3 * P], fill, ALU.min).then_inc(select_made, 1)

            def cumulate():
                dve.wait_ge(pre_made, 1)
                resets = qk[0]
                link(dve.memset(resets, 1.0))
                dve.memset(resets.rearrange("p (n u) -> p n u", u=P)[:, :, 0:1], 0.0)
                link(dve.scalar_tensor_tensor(out=qk[1], in0=cum, scalar=0.0, in1=expo[0], op0=ALU.min,
                                              op1=ALU.subtract))
                dve.tensor_tensor_scan(cum, resets, qk[1], 0.0, ALU.mult, ALU.add).then_inc(cum_made, 1)
                dve.wait_ge(cum_made, 1)
                link(dve.memset(attn, 0.0))

            def level(i):
                m = P if i == 0 else LEVELS[i - 1]
                dve.wait_ge(decay_made, i + 1)
                if i >= 2:
                    wait_filled(dve, "cross" if i == 2 else f"L{LEVELS[i - 3]}")
                if i == 0:
                    wait_drained(dve, "T_bk_1")
                v = lambda a: a.rearrange("p (n two m) -> p n two m", two=2, m=m)
                dve.tensor_tensor(v(qk[i % 2])[:, :, 1, :], v(bqT)[:, :, 1, :], v(expo[i % 2])[:, :, 1, :], ALU.mult)
                dve.tensor_tensor(v(qk[i % 2])[:, :, 0, :], v(bkT)[:, :, 0, :], v(expo[i % 2])[:, :, 0, :], ALU.mult
                                  ).then_inc(level_made, 1)

            def take_diagonal(t):
                name = f"diag{t}"
                wait_filled(dve, name)
                hv = lambda a: a.rearrange("p (h t) -> p h t", h=HB)
                dve.copy_predicated(hv(attn[:, t, :]), lvl_mask[:, 0, :].unsqueeze(1).to_broadcast([P, HB, P]),
                                    hv(side(name)[:, :])).then_inc(drained_dve, 1)
                wait_drained(dve, name)

            def take_level(lvl):
                m = LEVELS[lvl - 1]
                n = P // (2 * m)
                name = f"L{m}"
                wait_filled(dve, name)
                msk = lvl_mask[:, lvl, :].rearrange("p (n two m) -> p n two m", two=2, m=m)[:, :, 1, :]
                for t in range(TT):
                    dst = attn[:, t, :].rearrange("p (h n two m) -> p h n two m", h=HB, two=2, m=m)[:, :, :, 1, :]
                    src = side(name)[:, t * HB * P // 2:(t + 1) * HB * P // 2].rearrange("p (h n m) -> p h n m", h=HB, m=m)
                    ins = dve.copy_predicated(dst, msk.unsqueeze(1).to_broadcast([P, HB, n, m]), src)
                ins.then_inc(drained_dve, 1)
                wait_drained(dve, name)

            def norm_b():
                dve.wait_ge(tables_in, 16 * 2)
                dve.wait_ge(grs_made, 1)
                wait_drained(dve, "gla_o3")
                for t in range(TT):
                    for hd in range(HB):
                        n = t * HB + hd
                        v = o_b[:, t, hd * DV:(hd + 1) * DV]
                        ins = dve.scalar_tensor_tensor(out=v, in0=v, scalar=grs[:, n:n + 1], in1=gla_gb[:, :],
                                                       op0=ALU.mult, op1=ALU.mult)
                ins.then_inc(o_b_made, 1)

            def logits(lo, hi):
                for h in range(lo, hi):
                    wait_filled(dve, f"qk{h}")
                    for t, c0, c1 in parts:
                        ins = dve.tensor_tensor_reduce(prob[:, h, c0:c1], side(f"qk{h}")[:, c0:c1], select[:, c0:c1], 1.0,
                                                       TAKEN, ALU.add, ALU.max, lmax[:, 2 * h + t:2 * h + t + 1])
                    ins.then_inc(drained_dve, 1)
                wait_drained(dve, f"qk{hi - 1}")
                dve.tensor_scalar(nmax[:, 2 * lo:2 * hi], lmax[:, 2 * lo:2 * hi], -1.0, None, ALU.mult
                                  ).then_inc(nmax_made, 1)

            def take_outputs(lo, hi):
                for h in range(lo, hi, 2):
                    wait_filled(dve, f"pv{h}")
                    for j in range(2):
                        for t in range(TT):
                            n = 2 * (h + j) + t
                            ins = dve.tensor_scalar(mix_a[:, t, (h + j) * DA:(h + j + 1) * DA],
                                                    side(f"pv{h}")[:, j * T + t * P:j * T + (t + 1) * P],
                                                    rinv[:, n:n + 1], None, ALU.mult)
                    ins.then_inc(drained_dve, 1)

            def mixT_lo(stem, hi_dst, lo_dst, before):
                for i in range(4):
                    dve.wait_ge(mixT_hi_made, before + i + 1)
                    dve.tensor_tensor(lo_dst[:, 2 * i:2 * i + 2, :].rearrange("p c t -> p (c t)"), side(f"{stem}{i}")[:, :],
                                      hi_dst[:, 2 * i:2 * i + 2, :].rearrange("p c t -> p (c t)"), ALU.subtract
                                      ).then_inc(drained_dve, 1)

            def sum_gate(n):
                j, hf = divmod(n, 2)
                dve.wait_ge(gate_in[n % 3], 16 * (n // 3 + 1))
                if hf == 0 and j >= 4:
                    wait_filled(dve, f"gate{j - 4}")
                if hf == 1:
                    dve.wait_ge(gate_used, n)
                sum_rows(gate_slot(n), gate_acc[2 * (j % 4):2 * (j % 4) + 2], hf, gate_used)

            def take_gate(j):
                wait_filled(dve, f"gate{j}")
                g = gate_b[:, j * ADA_COLS:(j + 1) * ADA_COLS]
                dve.tensor_tensor(g, side(f"gate{j}")[:, 0:ADA_COLS], g, ALU.add).then_inc(drained_dve, 1)

            def residual(blk):
                dve.wait_ge(chunk_used, E0 + HALF * (OUT_DONE[blk] + 1))
                dve.wait_ge(x_again, 16)
                wait_drained(dve, f"gate{2 * blk + 1}")
                cs = slice(blk * BLK, (blk + 1) * BLK)
                for t in range(TT):
                    dve.tensor_tensor(silu_b[0][:, t, :], bank[2 * ((NIN + blk) % 2) + t][:, :], gate_b[:, cs], ALU.mult
                                      ).then_inc(y_gated, 1)
                dve.wait_ge(y_gated, TT * (blk + 1))
                for t in range(TT):
                    dve.tensor_tensor(z[:, t, cs], z[:, t, cs], silu_b[0][:, t, :], ALU.add).then_inc(z_made, 1)
                dve.wait_ge(z_made, TT * (blk + 1))

            def last_residual(t):
                blk = NOUT - 1
                dve.wait_ge(last_filled, t + 1)
                wait_drained(dve, f"gate{2 * blk + 1}")
                cs = slice(blk * BLK, (blk + 1) * BLK)
                link(dve.tensor_tensor(silu_b[0][:, t, :], bank[2 * ((NIN + blk) % 2) + t][:, :], gate_b[:, cs], ALU.mult))
                dve.tensor_tensor(z_part(blk, t), z[:, t, cs], silu_b[0][:, t, :], ALU.add).then_inc(z_made, 1)
                dve.wait_ge(z_made, TT * blk + t + 1)
                dve.wait_ge(fin_in, 16)
                link(dve.tensor_tensor(z[:, t, cs], z_part(blk, t), fin_g[:, cs], ALU.mult))

            for s in range(STEPS):
                for i in range(HALF):
                    make_lo(E0 + HALF * s + i)
                if s == 25:
                    mixT_lo("mixB", h_hi[:, KT // 2:KT, :], h_lo[:, KT // 2:KT, :], 4)
                if s == 1:
                    start_scores()
                if s == 4:
                    cumulate()
                if s == 8:
                    dve.wait_ge(masks_made, 1)
                    wait_filled(dve, "cross")
                    dve.tensor_copy(attn[:, 2, :], side("cross")[:, :]).then_inc(drained_dve, 1)
                if s == 9:
                    take_level(1)
                    take_level(2)
                    for t in range(TT):
                        take_diagonal(t)
                if s == 10:
                    take_level(3)
                    take_level(4)
                if s == 11:
                    take_level(5)
                    take_level(6)
                if s == 12:
                    take_level(7)
                if s - 1 in HEADS:
                    add_heads(*HEADS[s - 1])
                for i in LEVEL_FACTORS.get(s, ()):
                    level(i)
                if s == 8:
                    dve.wait_ge(relu_used, IH)
                topk_rounds(ROUNDS.get(s, 0))
                if s == 14:
                    make_select()
                    dve.wait_ge(select_made, 1)
                    norm_b()
                if s == 15:
                    logits(0, 4)
                if s == 16:
                    logits(4, 8)
                if s == 18:
                    dve.wait_ge(prob_made, HA)
                    dve.reciprocal(rinv, rsum).then_inc(rinv_made, 1)
                    dve.wait_ge(rinv_made, 1)
                if s == 19:
                    take_outputs(0, 4)
                if s == 20:
                    take_outputs(4, 8)
                if s == 21:
                    dve.wait_ge(block_drained, B_AG + 2)
                    wait_drained(dve, "pv6")
                    for t in range(TT):
                        dve.tensor_tensor(mix_a[:, t, :], mix_a[:, t, :], silu_a[:, t, :], ALU.mult).then_inc(mix_a_made, 1)
                if s == 23:
                    mixT_lo("mixA", a_hi, a_lo, 0)
                if s in (23, 24):
                    j = s - 23
                    dve.wait_ge(block_drained, B_BG + 1 + j)
                    dve.wait_ge(o_b_made, 1)
                    for t in range(TT):
                        v = o_b[:, t, j * BLK:(j + 1) * BLK]
                        dve.tensor_tensor(v, v, silu_b[j][:, t, :], ALU.mult).then_inc(mix_b_made, 1)
                for blk in range(NOUT - 1):
                    if s == OUT_DONE[blk] + 1:
                        residual(blk)
                for j, ps in ((j, ps) for ps, j in GATE_STEPS.items() if ps + 1 == s):
                    take_gate(j)
                for n in GATE_SUMS.get(s, ()):
                    sum_gate(n)
            for t in range(TT):
                last_residual(t)
                dve.wait_ge(z_squared, TT * (NOUT - 1) + t + 1)
                dve.tensor_reduce(zsum[:, t:t + 1], zss[:, NOUT * t:NOUT * (t + 1)], AX_X, ALU.add).then_inc(zsum_made, 1)
                dve.wait_ge(z_weighted, TT * (NOUT - 1))
                dve.wait_ge(z_rstd, t + 1)
                dve.tensor_scalar(z[:, t, ACT_COLS:], z[:, t, ACT_COLS:], zrs[:, t:t + 1], None, ALU.mult
                                  ).then_inc(scaled_dve, 1)

        @block.tensor
        def _(pe):
            def three(out_, hi, lo, whi, wlo, first, last):
                pe.matmul(out_, hi, whi, start=first, stop=False, skip_group_check=True)
                pe.matmul(out_, hi, wlo, start=False, stop=False, skip_group_check=True)
                return pe.matmul(out_, lo, whi, start=False, stop=last, skip_group_check=True)

            def products(g, kp, banks, s_hi, s_lo, between=None):
                pe.wait_ge(lo_made, g + 1)
                for i in range(CHUNK_KT):
                    k = kp * CHUNK_KT + i
                    for t in range(TT):
                        ts = slice(t * P, (t + 1) * P)
                        if between:
                            between(i * TT + t)
                        ins = three(bank[banks + t][:, :], s_hi(k)[:, ts], s_lo(k)[:, ts],
                                    w_hi[:, g % SPLIT, i, :], w_lo[:, g % SPLIT, i, :], k == 0, k == KT - 1)
                return ins

            def use_chunk(*chunk):
                products(*chunk).then_inc(chunk_used, 1)

            def fill_side(name):
                if ORDER[name] >= 4:
                    wait_drained(pe, USES[ORDER[name] - 4][0])
                return side(name)

            def turn(stem, st):
                for i in range(2):
                    b = fill_side(f"{stem}{i}")
                    for j in range(2):
                        for t in range(TT):
                            c0 = (2 * i + j) * P
                            ins = pe.transpose(b[:, (2 * j + t) * P:(2 * j + t + 1) * P], st[:, t, c0:c0 + P], ident)
                    ins.then_inc(side_filled, 1)

            pe.wait_ge(diag_made, TT)
            for i in range(8):
                if i >= 6:
                    pe.wait_ge(xT_drained, i - 5)
                for j in range(2):
                    for t in range(TT):
                        k = 2 * i + j
                        ins = pe.matmul(bank[i % 6][:, (2 * j + t) * P:(2 * j + t + 1) * P],
                                        x_nat[:, t, k * P:(k + 1) * P], rstd_diag[:, t, :], start=True, stop=True)
                ins.then_inc(xT_filled, 1)
            pe.wait_ge(square_in, 16)
            pe.wait_ge(rows_in, 48)
            pe.transpose(bank[ADA_BANK][:, 0:NROWS], rows[0:NROWS, :], ident[0:NROWS, 0:NROWS]).then_inc(cols_filled, 1)
            pe.wait_ge(cols_made, 1)
            pe.wait_ge(c_acted, 1)

            def wait_shift(kp):
                if kp > 0:
                    pe.wait_ge(mod_read, kp)
                pe.wait_ge(ada_in[4 * kp % ADA_SLOTS], 16 * (4 * kp // ADA_SLOTS + 1))

            def shift_products(kp, n):
                ct, quarter = divmod(n, 2)
                for i in range(ADA_KT - SHIFT_PE + quarter * SHIFT_PE // 2, ADA_KT - (1 - quarter) * SHIFT_PE // 2):
                    ins = pe.matmul(bank[ADA_BANK][:, 4 * kp + 2 + ct:4 * kp + 3 + ct],
                                    ada[4 * kp % ADA_SLOTS][:, i, ct * P:(ct + 1) * P], c_act[:, i:i + 1],
                                    start=(kp == 0 and ct == 0 and i == ADA_KT - SHIFT_PE), stop=False,
                                    skip_group_check=True)
                if n == 3:
                    ins.then_inc(shift_used, 1)

            def sum_columns(kp, r):
                pe.wait_ge(ones_made, 1)
                pe.wait_ge(acc_folded, 2 * kp + r + 1)
                for ct in range(2):
                    o = 4 * kp + 2 * (1 - r) + ct
                    ins = pe.matmul(bank[ADA_BANK][:, o:o + 1], acc[4 * (kp % 2) + 2 * r][:, ct * P:(ct + 1) * P],
                                    ones[:, 0:1], start=False, stop=True, skip_group_check=True)
                if r == 1:
                    ins.then_inc(mod_filled, 1)

            wait_shift(0)
            for n in range(4):
                shift_products(0, n)
            for r in range(2):
                sum_columns(0, r)
            pe.wait_ge(xT_drained, 8)
            for kp in range(NKP):
                pe.wait_ge(h_lo_made, kp + 1)
                if kp == 3:
                    pe.wait_ge(nar_lo_made, 1)
                for k in range(0 if kp == 3 else kp * CHUNK_KT, (kp + 1) * CHUNK_KT if kp >= 3 else 0):
                    ins = three(nar_out, nar_hi[:, k, :], nar_lo[:, k, :], h_hi[:, k, :], h_lo[:, k, :], False, k == KT - 1)
                if kp == NKP - 1:
                    ins.then_inc(nar_done, 1)
                own = (lambda k: h_hi[:, k, :]), (lambda k: h_lo[:, k, :])
                g = len(EARLY) * kp
                use_chunk(g + E_IQ0, kp, EARLY_BANK[E_IQ0], *own)
                last = kp == NKP - 1
                for t in range(TT):
                    if t == 1:
                        if last:
                            products(g + E_IQ1, kp, EARLY_BANK[E_IQ1], *own)
                        else:
                            wait_shift(kp + 1)
                            products(g + E_IQ1, kp, EARLY_BANK[E_IQ1], *own, lambda n: shift_products(kp + 1, n))
                    pe.wait_ge(lo_made, g + E_BQ + 1)
                    if kp > 0 or t > 0:
                        pe.wait_ge(bq_copied, TT * kp + t)
                    for n in range(3 * CHUNK_KT):
                        if t == 1 and n in (1, 2) and not last:
                            sum_columns(kp + 1, n - 1)
                        i, turn_ = divmod(n, 3)
                        ins = pe.matmul(bank[BQ_BANK][:, :],
                                        (h_lo if turn_ == 2 else h_hi)[:, kp * CHUNK_KT + i, t * P:(t + 1) * P],
                                        (w_lo if turn_ == 1 else w_hi)[:, (g + E_BQ) % SPLIT, i, :],
                                        start=(n == 0), stop=(n == 3 * CHUNK_KT - 1), skip_group_check=True)
                    if t == 0:
                        ins.then_inc(bq_filled, 1)
                    else:
                        ins.then_inc(chunk_used, 2)
                use_chunk(g + E_BK, kp, EARLY_BANK[E_BK], *own)

            def index_heads(lo, hi):
                for j in range(lo, hi):
                    b = fill_side(f"idx{j}")
                    r = slice((j % 2) * ID, (j % 2 + 1) * ID)
                    pe.matmul(b[:, 0:P], iqT[r, j // 2, 0:P], ikT[r, 0:P], start=True, stop=True)
                    pe.matmul(b[:, P:3 * P], iqT[r, j // 2, P:T], ikT[r, :], start=True, stop=True
                              ).then_inc(side_filled, 1)

            bqv, bkv = (a.rearrange("p (h t) -> p h t", h=HB) for a in (bqT, bkT))
            qkv = [a.rearrange("p (h t) -> p h t", h=HB) for a in qk]

            def pair_products(name, left, right):
                b = fill_side(name)
                for hd in range(HB):
                    ins = pe.matmul(b[:, hd * P:(hd + 1) * P], left(hd), right(hd), start=True, stop=True)
                ins.then_inc(side_filled, 1)

            def level_products(i):
                pe.wait_ge(level_made, i + 1)
                m = LEVELS[i - 1]
                b = fill_side(f"L{m}")
                for t in range(TT):
                    for hd in range(HB):
                        tile = qkv[i % 2][:, hd, t * P:(t + 1) * P]
                        o = (t * HB + hd) * P // 2
                        ins = pe.matmul(b[:, o:o + P // 2], tile,
                                        tile.rearrange("p (n two m) -> p n two m", two=2, m=m)[:, :, 1, :],
                                        start=True, stop=True)
                ins.then_inc(side_filled, 1)

            def turn_mix(stem, src):
                for i in range(4):
                    b = fill_side(f"{stem}{i}")
                    for j in range(2):
                        for t in range(TT):
                            c0 = (2 * i + j) * P
                            ins = pe.transpose(b[:, (2 * j + t) * P:(2 * j + t + 1) * P], src[:, t, c0:c0 + P], ident)
                    ins.then_inc(side_filled, 1)

            for s in range(STEPS):
                blk, second = block_of(s)
                if second == 0:
                    if blk >= 2:
                        if blk - 2 < NIN:
                            pe.wait_ge(block_drained, blk - 1)
                        else:
                            pe.wait_ge(y_gated, TT * (blk - 2 - NIN + 1))
                    elif blk == 0:
                        pe.wait_ge(early_drained, 2)
                    else:
                        pe.wait_ge(early_drained, 7)
                if s == 24:
                    wait_drained(pe, "mixA3")
                if s == 26:
                    wait_drained(pe, "mixB3")
                if blk < NIN:
                    s_hi, s_lo = (lambda k: h_hi[:, k, :]), (lambda k: h_lo[:, k, :])
                else:
                    s_hi = lambda k: a_hi[:, k, :] if k < KT // 2 else h_hi[:, k, :]
                    s_lo = lambda k: a_lo[:, k, :] if k < KT // 2 else h_lo[:, k, :]
                if s < STEPS - 1:
                    for i in range(HALF):
                        use_chunk(E0 + s * HALF + i, second * HALF + i, 2 * (blk % 2), s_hi, s_lo)
                else:
                    for t in range(TT):
                        for i in range(HALF):
                            g = E0 + s * HALF + i
                            pe.wait_ge(lo_made, g + 1)
                            for j in range(CHUNK_KT):
                                k = (second * HALF + i) * CHUNK_KT + j
                                ins = three(bank[2 * (blk % 2) + t][:, :], s_hi(k)[:, t * P:(t + 1) * P],
                                            s_lo(k)[:, t * P:(t + 1) * P], w_hi[:, g % SPLIT, j, :], w_lo[:, g % SPLIT, j, :],
                                            k == 0, k == KT - 1)
                        ins.then_inc(last_filled, 1)

                if s == 0:
                    pe.wait_ge(early_drained, 7)
                    pe.wait_ge(mod_read, NKP)
                    pe.wait_ge(bq_copied, TT * NKP)
                    turn("T_iq0_", stage[0])
                    b = fill_side("T_nar")
                    for r in range(2):
                        pe.matmul(b[r * ID:(r + 1) * ID, 0:T], ident[0:ID, 0:ID], narT[0:ID, :], start=True, stop=True)
                    for t in range(TT):
                        ins = pe.transpose(b[:, T + t * NB:T + (t + 1) * NB], narT[ID:NAR, t * P:(t + 1) * P],
                                           ident[ID:NAR, ID:NAR])
                    ins.then_inc(side_filled, 1)
                if s == 1:
                    turn("T_iq1_", stage[1])
                    pe.wait_ge(bq_added, TT * (NKP - 1))
                    turn("T_bq_", bq_sum)
                if s == 2:
                    turn("T_bk_", stage[2])
                    pe.wait_ge(tables_in, 16 * 2)
                    for i in range(2):
                        b = fill_side(f"pre{i}")
                        for j in range(2):
                            hd = 2 * i + j
                            ins = pe.matmul(b[:, j * T:(j + 1) * T], w_alpha[ID:ID + RANK, hd * DK:(hd + 1) * DK],
                                            narT[ID:ID + RANK, :], start=True, stop=True)
                        ins.then_inc(side_filled, 1)
                if s == 3:
                    pe.wait_ge(bias_tables_in, 16 * 2)
                    b = fill_side("band")
                    pe.matmul(b[0:HA, 0:T + P], relb[0:BUCKETS, :], onehot_sb[0:BUCKETS, :], start=True, stop=True
                              ).then_inc(side_filled, 1)
                    wait_drained(pe, "T_iq1_1")
                if s in HEADS:
                    index_heads(*HEADS[s])
                if s == 7:
                    pe.wait_ge(block_drained, B_AQ + 1)
                    turn("T_aq0_", stage[0])
                    pe.wait_ge(level_made, 1)
                    pair_products("cross", lambda hd: qkv[0][:, hd, 0:P], lambda hd: qkv[0][:, hd, P:T])
                if s == 8:
                    level_products(1)
                    level_products(2)
                    wait_drained(pe, "T_bk_1")
                    for t in range(TT):
                        pair_products(f"diag{t}", lambda hd: bkv[:, hd, t * P:(t + 1) * P],
                                      lambda hd: bqv[:, hd, t * P:(t + 1) * P])
                if s == 9:
                    pe.wait_ge(block_drained, B_AQ + 2)
                    turn("T_aq1_", stage[1])
                    level_products(3)
                    level_products(4)
                if s == 10:
                    level_products(5)
                    level_products(6)
                if s == 11:
                    pe.wait_ge(block_drained, B_AK + 1)
                    turn("T_ak0_", stage[0])
                    level_products(7)
                if s == 12:
                    wait_drained(pe, "L1")
                    for i in range(4):
                        t, pair = divmod(i, 2)
                        b = fill_side(f"gla_o{i}")
                        for j in range(2):
                            hd = 2 * pair + j
                            o, vs, hs = b[:, j * DV:(j + 1) * DV], slice(hd * DV, (hd + 1) * DV), slice(hd * P, (hd + 1) * P)
                            if t == 1:
                                pe.matmul(o, attn[:, 2, hs], bv[:, 0, vs], start=True, stop=False)
                            ins = pe.matmul(o, attn[:, t, hs], bv[:, t, vs], start=(t == 0), stop=True)
                        ins.then_inc(side_filled, 1)
                if s == 13:
                    pe.wait_ge(block_drained, B_AK + 2)
                    turn("T_ak1_", stage[1])
                if s in (14, 15):
                    wait_drained(pe, "T_ak1_1")
                    pe.wait_ge(hankel_in, 16)
                    for h in range(4 * (s - 14), 4 * (s - 13)):
                        b = fill_side(f"qk{h}")
                        for t, c0, c1 in ((0, 0, P), (1, P, 3 * P)):
                            pe.matmul(b[:, c0:c1], qT[:, h, t * P:(t + 1) * P], kT[:, h, 0:c1 - c0], start=True, stop=False)
                            ins = pe.matmul(b[:, c0:c1], flip, hankel[:, h, T - (c1 - c0):T], start=False, stop=True)
                        ins.then_inc(side_filled, 1)
                if s in (16, 17):
                    for h in range(4 * (s - 16), 4 * (s - 15)):
                        b = fill_side(f"pt{h}")
                        pe.wait_ge(prob_made, h + 1)
                        for i in range(3):
                            ins = pe.transpose(b[:, i * P:(i + 1) * P], prob[:, h, i * P:(i + 1) * P], ident)
                        ins.then_inc(side_filled, 1)
                if s in (18, 19):
                    pe.wait_ge(block_drained, B_AV + 2)
                    for h in range(4 * (s - 18), 4 * (s - 17), 2):
                        b = fill_side(f"pv{h}")
                        wait_drained(pe, f"pt{h + 1}")
                        for hd in (h, h + 1):
                            o, vs = (hd - h) * T, slice(hd * DA, (hd + 1) * DA)
                            pe.matmul(b[:, o:o + P], probT[:, hd, 0:P], v_a[:, 0, vs], start=True, stop=True)
                            pe.matmul(b[:, o + P:o + T], probT[:, hd, P:2 * P], v_a[:, 0, vs], start=True, stop=False)
                            ins = pe.matmul(b[:, o + P:o + T], probT[:, hd, 2 * P:3 * P], v_a[:, 1, vs], start=False,
                                            stop=True)
                        ins.then_inc(side_filled, 1)
                if s == 22:
                    pe.wait_ge(mix_a_made, TT)
                    turn_mix("mixA", mix_a)
                if s == 24:
                    pe.wait_ge(mix_b_made, 2 * TT)
                    turn_mix("mixB", o_b)
                if s in GATE_STEPS:
                    j = GATE_STEPS[s]
                    b = fill_side(f"gate{j}")
                    pe.wait_ge(gate_folded, j + 1)
                    pe.wait_ge(gate_bias_in, 16)
                    pe.matmul(b[:, 0:ADA_COLS], ones[:, :], gate_acc[2 * (j % 4)], start=True, stop=True
                              ).then_inc(side_filled, 1)


_INS = ["x", "c", "w_ada", "b_ada", "norm_g", "w_in", "w_alpha_up", "b_alpha", "gla_g", "w_out", "rel_bias", "final_g"]


def kernel(**inputs):
    import numpy as _np
    import concourse.bacc as _bacc
    from concourse import mybir as _mybir
    from concourse.bass_utils import run_bass_kernel_spmd as _run

    nc = _bacc.Bacc("TRN2", target_bir_lowering=False, num_devices=1)
    arrays, args = {}, []
    for name in _INS:
        a = _np.ascontiguousarray(inputs[name])
        if name not in ("rel_bias", "final_g"):
            a = a[0]
        arrays[f"in_{name}"] = a
        args.append(nc.dram_tensor(f"in_{name}", a.shape, _mybir.dt.from_np(a.dtype), kind="ExternalInput").ap())
    T, D = inputs["x"].shape[1:]
    for name, a in zip(("square", "onehot", "masks"), constants(T)):
        arrays[f"const_{name}"] = a
        args.append(nc.dram_tensor(f"const_{name}", a.shape, _mybir.dt.from_np(a.dtype), kind="ExternalInput").ap())
    args.append(nc.dram_tensor("band_scratch", (inputs["rel_bias"].shape[1], T + P), _mybir.dt.float32,
                               kind="Internal").ap())
    args.append(nc.dram_tensor("out", (T, D), _mybir.dt.float32, kind="ExternalOutput").ap())
    build(nc, *args)
    r = _run(nc, [arrays], core_ids=[0])
    return r.results[0]["out"].reshape(1, T, D)
```
